# Optimizing a Trainium2 kernel written in Bass

```python
import math
import jax, jax.numpy as jnp
from jax import lax
import numpy as np

D_MODEL = 1024
BATCH = 1
SEQ = 256
DEPTH = 2

GRID_W = 64
CTX_LEN = 256

N_ATT_HEADS = 4
ATT_HEAD_DIM = 64
ATT_V_DIM = 2 * ATT_HEAD_DIM
QK_WIDTH = N_ATT_HEADS * 2 * ATT_HEAD_DIM
ATT_WIDTH = N_ATT_HEADS * ATT_V_DIM
CONV_WIDTH = D_MODEL // 4
CONV_WIDTH_K = 3
FOURIER_WIDTH = D_MODEL // 4
FOURIER_GROUPS = 4
FOURIER_GROUP_DIM = FOURIER_WIDTH // FOURIER_GROUPS

MIX_WIDTH = ATT_WIDTH + CONV_WIDTH + FOURIER_WIDTH
IN_WIDTH = 2 * QK_WIDTH + ATT_WIDTH + 3 * CONV_WIDTH + FOURIER_WIDTH
SPLITS = (QK_WIDTH, 2 * QK_WIDTH, 2 * QK_WIDTH + ATT_WIDTH,
          2 * QK_WIDTH + ATT_WIDTH + CONV_WIDTH,
          2 * QK_WIDTH + ATT_WIDTH + 2 * CONV_WIDTH,
          2 * QK_WIDTH + ATT_WIDTH + 3 * CONV_WIDTH)

D_FF = 4 * D_MODEL
Q_BLOCK = 128
ROPE_BASE = 10000.0
LN_EPS = 1e-5
RMS_EPS = 1e-5
DEEPNORM_ALPHA = (2 * DEPTH) ** 0.25
DEEPNORM_BETA = (8 * DEPTH) ** -0.25


def layer_norm(x, g, b):
    xf = x.astype(jnp.float32)
    mu = jnp.mean(xf, axis=-1, keepdims=True)
    var = jnp.mean(jnp.square(xf - mu), axis=-1, keepdims=True)
    y = (xf - mu) * lax.rsqrt(var + LN_EPS)
    return (y * g.astype(jnp.float32) + b.astype(jnp.float32)).astype(x.dtype)

def rms_norm(x, w):
    xf = x.astype(jnp.float32)
    y = xf * lax.rsqrt(jnp.mean(jnp.square(xf), axis=-1, keepdims=True) + RMS_EPS)
    return (y * w.astype(jnp.float32)).astype(x.dtype)

def modulate(x, shift, scale):
    return x * (1.0 + scale) + shift

def axial_rope(x, rows, cols):
    half = ATT_HEAD_DIM // 2
    quarter = half // 2
    inv_freq = 1.0 / (ROPE_BASE ** (jnp.arange(0, half, 2, dtype=jnp.float32) / half))

    def rot(xa, pos):
        ang = pos.astype(jnp.float32)[:, None] * inv_freq[None, :]
        cos = jnp.cos(ang)[None, :, None, None, :].astype(xa.dtype)
        sin = jnp.sin(ang)[None, :, None, None, :].astype(xa.dtype)
        x1, x2 = xa[..., :quarter], xa[..., quarter:]
        return jnp.concatenate([x1 * cos - x2 * sin, x2 * cos + x1 * sin], axis=-1)

    return jnp.concatenate([rot(x[..., :half], rows), rot(x[..., half:], cols)], axis=-1)

def split_proj(p):
    B, L, _ = p.shape
    q, k, v, u, gb, gc, f = jnp.split(p, SPLITS, axis=-1)
    q = q.reshape(B, L, N_ATT_HEADS, 2, ATT_HEAD_DIM)
    k = k.reshape(B, L, N_ATT_HEADS, 2, ATT_HEAD_DIM)
    v = v.reshape(B, L, N_ATT_HEADS, ATT_V_DIM)
    return q, k, v, u, gb, gc, f

def diff_attention(q, k, v, lam):
    s = jnp.einsum('bqhpd,bkhpd->bhpqk', q, k).astype(jnp.float32) * (ATT_HEAD_DIM ** -0.5)
    p = jax.nn.softmax(s, axis=-1)
    a = p[:, :, 0] - lam * p[:, :, 1]
    return jnp.einsum('bhqk,bkhe->bqhe', a.astype(v.dtype), v)

def diff_attention_blocked(q, k, v, lam):
    B, L = q.shape[0], q.shape[1]
    nb = L // Q_BLOCK
    qb = q.reshape(B, nb, Q_BLOCK, N_ATT_HEADS, 2, ATT_HEAD_DIM).transpose(1, 0, 2, 3, 4, 5)
    out = lax.map(lambda qi: diff_attention(qi, k, v, lam), qb)
    return out.transpose(1, 0, 2, 3, 4).reshape(B, L, N_ATT_HEADS, ATT_V_DIM)

def diff_head_out(o, subln_w, lam_init):
    B, L = o.shape[0], o.shape[1]
    return (rms_norm(o, subln_w) * (1.0 - lam_init)).reshape(B, L, ATT_WIDTH)

def short_conv(u, gb, gc, w, b):
    z = gc * u
    y = lax.conv_general_dilated(z, w[:, None, :].astype(z.dtype), window_strides=(1,),
                                 padding=((1, 1),), dimension_numbers=('NWC', 'WIO', 'NWC'),
                                 feature_group_count=CONV_WIDTH)
    return gb * (y + b)

def fourier_mix(f):
    B, L, _ = f.shape
    fg = f.reshape(B, L, FOURIER_GROUPS, FOURIER_GROUP_DIM).astype(jnp.float32)
    F = jnp.fft.fftn(fg, axes=(1, 3), norm='ortho')
    return jnp.real(F).reshape(B, L, FOURIER_WIDTH).astype(f.dtype)

def squared_relu_mlp(h, w_up, w_down):
    return jnp.square(jax.nn.relu(h @ w_up)) @ w_down

def first_inputs(seed: int = 0) -> dict:
    key = jax.random.key(seed)
    ks = jax.random.split(key, 20)
    f32 = jnp.float32
    D = D_MODEL
    x = jax.random.normal(ks[0], (BATCH, SEQ, D), f32)
    c = jax.random.normal(ks[1], (BATCH, D), f32)
    ctx = jax.random.normal(ks[2], (BATCH, CTX_LEN, D), f32)
    c_ctx = jax.random.normal(ks[3], (D,), f32)
    w_mod = jax.random.normal(ks[4], (DEPTH, D, 6 * D), f32) * D ** -0.5
    b_mod = jax.random.normal(ks[5], (DEPTH, 6 * D), f32) * 0.02
    col_scale = jnp.ones((IN_WIDTH,), f32).at[2 * QK_WIDTH:2 * QK_WIDTH + ATT_WIDTH].set(DEEPNORM_BETA)
    w_in = jax.random.normal(ks[6], (DEPTH, D, IN_WIDTH), f32) * D ** -0.5 * col_scale
    diff_lambda = jax.random.normal(ks[7], (DEPTH, 4, ATT_HEAD_DIM), f32) * 0.1
    subln_w = 1.0 + 0.02 * jax.random.normal(ks[8], (DEPTH, ATT_V_DIM), f32)
    conv_w = jax.random.normal(ks[9], (DEPTH, CONV_WIDTH_K, CONV_WIDTH), f32) * CONV_WIDTH_K ** -0.5
    conv_b = jax.random.normal(ks[10], (DEPTH, CONV_WIDTH), f32) * 0.02
    w_out = jax.random.normal(ks[11], (DEPTH, MIX_WIDTH, D), f32) * MIX_WIDTH ** -0.5 * DEEPNORM_BETA
    ln1_g = 1.0 + 0.02 * jax.random.normal(ks[12], (DEPTH, D), f32)
    ln1_b = 0.02 * jax.random.normal(ks[13], (DEPTH, D), f32)
    w_up = jax.random.normal(ks[14], (DEPTH, D, D_FF), f32) * D ** -0.5 * DEEPNORM_BETA
    w_down = jax.random.normal(ks[15], (DEPTH, D_FF, D), f32) * D_FF ** -0.5 * DEEPNORM_BETA
    ln2_g = 1.0 + 0.02 * jax.random.normal(ks[16], (DEPTH, D), f32)
    ln2_b = 0.02 * jax.random.normal(ks[17], (DEPTH, D), f32)
    return {"x": x, "c": c, "ctx": ctx, "c_ctx": c_ctx, "w_mod": w_mod, "b_mod": b_mod,
            "w_in": w_in, "diff_lambda": diff_lambda, "subln_w": subln_w, "conv_w": conv_w,
            "conv_b": conv_b, "w_out": w_out, "ln1_g": ln1_g, "ln1_b": ln1_b, "w_up": w_up,
            "w_down": w_down, "ln2_g": ln2_g, "ln2_b": ln2_b}

def first_block(x, c, ctx, c_ctx, w_mod, b_mod, w_in, diff_lambda, subln_w, conv_w, conv_b,
              w_out, ln1_g, ln1_b, w_up, w_down, ln2_g, ln2_b):
    B, S, D = x.shape
    ROWS = S // GRID_W
    rows = jnp.repeat(jnp.arange(ROWS), GRID_W)
    cols = jnp.tile(jnp.arange(GRID_W), ROWS)
    silu_c = jax.nn.silu(c)
    silu_cc = jax.nn.silu(c_ctx)

    for l in range(DEPTH):
        last = l == DEPTH - 1
        mod_x = (silu_c @ w_mod[l] + b_mod[l])[:, None, :]
        mod_c = (silu_cc @ w_mod[l] + b_mod[l])[None, None, :]
        sh1, sc1, g1, sh2, sc2, g2 = jnp.split(mod_x, 6, axis=-1)
        csh1, csc1, cg1, csh2, csc2, cg2 = jnp.split(mod_c, 6, axis=-1)

        lam_init = 0.8 - 0.6 * math.exp(-0.3 * l)
        lam_p = diff_lambda[l].astype(jnp.float32)
        lam = (jnp.exp(jnp.sum(lam_p[0] * lam_p[1])) - jnp.exp(jnp.sum(lam_p[2] * lam_p[3]))
               + lam_init)

        px = modulate(x, sh1, sc1) @ w_in[l]
        pc = modulate(ctx, csh1, csc1) @ w_in[l]
        qx, kx, vx, ux, gbx, gcx, fx = split_proj(px)
        qc, kc, vc, uc, gbc, gcc, fc = split_proj(pc)
        qx = axial_rope(qx, rows, cols)
        kx = axial_rope(kx, rows, cols)
        k_all = jnp.concatenate([kc, kx], axis=1)
        v_all = jnp.concatenate([vc, vx], axis=1)

        ox = diff_attention_blocked(qx, k_all, v_all, lam)
        mix_x = jnp.concatenate([
            diff_head_out(ox, subln_w[l], lam_init),
            short_conv(ux, gbx, gcx, conv_w[l], conv_b[l]),
            fourier_mix(fx)], axis=-1) @ w_out[l]
        x = layer_norm(DEEPNORM_ALPHA * x + g1 * mix_x, ln1_g[l], ln1_b[l])

        x = layer_norm(DEEPNORM_ALPHA * x + g2 * squared_relu_mlp(modulate(x, sh2, sc2), w_up[l], w_down[l]),
                       ln2_g[l], ln2_b[l])

        if not last:
            oc = diff_attention(qc, kc, vc, lam)
            mix_c = jnp.concatenate([
                diff_head_out(oc, subln_w[l], lam_init),
                short_conv(uc, gbc, gcc, conv_w[l], conv_b[l]),
                fourier_mix(fc)], axis=-1) @ w_out[l]
            ctx = layer_norm(DEEPNORM_ALPHA * ctx + cg1 * mix_c, ln1_g[l], ln1_b[l])
            ctx = layer_norm(DEEPNORM_ALPHA * ctx + cg2 * squared_relu_mlp(modulate(ctx, csh2, csc2), w_up[l], w_down[l]),
                             ln2_g[l], ln2_b[l])
    return x


EPS = 1e-6

MLA_HEADS = D_MODEL // 128
MLA_NOPE = 64
MLA_ROPE = 32
MLA_QK = MLA_NOPE + MLA_ROPE
MLA_V = 64
Q_LORA = 3 * D_MODEL // 8
KV_LORA = D_MODEL // 4
MLA_IN = Q_LORA + KV_LORA + MLA_ROPE
CONV_CH = D_MODEL // 2
CONV_K = 31
EVEN_IN = MLA_IN + 2 * CONV_CH
EVEN_OUT = MLA_HEADS * MLA_V + CONV_CH

RW_N = 64
RW_HEADS = D_MODEL // 128
RW_DIM = RW_HEADS * RW_N
DECAY_LORA = 64
ICLR_LORA = 64
GATE_LORA = 128
SHIFT_K = 3
RW_IN = 3 * RW_DIM + 2 * DECAY_LORA + 2 * ICLR_LORA + GATE_LORA
GN_EPS = 64e-5

NA_HEADS = D_MODEL // 128
NA_DIM = 64
WIN_H = 8
WIN_W = 16
NA_IN = 3 * NA_HEADS * NA_DIM
ODD_IN = RW_IN + NA_IN
ODD_OUT = RW_DIM + NA_HEADS * NA_DIM

N_EXPERTS = 16
D_EXPERT = D_MODEL
EC_FACTOR = 2


def rms_norm_2(x, g):
    xf = x.astype(jnp.float32)
    y = xf * lax.rsqrt(jnp.mean(jnp.square(xf), -1, keepdims=True) + EPS)
    return (y * g.astype(jnp.float32)).astype(x.dtype)

def layer_norm_2(x, g, b):
    xf = x.astype(jnp.float32)
    mu = jnp.mean(xf, -1, keepdims=True)
    var = jnp.mean(jnp.square(xf - mu), -1, keepdims=True)
    y = (xf - mu) * lax.rsqrt(var + EPS)
    return (y * g.astype(jnp.float32) + b.astype(jnp.float32)).astype(x.dtype)

def head_group_norm(y, g, b):
    B, T, H, N = y.shape
    mu = jnp.mean(y, -1, keepdims=True)
    var = jnp.mean(jnp.square(y - mu), -1, keepdims=True)
    yn = ((y - mu) * lax.rsqrt(var + GN_EPS)).reshape(B, T, H * N)
    return yn * g + b

def depthwise_conv(x, w):
    pad = (w.shape[0] - 1) // 2
    return lax.conv_general_dilated(x, w[:, None, :].astype(x.dtype), (1,), [(pad, pad)],
                                    dimension_numbers=('NWC', 'WIO', 'NWC'),
                                    feature_group_count=x.shape[-1])

def axial_rope_tables(n_tok, rot_dim):
    t = jnp.arange(n_tok, dtype=jnp.int32)
    row = (t // GRID_W).astype(jnp.float32)
    col = (t % GRID_W).astype(jnp.float32)
    half = rot_dim // 2
    inv = ROPE_BASE ** (-jnp.arange(0, half, 2, dtype=jnp.float32) / half)
    ar = row[:, None] * inv
    ac = col[:, None] * inv
    ang = jnp.concatenate([ar, ar, ac, ac], -1)
    return jnp.cos(ang), jnp.sin(ang)

def rotate_half(u):
    u1, u2 = jnp.split(u, 2, -1)
    return jnp.concatenate([-u2, u1], -1)

def apply_axial_rope(x, cos, sin):
    half = x.shape[-1] // 2
    rot = jnp.concatenate([rotate_half(x[..., :half]), rotate_half(x[..., half:])], -1)
    return (x * cos[:, None, :] + rot * sin[:, None, :]).astype(x.dtype)

def dense_attention(q, k, v):
    scale = q.shape[-1] ** -0.5
    s = jnp.einsum('bqhd,bkhd->bhqk', q, k).astype(jnp.float32) * scale
    p = jax.nn.softmax(s, -1).astype(v.dtype)
    return jnp.einsum('bhqk,bkhd->bqhd', p, v)

def blocked_attention(q, k, v):
    B, T, H, D = q.shape
    nb = T // Q_BLOCK
    qb = jnp.moveaxis(q.reshape(B, nb, Q_BLOCK, H, D), 1, 0)
    out = lax.map(lambda qq: dense_attention(qq, k, v), qb)
    return jnp.moveaxis(out, 0, 1).reshape(B, T, H, v.shape[-1])

def mla_qkv(u, q_norm, w_uq, kv_norm, w_ukv, q_g, k_g, rope_cs=None):
    B, T, _ = u.shape
    cq = u[..., :Q_LORA]
    ckv = u[..., Q_LORA:Q_LORA + KV_LORA]
    kr = u[..., Q_LORA + KV_LORA:MLA_IN]
    q = (rms_norm_2(cq, q_norm) @ w_uq).reshape(B, T, MLA_HEADS, MLA_QK)
    kv = (rms_norm_2(ckv, kv_norm) @ w_ukv).reshape(B, T, MLA_HEADS, MLA_NOPE + MLA_V)
    k_nope, v = kv[..., :MLA_NOPE], kv[..., MLA_NOPE:]
    k = jnp.concatenate([k_nope, jnp.broadcast_to(kr[:, :, None, :], (B, T, MLA_HEADS, MLA_ROPE))], -1)
    q = rms_norm_2(q, q_g)
    k = rms_norm_2(k, k_g)
    if rope_cs is not None:
        cos, sin = rope_cs
        q = jnp.concatenate([q[..., :MLA_NOPE], apply_axial_rope(q[..., MLA_NOPE:], cos, sin)], -1)
        k = jnp.concatenate([k[..., :MLA_NOPE], apply_axial_rope(k[..., MLA_NOPE:], cos, sin)], -1)
    return q, k, v

def conformer_conv(u, dw_w, dw_b, ln_g, ln_b):
    a, gate = jnp.split(u, 2, -1)
    h = a * jax.nn.sigmoid(gate)
    h = depthwise_conv(h, dw_w) + dw_b
    return jax.nn.silu(layer_norm_2(h, ln_g, ln_b))

def even_mixer(h, hc, rope_cs, w_in, w_out, q_norm, w_uq, kv_norm, w_ukv, q_g, k_g,
               dw_w, dw_b, ln_g, ln_b, with_ctx_out):
    B, T, _ = h.shape
    u = h @ w_in
    uc = hc @ w_in
    mla_p = (q_norm, w_uq, kv_norm, w_ukv, q_g, k_g)
    q, k, v = mla_qkv(u[..., :MLA_IN], *mla_p, rope_cs=rope_cs)
    qc, kc, vc = mla_qkv(uc[..., :MLA_IN], *mla_p)
    o_att = blocked_attention(q, jnp.concatenate([k, kc], 1), jnp.concatenate([v, vc], 1))
    o_conv = conformer_conv(u[..., MLA_IN:], dw_w, dw_b, ln_g, ln_b)
    y = jnp.concatenate([o_att.reshape(B, T, -1), o_conv], -1) @ w_out
    if not with_ctx_out:
        return y, None
    oc_att = dense_attention(qc, kc, vc)
    oc_conv = conformer_conv(uc[..., MLA_IN:], dw_w, dw_b, ln_g, ln_b)
    yc = jnp.concatenate([oc_att.reshape(B, hc.shape[1], -1), oc_conv], -1) @ w_out
    return y, yc

def wkv7_step(S, inp):
    r, w, k, v, a, b = inp
    sa = jnp.einsum('bhvk,bhk->bhv', S, a)
    S = S * w[:, :, None, :] + sa[..., None] * b[:, :, None, :] + v[..., None] * k[:, :, None, :]
    return S, jnp.einsum('bhvk,bhk->bhv', S, r)

def wkv7_scan(S0, r, w, k, v, a, b, reverse):
    xs = tuple(jnp.moveaxis(t.astype(jnp.float32), 1, 0) for t in (r, w, k, v, a, b))
    S, ys = lax.scan(wkv7_step, S0, xs, reverse=reverse)
    return S, jnp.moveaxis(ys, 0, 1)

def rwkv_inputs(u, shift_w, w0, w2, a0, a2, g2, k_k, k_a):
    u = depthwise_conv(u, shift_w)
    B, T, _ = u.shape
    o1 = 3 * RW_DIM
    o2 = o1 + 2 * DECAY_LORA
    o3 = o2 + 2 * ICLR_LORA
    r, k, v = jnp.split(u[..., :o1], 3, axis=-1)
    lw = u[..., o1:o2].reshape(B, T, 2, DECAY_LORA)
    la = u[..., o2:o3].reshape(B, T, 2, ICLR_LORA)
    lg = u[..., o3:]
    logw = (w0 + jnp.einsum('btdr,drc->btdc', jnp.tanh(lw), w2)).astype(jnp.float32)
    w = jnp.exp(-jnp.exp(-jax.nn.softplus(-logw) - 0.5))
    a = jax.nn.sigmoid((a0 + jnp.einsum('btdr,drc->btdc', la, a2)).astype(jnp.float32))
    kk = (k * k_k).reshape(B, T, RW_HEADS, RW_N).astype(jnp.float32)
    kk = kk * lax.rsqrt(jnp.sum(kk * kk, -1, keepdims=True) + 1e-12)
    k_eff = k[:, :, None, :].astype(jnp.float32) * (1.0 + (a - 1.0) * k_a)
    g = jax.nn.sigmoid(lg) @ g2
    hd = lambda t: t.reshape(B, T, RW_HEADS, RW_N).astype(jnp.float32)
    dir_hd = lambda t: t.reshape(B, T, 2, RW_HEADS, RW_N)
    return hd(r), hd(v), kk, dir_hd(w), dir_hd(a), dir_hd(k_eff), g

def rwkv_mixer(u, uc, shift_w, w0, w2, a0, a2, g2, k_k, k_a, r_k, gn_g, gn_b, with_ctx_out):
    p = (shift_w, w0, w2, a0, a2, g2, k_k, k_a)
    lat = rwkv_inputs(u, *p)
    cx = rwkv_inputs(uc, *p)
    rk = r_k.reshape(RW_HEADS, RW_N).astype(jnp.float32)
    B = u.shape[0]

    def direction(inp, d, S0):
        r, v, kk, w, a, k_eff, _ = inp
        a_d, k_d = a[:, :, d], k_eff[:, :, d]
        S, y = wkv7_scan(S0, r, w[:, :, d], k_d, v, -kk, kk * a_d, reverse=(d == 1))
        return S, y + jnp.sum(r * k_d * rk, -1, keepdims=True) * v

    y_lat, y_ctx = [], []
    for d in range(2):
        S0 = jnp.zeros((B, RW_HEADS, RW_N, RW_N), jnp.float32)
        S_c, yc_d = direction(cx, d, S0)
        _, yl_d = direction(lat, d, S_c)
        y_lat.append(yl_d)
        y_ctx.append(yc_d)
    y = head_group_norm(y_lat[0] + y_lat[1], gn_g, gn_b) * lat[6]
    if not with_ctx_out:
        return y, None
    yc = head_group_norm(y_ctx[0] + y_ctx[1], gn_g, gn_b) * cx[6]
    return y, yc

def natten_qkv(u, q_g, k_g):
    B, T, _ = u.shape
    q, k, v = [t.reshape(B, T, NA_HEADS, NA_DIM) for t in jnp.split(u, 3, -1)]
    return rms_norm_2(q, q_g), rms_norm_2(k, k_g), v

def neighbourhood_attention(q, k, v, k_ctx, v_ctx, rpb):
    B, T, H, Dh = q.shape
    rows = T // GRID_W
    kh = min(WIN_H, rows)
    kw = min(WIN_W, GRID_W)
    n_loc = kh * kw
    scale = Dh ** -0.5
    qg = q.reshape(B, rows, GRID_W, H, Dh)
    kg = k.reshape(B, rows, GRID_W, H, Dh)
    vg = v.reshape(B, rows, GRID_W, H, Dh)
    cols = jnp.arange(GRID_W, dtype=jnp.int32)
    col_start = jnp.clip(cols - kw // 2, 0, GRID_W - kw)
    col_idx = col_start[:, None] + jnp.arange(kw, dtype=jnp.int32)[None, :]
    dcol = col_idx - cols[:, None] + (WIN_W - 1)

    def one_row(r):
        rs = jnp.clip(r - kh // 2, 0, rows - kh)
        k_band = lax.dynamic_slice_in_dim(kg, rs, kh, axis=1)
        v_band = lax.dynamic_slice_in_dim(vg, rs, kh, axis=1)
        k_win = k_band[:, :, col_idx]
        v_win = v_band[:, :, col_idx]
        q_row = lax.dynamic_index_in_dim(qg, r, axis=1, keepdims=False)
        drow = rs + jnp.arange(kh, dtype=jnp.int32) - r + (WIN_H - 1)
        bias = jnp.transpose(rpb[:, drow][:, :, dcol], (0, 2, 1, 3))
        s_loc = jnp.einsum('bchd,bicjhd->bhcij', q_row, k_win).astype(jnp.float32) * scale + bias.astype(jnp.float32)
        s_ctx = jnp.einsum('bchd,bnhd->bhcn', q_row, k_ctx).astype(jnp.float32) * scale
        s = jnp.concatenate([s_loc.reshape(B, H, GRID_W, n_loc), s_ctx], -1)
        p = jax.nn.softmax(s, -1).astype(v.dtype)
        o = jnp.einsum('bhcij,bicjhd->bchd', p[..., :n_loc].reshape(B, H, GRID_W, kh, kw), v_win)
        return o + jnp.einsum('bhcn,bnhd->bchd', p[..., n_loc:], v_ctx)

    out = lax.map(one_row, jnp.arange(rows, dtype=jnp.int32))
    return jnp.moveaxis(out, 0, 1).reshape(B, T, H, Dh)

def odd_mixer(h, hc, w_in, w_out, shift_w, w0, w2, a0, a2, g2, k_k, k_a, r_k, gn_g, gn_b,
              q_g, k_g, rpb, with_ctx_out):
    B, T, _ = h.shape
    u = h @ w_in
    uc = hc @ w_in
    y_rw, yc_rw = rwkv_mixer(u[..., :RW_IN], uc[..., :RW_IN], shift_w, w0, w2, a0, a2, g2,
                             k_k, k_a, r_k, gn_g, gn_b, with_ctx_out)
    q, k, v = natten_qkv(u[..., RW_IN:], q_g, k_g)
    qc, kc, vc = natten_qkv(uc[..., RW_IN:], q_g, k_g)
    y_na = neighbourhood_attention(q, k, v, kc, vc, rpb)
    y = jnp.concatenate([y_rw, y_na.reshape(B, T, -1)], -1) @ w_out
    if not with_ctx_out:
        return y, None
    yc_na = dense_attention(qc, kc, vc)
    yc = jnp.concatenate([yc_rw, yc_na.reshape(B, hc.shape[1], -1)], -1) @ w_out
    return y, yc

def expert_choice_ffn(h, router, w1, w3, w2):
    B, T, D = h.shape
    cap = max(1, EC_FACTOR * T // N_EXPERTS)
    aff = jax.nn.softmax(jnp.einsum('btd,de->bte', h, router).astype(jnp.float32), -1)
    gate, idx = lax.top_k(jnp.swapaxes(aff, 1, 2), cap)
    xs = jax.vmap(lambda hb, ib: hb[ib])(h, idx)
    hid = jax.nn.silu(jnp.einsum('becd,edf->becf', xs, w1)) * jnp.einsum('becd,edf->becf', xs, w3)
    ys = jnp.einsum('becf,efd->becd', hid, w2) * gate[..., None].astype(h.dtype)
    return jax.vmap(lambda yb, ib: jnp.zeros((T, D), yb.dtype).at[ib.reshape(-1)].add(yb.reshape(-1, D)))(ys, idx)

def second_inputs(seed: int = 0) -> dict:
    key = jax.random.key(seed)
    keys = iter(jax.random.split(key, 64))

    def nrm(shape, scale):
        return jax.random.normal(next(keys), shape, jnp.float32) * scale

    def gain(shape):
        return 1.0 + nrm(shape, 0.05)

    ne, no = (DEPTH + 1) // 2, DEPTH // 2
    d = D_MODEL
    shift_base = jnp.array([0.25, 0.5, 0.25], jnp.float32)[None, :, None]
    return {
        'x': nrm((BATCH, SEQ, d), 1.0),
        'c': nrm((BATCH, d), 1.0),
        'ctx': nrm((BATCH, CTX_LEN, d), 1.0),
        'c_ctx': nrm((d,), 1.0),
        'ada_w': nrm((DEPTH, d, 6 * d), 0.5 * d ** -0.5),
        'ada_b': nrm((DEPTH, 6 * d), 0.02),
        'norm1_g': gain((DEPTH, d)),
        'norm2_g': gain((DEPTH, d)),
        'ev_w_in': nrm((ne, d, EVEN_IN), d ** -0.5),
        'ev_w_out': nrm((ne, EVEN_OUT, d), EVEN_OUT ** -0.5),
        'mla_q_norm': gain((ne, Q_LORA)),
        'mla_w_uq': nrm((ne, Q_LORA, MLA_HEADS * MLA_QK), Q_LORA ** -0.5),
        'mla_kv_norm': gain((ne, KV_LORA)),
        'mla_w_ukv': nrm((ne, KV_LORA, MLA_HEADS * (MLA_NOPE + MLA_V)), KV_LORA ** -0.5),
        'mla_q_g': gain((ne, MLA_QK)),
        'mla_k_g': gain((ne, MLA_QK)),
        'cv_dw_w': nrm((ne, CONV_K, CONV_CH), CONV_K ** -0.5),
        'cv_dw_b': nrm((ne, CONV_CH), 0.02),
        'cv_ln_g': gain((ne, CONV_CH)),
        'cv_ln_b': nrm((ne, CONV_CH), 0.02),
        'od_w_in': nrm((no, d, ODD_IN), d ** -0.5),
        'od_w_out': nrm((no, ODD_OUT, d), ODD_OUT ** -0.5),
        'rw_shift_w': shift_base + nrm((no, SHIFT_K, RW_IN), 0.1),
        'rw_w0': jax.random.uniform(next(keys), (no, 2, RW_DIM), jnp.float32, -4.0, 1.0),
        'rw_w2': nrm((no, 2, DECAY_LORA, RW_DIM), 0.5 * DECAY_LORA ** -0.5),
        'rw_a0': nrm((no, 2, RW_DIM), 0.5),
        'rw_a2': nrm((no, 2, ICLR_LORA, RW_DIM), 0.5 * ICLR_LORA ** -0.5),
        'rw_g2': nrm((no, GATE_LORA, RW_DIM), GATE_LORA ** -0.5),
        'rw_k_k': 0.85 + nrm((no, RW_DIM), 0.05),
        'rw_k_a': gain((no, RW_DIM)),
        'rw_r_k': nrm((no, RW_DIM), 0.3),
        'rw_gn_g': gain((no, RW_DIM)),
        'rw_gn_b': nrm((no, RW_DIM), 0.02),
        'na_q_g': gain((no, NA_DIM)),
        'na_k_g': gain((no, NA_DIM)),
        'na_rpb': nrm((no, NA_HEADS, 2 * WIN_H - 1, 2 * WIN_W - 1), 0.5),
        'moe_router': nrm((DEPTH, d, N_EXPERTS), d ** -0.5),
        'moe_w1': nrm((DEPTH, N_EXPERTS, d, D_EXPERT), d ** -0.5),
        'moe_w3': nrm((DEPTH, N_EXPERTS, d, D_EXPERT), d ** -0.5),
        'moe_w2': nrm((DEPTH, N_EXPERTS, D_EXPERT, d), D_EXPERT ** -0.5),
    }

def second_block(x, c, ctx, c_ctx, ada_w, ada_b, norm1_g, norm2_g,
              ev_w_in, ev_w_out, mla_q_norm, mla_w_uq, mla_kv_norm, mla_w_ukv, mla_q_g, mla_k_g,
              cv_dw_w, cv_dw_b, cv_ln_g, cv_ln_b,
              od_w_in, od_w_out, rw_shift_w, rw_w0, rw_w2, rw_a0, rw_a2, rw_g2, rw_k_k, rw_k_a, rw_r_k,
              rw_gn_g, rw_gn_b, na_q_g, na_k_g, na_rpb,
              moe_router, moe_w1, moe_w3, moe_w2):
    rope_cs = axial_rope_tables(x.shape[1], MLA_ROPE)
    for i in range(DEPTH):
        last = i == DEPTH - 1
        j = i // 2
        mod = jnp.einsum('bd,de->be', jax.nn.silu(c), ada_w[i]) + ada_b[i]
        mod_c = jax.nn.silu(c_ctx) @ ada_w[i] + ada_b[i]
        sh1, sc1, g1, sh2, sc2, g2 = jnp.split(mod[:, None, :], 6, -1)
        csh1, csc1, cg1, csh2, csc2, cg2 = jnp.split(mod_c[None, None, :], 6, -1)
        h = rms_norm_2(x, norm1_g[i]) * (1.0 + sc1) + sh1
        hc = rms_norm_2(ctx, norm1_g[i]) * (1.0 + csc1) + csh1
        if i % 2 == 0:
            y, yc = even_mixer(h, hc, rope_cs, ev_w_in[j], ev_w_out[j], mla_q_norm[j], mla_w_uq[j],
                               mla_kv_norm[j], mla_w_ukv[j], mla_q_g[j], mla_k_g[j],
                               cv_dw_w[j], cv_dw_b[j], cv_ln_g[j], cv_ln_b[j], not last)
        else:
            y, yc = odd_mixer(h, hc, od_w_in[j], od_w_out[j], rw_shift_w[j], rw_w0[j], rw_w2[j],
                              rw_a0[j], rw_a2[j], rw_g2[j], rw_k_k[j], rw_k_a[j], rw_r_k[j],
                              rw_gn_g[j], rw_gn_b[j], na_q_g[j], na_k_g[j], na_rpb[j], not last)
        x = x + g1 * y
        h = rms_norm_2(x, norm2_g[i]) * (1.0 + sc2) + sh2
        x = x + g2 * expert_choice_ffn(h, moe_router[i], moe_w1[i], moe_w3[i], moe_w2[i])
        if not last:
            ctx = ctx + cg1 * yc
            hc = rms_norm_2(ctx, norm2_g[i]) * (1.0 + csc2) + csh2
            ctx = ctx + cg2 * expert_choice_ffn(hc, moe_router[i], moe_w1[i], moe_w3[i], moe_w2[i])
    return x


def setup_inputs(seed=0):
    out = dict(first_inputs(seed))
    for name, value in second_inputs(seed + 1).items():
        if name != "x":
            out[name + "_2"] = value
    return out


def reference(
    x, c, ctx, c_ctx, w_mod, b_mod, w_in, diff_lambda, subln_w, conv_w, conv_b, w_out, ln1_g,
    ln1_b, w_up, w_down, ln2_g, ln2_b, c_2, ctx_2, c_ctx_2, ada_w_2, ada_b_2, norm1_g_2,
    norm2_g_2, ev_w_in_2, ev_w_out_2, mla_q_norm_2, mla_w_uq_2, mla_kv_norm_2, mla_w_ukv_2,
    mla_q_g_2, mla_k_g_2, cv_dw_w_2, cv_dw_b_2, cv_ln_g_2, cv_ln_b_2, od_w_in_2, od_w_out_2,
    rw_shift_w_2, rw_w0_2, rw_w2_2, rw_a0_2, rw_a2_2, rw_g2_2, rw_k_k_2, rw_k_a_2, rw_r_k_2,
    rw_gn_g_2, rw_gn_b_2, na_q_g_2, na_k_g_2, na_rpb_2, moe_router_2, moe_w1_2, moe_w3_2,
    moe_w2_2,
):
    x = first_block(
        x, c, ctx, c_ctx, w_mod, b_mod, w_in, diff_lambda, subln_w, conv_w, conv_b, w_out,
        ln1_g, ln1_b, w_up, w_down, ln2_g, ln2_b,
    )
    return second_block(
        x, c_2, ctx_2, c_ctx_2, ada_w_2, ada_b_2, norm1_g_2, norm2_g_2, ev_w_in_2, ev_w_out_2,
        mla_q_norm_2, mla_w_uq_2, mla_kv_norm_2, mla_w_ukv_2, mla_q_g_2, mla_k_g_2, cv_dw_w_2,
        cv_dw_b_2, cv_ln_g_2, cv_ln_b_2, od_w_in_2, od_w_out_2, rw_shift_w_2, rw_w0_2, rw_w2_2,
        rw_a0_2, rw_a2_2, rw_g2_2, rw_k_k_2, rw_k_a_2, rw_r_k_2, rw_gn_g_2, rw_gn_b_2, na_q_g_2,
        na_k_g_2, na_rpb_2, moe_router_2, moe_w1_2, moe_w3_2, moe_w2_2,
    )


_drawn_inputs = setup_inputs


def setup_inputs(seed=0):
    import zlib

    import numpy as np

    out = dict(_drawn_inputs(seed))
    spreads = {}
    factors = {'diff_lambda': 2.741,
     'subln_w': 8.0,
     'conv_b': 8.0,
     'ada_b_2': 2.877,
     'norm1_g_2': 4.324,
     'norm2_g_2': 3.803,
     'mla_q_norm_2': 8.0,
     'mla_w_uq_2': 2.79,
     'mla_kv_norm_2': 8.0,
     'mla_q_g_2': 8.0,
     'mla_k_g_2': 8.0,
     'cv_dw_b_2': 8.0,
     'cv_ln_g_2': 6.69,
     'cv_ln_b_2': 8.0,
     'rw_w2_2': 6.889,
     'rw_a2_2': 3.237,
     'rw_k_k_2': 5.409,
     'rw_k_a_2': 4.45,
     'rw_r_k_2': 3.6,
     'rw_gn_g_2': 8.0,
     'rw_gn_b_2': 8.0,
     'na_q_g_2': 8.0,
     'na_k_g_2': 8.0,
     'na_rpb_2': 8.0}
    for name, (base, spread) in spreads.items():
        noise = np.random.default_rng([zlib.crc32(name.encode()), seed]).standard_normal(out[name].shape)
        drawn = base * np.exp(spread * noise) if base else spread * noise
        out[name] = __import__('jax').numpy.asarray(drawn.astype(out[name].dtype))
    for name, factor in factors.items():
        out[name] = (out[name] * factor).astype(out[name].dtype)
    return out
```

```python
import math
from contextlib import ExitStack

import numpy as np

import concourse.bass as bass
from concourse import mybir

F32 = mybir.dt.float32
ALU = mybir.AluOpType
ACT = mybir.ActivationFunctionType
AX = mybir.AxisListType.X

P = 128
D = 1024
KD = D // P
T = 256
TT = 2 * T
X, C = slice(0, T), slice(T, TT)
SEGS = (X, C)
DEPTH = 2
FF = 4 * D
RING = 6
SLOT = 4096
NBANK = 8
ALPHA = (2 * DEPTH) ** 0.25
NE = 16
CAP = 32
CH = 64
GRID_W = 64


def column_parts(w, step=512):
    rows, cols = w
    return [(0, rows, c, min(c + step, cols)) for c in range(0, cols, step)]


def ranges(rows, *cuts):
    return [(0, rows, a, b) for a, b in cuts]


PARTS = {
    "w_mod": column_parts((D, 6 * D)),
    "w_in": column_parts((D, 2560)),
    "w_out": column_parts((D, D)),
    "w_up": column_parts((D, FF)),
    "w_down": [(r, r + D, c, c + 512) for c in (0, 512) for r in range(0, FF, D)],
    "ada_w": column_parts((D, 6 * D)),
    "ev_w_in": ranges(D, (0, 384), (384, 672), (672, 1184), (1184, 1696)),
    "ev_w_out": column_parts((D, D)),
    "w_uq": ranges(384, (0, 768)),
    "w_ukv": ranges(256, (0, 1024)),
    "router": ranges(D, (0, NE)),
    "od_w_in": ranges(D, (1920, 2432), (2432, 2944), (2944, 3456), (0, 512), (512, 1024), (1024, 1536), (1536, 1920)),
    "lora": ranges(384, (0, 512)),
    "od_w_out": column_parts((D, D)),
    "moe": column_parts((D, D)),
}

COLS = {
    "c": D, "c_ctx": D, "c_2": D, "c_ctx_2": D,
    "b_mod0": 6 * D, "b_mod1": 6 * D, "ada_b0": 6 * D, "ada_b1": 6 * D,
    "subln0": P, "subln1": P,
    "conv_w0": 3 * T, "conv_w1": 3 * T, "conv_b0": T, "conv_b1": T,
    "ln1_g0": D, "ln1_b0": D, "ln2_g0": D, "ln2_b0": D,
    "ln1_g1": D, "ln1_b1": D, "ln2_g1": D, "ln2_b1": D,
    "norm1_g0": D, "norm1_g1": D, "norm2_g0": D, "norm2_g1": D,
    "q_norm": 384, "kv_norm": 256, "q_g": P, "k_g": P,
    "dw_w": 31 * 512, "dw_b": 512, "cln_g": 512, "cln_b": 512,
    "shift_w": 3 * 1920, "w0": 1024, "a0": 1024, "k_k": 512, "k_a": 512, "r_k": 512,
    "gn_g": 512, "gn_b": 512, "na_q": P, "na_k": P,
}
COL_AT, NCOL = {}, 0
for _name, _n in COLS.items():
    COL_AT[_name] = NCOL
    NCOL += _n // P

CONSTS = {
    "ident": 128, "ones": 128, "pair": 128, "swap1": 128, "cos1": 256, "sin1": 256,
    "swap2": 128, "cos2": 256, "sin2": 256, "cn": 512, "sn": 512, "cm": 128, "sm": 128,
    "tri": 128, "iota": 64, "window": 512, "causal": 256, "level": 768,
    "flip": 128,
}
CONST_AT, NCONST = {}, 0
for _name, _n in CONSTS.items():
    CONST_AT[_name] = NCONST
    NCONST += _n


class Kit:

    def __init__(self, nc, ctx, dram):
        self.nc, self.ctx, self.dram = nc, ctx, dram
        self.times = 1
        self.sems, self.given, self.base = {}, {}, {}
        self.stream, self.cursor, self.issued, self.stages = [], 0, 0, 0
        self.ring = self.sb("ring", [P, RING, SLOT])
        self.XT = self.sb("XT", [P, KD, TT])
        self.HT = self.sb("HT", [P, KD, TT])
        self.arena = self.sb("arena", [P, 18432])
        self.cols = self.sb("cols", [P, NCOL])
        self.base_consts = self.sb("base_consts", [P, 3 * 128])
        self.sil = self.sb("sil", [P, 2, KD, 32])
        self.modcol = self.sb("modcol", [P, 2, 48])
        self.gain = self.sb("gain", [P, 2, KD])
        self.small = self.sb("small", [P, 80])
        self.ps = ctx.enter_context(nc.psum_tensor("ps", [P, NBANK, 512], F32))
        self.ident = self.base_consts[:, 0:128]
        self.ones = self.base_consts[:, 128:256]
        self.pair = self.base_consts[:, 256:384]

    def sb(self, name, shape):
        return self.ctx.enter_context(self.nc.sbuf_tensor(name, shape, F32))

    def block(self, name):
        self.stages += 1
        return self.nc.Block(f"{name}_{self.stages}")

    def sem(self, name):
        if name not in self.sems:
            self.sems[name] = self.ctx.enter_context(self.nc.semaphore(name))
            self.given[name] = self.base[name] = 0
        return self.sems[name]

    def inc(self, name, n=1):
        s = self.sem(name)
        self.given[name] += n * self.times
        return s, n

    def at(self, name, n):
        return self.sem(name), self.base[name] + n

    def end_stage(self):
        self.base = dict(self.given)

    def step(self, eng, ins, name):
        s, n = self.inc(name)
        ins.then_inc(s, n)
        eng.wait_ge(s, self.given[name])

    def col(self, name, i=0, n=1):
        return self.cols[:, COL_AT[name] + i:COL_AT[name] + i + n]

    def plan(self, name, layer=None, parts=None):
        at = 0
        flat = self.dram[name] if layer is None else self.dram[name][layer]
        for r0, r1, c0, c1 in parts or PARTS[name]:
            n = (r1 - r0) * (c1 - c0)
            self.stream.append((flat[at:at + n], (r1 - r0) // P, c1 - c0))
            at += n

    def slot(self, i):
        _, kc, w = self.stream[i]
        return self.ring[:, i % RING, 0:kc * w].rearrange("p (k w) -> p k w", k=kc)

    def load_next(self, sp):
        i = self.issued
        if i < len(self.stream):
            src, kc, w = self.stream[i]
            sp.dma_start(self.ring[:, i % RING, 0:kc * w], src.rearrange("(p n) -> p n", p=P)).then_inc(
                self.sem(f"slot{i % RING}_landed"), 16)
        self.issued += 1

    def landed(self, i):
        return self.sem(f"slot{i % RING}_landed"), 16 * (i // RING + 1)


def evacuate(K, side, out, in_, scale=None, bias=None):
    nc = K.nc
    if side == "act":
        kw = {}
        if scale is not None:
            kw["scale"] = scale
        if bias is not None:
            kw["bias"] = bias
        return nc.scalar.activation(out, in_, ACT.Identity if kw else ACT.Copy, **kw)
    if scale is None and bias is None:
        return nc.vector.tensor_copy(out, in_)
    if bias is None:
        return nc.vector.tensor_scalar(out, in_, scale, None, ALU.mult)
    if scale is None:
        return nc.vector.tensor_scalar(out, in_, bias, None, ALU.add)
    return nc.vector.tensor_scalar(out, in_, scale, bias, ALU.mult, ALU.add)


def gemm_stage(K, npieces, jobs, name="gemm", feed=None):
    nc, first = K.nc, K.cursor
    uses = [max(j for j, job in enumerate(jobs) if i in job["pieces"]) for i in range(npieces)]
    sides = [job.get("only") or ("act", "dve")[j % 2] for j, job in enumerate(jobs)]
    turn = [sides[:j + 1].count(sides[j]) for j in range(len(jobs))]

    def bank_of(job, j):
        p0, p1 = job["rows"]
        return K.ps[p0:p1, j % NBANK, 0:job["n"]]

    with K.block(name) as block:
        @block.sync
        def _(sp):
            for i in range(npieces):
                if feed is None or i < feed:
                    sp.wait_ge(*K.at("products_done", uses[i] + 1))
                    K.load_next(sp)

        @block.tensor
        def _(pe):
            seen = set()
            for j, job in enumerate(jobs):
                for i in job["pieces"]:
                    if i not in seen:
                        seen.add(i)
                        pe.wait_ge(*K.landed(first + i))
                if j >= NBANK:
                    pe.wait_ge(*K.at(sides[j - NBANK] + "_evacuated", turn[j - NBANK]))
                if "emit" in job:
                    last = job["emit"](j % NBANK)
                else:
                    terms = job["mm"]([K.slot(first + i) for i in job["pieces"]])
                    for n, (lhsT, rhs) in enumerate(terms):
                        last = nc.tensor.matmul(bank_of(job, j), lhsT, rhs, start=n == 0, stop=n == len(terms) - 1)
                last.then_inc(*K.inc("products_done"))

        @block.scalar
        def _(act):
            for j, job in enumerate(jobs):
                if sides[j] == "act":
                    act.wait_ge(*K.at("products_done", j + 1))
                    job["evac"]("act", bank_of(job, j), act).then_inc(*K.inc("act_evacuated"))

        @block.vector
        def _(dve):
            for j, job in enumerate(jobs):
                if sides[j] == "dve":
                    dve.wait_ge(*K.at("products_done", j + 1))
                    job["evac"]("dve", bank_of(job, j), dve).then_inc(*K.inc("dve_evacuated"))
    K.cursor += npieces
    K.end_stage()


def feature_job(K, piece, c0, width, rhs, out, p0=0, scale=None, evac=None, only=None):
    n = rhs.shape[-1]
    return dict(
        pieces=[piece], rows=(p0, p0 + width), n=n, only=only,
        mm=lambda slots: [(slots[0][:, k, c0:c0 + width], rhs[:, k, :]) for k in range(slots[0].shape[1])],
        evac=evac or (lambda side, ps, eng: evacuate(K, side, out, ps, scale=scale)))


def token_job(K, piece, cols, lhs, t, out):
    return dict(
        pieces=[piece], rows=(0, P), n=out.shape[-1], only=None,
        mm=lambda slots: [(lhs[:, k, t * P:(t + 1) * P], cols(slots[0], k)) for k in range(slots[0].shape[1])],
        evac=lambda side, ps, eng: evacuate(K, side, out, ps))


def mod_stage(K, sil, bias, one_plus):
    nc, first, n = K.nc, K.cursor, 12
    rows = K.arena[:, 0:n * P].rearrange("p (n c) -> p n c", n=n)
    with K.block("modulation") as block:
        @block.sync
        def _(sp):
            for i in range(n):
                sp.wait_ge(*K.at("rows_done", i + 1))
                K.load_next(sp)

        @block.tensor
        def _(pe):
            def transpose(i):
                pe.wait_ge(*K.at("rows_kept", i + 1))
                if i >= 4:
                    pe.wait_ge(*K.at("columns_kept", i - 3))
                nc.tensor.transpose(K.ps[:, 4 + i % 4, 0:P], rows[:, i, :], K.ident).then_inc(*K.inc("columns_done"))
            for i in range(n):
                pe.wait_ge(*K.landed(first + i))
                if i >= 4:
                    pe.wait_ge(*K.at("rows_kept", i - 3))
                w = K.slot(first + i)
                for k in range(KD):
                    for j in range(4):
                        last = nc.tensor.matmul(K.ps[32 * j:32 * j + 32, i % 4, 0:P], sil[:, k, :],
                                                w[:, k, j * P:(j + 1) * P], start=k == 0, stop=k == KD - 1)
                last.then_inc(*K.inc("rows_done"))
                if i:
                    transpose(i - 1)
            transpose(n - 1)

        @block.scalar
        def _(act):
            for i in range(n):
                act.wait_ge(*K.at("rows_done", i + 1))
                nc.scalar.activation(rows[:, i, :], K.ps[:, i % 4, 0:P], ACT.Copy).then_inc(*K.inc("rows_kept"))

        @block.vector
        def _(dve):
            for i in range(n):
                dve.wait_ge(*K.at("columns_done", i + 1))
                got = K.ps[:, 4 + i % 4, 0:P].rearrange("p (j r) -> p r j", r=32)
                b = bias[:, 4 * i:4 * i + 4]
                nc.vector.tensor_tensor(K.modcol[:, 0, 4 * i:4 * i + 4], got[:, 0, :], b, ALU.add)
                nc.vector.tensor_tensor(K.modcol[:, 1, 4 * i:4 * i + 4], got[:, 1, :], b, ALU.add)\
                    .then_inc(*K.inc("columns_kept"))
            dve.wait_ge(*K.at("columns_kept", n))
            for j in one_plus:
                nc.vector.tensor_scalar(K.modcol[:, :, 8 * j:8 * j + 8], K.modcol[:, :, 8 * j:8 * j + 8],
                                        1.0, None, ALU.add)
    K.cursor += n
    K.end_stage()


def mod(K, which, seg, k):
    return K.modcol[:, seg, 8 * which + k:8 * which + k + 1]


def modulate_stage(K, shift, scale, n_seg):
    nc = K.nc
    with K.block("modulate") as block:
        @block.scalar
        def _(act):
            for k in range(0, KD, 2):
                for s in range(n_seg):
                    nc.scalar.activation(K.HT[:, k, SEGS[s]], K.XT[:, k, SEGS[s]], ACT.Identity,
                                         bias=mod(K, shift, s, k), scale=mod(K, scale, s, k))

        @block.vector
        def _(dve):
            for k in range(1, KD, 2):
                for s in range(n_seg):
                    nc.vector.tensor_scalar(K.HT[:, k, SEGS[s]], K.XT[:, k, SEGS[s]],
                                            mod(K, scale, s, k), mod(K, shift, s, k), ALU.mult, ALU.add)
    K.end_stage()


def norm_stage(K, groups, work, centre=False):
    nc = K.nc
    sq = work[:, 0:4 * 512].rearrange("p (b n) -> p b n", b=4)
    root = work[:, 4 * 512:6 * 512].rearrange("p (b n) -> p b n", b=2)
    G = len(groups)
    firsts = [sum(len(g["src"]) for g in groups[:i]) for i in range(G + 1)]
    with K.block("norm") as block:
        @block.tensor
        def _(pe):
            for g, grp in enumerate(groups):
                p, m = grp["ones"].shape
                n = grp["src"][0].shape[-1]
                if centre:
                    if g:
                        pe.wait_ge(*K.at("means_done", g))
                    for i, s in enumerate(grp["src"]):
                        last = nc.tensor.matmul(K.ps[0:m, 7, 0:n], grp["ones"], s, start=i == 0, stop=i == len(grp["src"]) - 1)
                    last.then_inc(*K.inc("sums_done"))
                if g >= 4:
                    pe.wait_ge(*K.at("roots_done", g - 3))
                for i, s in enumerate(grp["src"]):
                    b = firsts[g] + i
                    pe.wait_ge(*K.at("squares_done", b + 1))
                    nc.tensor.matmul(K.ps[0:m, g % 4, 0:n], grp["ones"], sq[0:p, b % 4, 0:n], start=i == 0,
                                     stop=i == len(grp["src"]) - 1).then_inc(*K.inc("squares_summed"))

        @block.scalar
        def _(act):
            for g, grp in enumerate(groups):
                p, m = grp["ones"].shape
                n = grp["src"][0].shape[-1]
                if centre:
                    act.wait_ge(*K.at("sums_done", g + 1))
                    if g:
                        act.wait_ge(*K.at("centred", firsts[g]))
                    nc.scalar.mul(root[0:m, 1, 0:n], K.ps[0:m, 7, 0:n], grp["inv"]).then_inc(*K.inc("means_done"))
                for i, s in enumerate(grp["src"]):
                    b = firsts[g] + i
                    if centre:
                        act.wait_ge(*K.at("centred", b + 1))
                    if b >= 4:
                        act.wait_ge(*K.at("squares_summed", b - 3))
                    nc.scalar.activation(sq[0:p, b % 4, 0:n], s, ACT.Square).then_inc(*K.inc("squares_done"))
                r = 0 if centre else g % 2
                if g >= (1 if centre else 2):
                    act.wait_ge(*K.at("group_scaled", g if centre else g - 1))
                act.wait_ge(*K.at("squares_summed", firsts[g + 1]))
                nc.scalar.activation(root[0:m, r, 0:n], K.ps[0:m, g % 4, 0:n], ACT.Sqrt, bias=grp["eps"][0:m],
                                     scale=grp["inv"]).then_inc(*K.inc("roots_done"))

        @block.vector
        def _(dve):
            for g, grp in enumerate(groups):
                m = grp["ones"].shape[1]
                n = grp["src"][0].shape[-1]
                if centre:
                    dve.wait_ge(*K.at("means_done", g + 1))
                    for s in grp["src"]:
                        nc.vector.tensor_tensor(s, s, root[0:m, 1, 0:n], ALU.subtract).then_inc(*K.inc("centred"))
                    dve.wait_ge(*K.at("centred", firsts[g + 1]))
                r = 0 if centre else g % 2
                dve.wait_ge(*K.at("roots_done", g + 1))
                K.step(dve, nc.vector.reciprocal(root[0:m, r, 0:n], root[0:m, r, 0:n]), "dve_step")
                for dst, src, cs, gain, bias in grp["out"]:
                    rr = root[0:src.shape[0], r, cs]
                    if gain is None:
                        ins = nc.vector.tensor_tensor(dst, src, rr, ALU.mult)
                    else:
                        ins = nc.vector.scalar_tensor_tensor(out=dst, in0=src, scalar=gain, in1=rr, op0=ALU.mult, op1=ALU.mult)
                    if bias is not None:
                        K.step(dve, ins, "dve_step")
                        ins = nc.vector.tensor_scalar(dst, dst, bias, None, ALU.add)
                ins.then_inc(*K.inc("group_scaled"))
    K.end_stage()


def attention_stage(K, units, work, passes, name="attention"):
    nc, U = K.nc, len(units)
    E = work[:, 0:2048].rearrange("p (u s n) -> p u s n", u=2, s=2)
    A = work[:, 2048:3072].rearrange("p (u n) -> p u n", u=2)
    AT = work[:, 3072:4096].rearrange("p (u k q) -> p u k q", u=2, k=4)
    stat = K.small[:, 0:12].rearrange("p (u s c) -> p u s c", u=2, s=2)
    with K.block(name) as block:
        @block.tensor
        def _(pe):
            for i in range(U + 2):
                if i < U:
                    u = units[i]
                    if i >= 2:
                        pe.wait_ge(*K.at("exps_done", passes * (i - 1)))
                        if u["bias"] is not None:
                            pe.wait_ge(*K.at("biased", i - 1))
                    for s in range(passes):
                        last = nc.tensor.matmul(K.ps[:, 2 * (i % 2) + s, 0:u["k"].shape[-1]], u["q"][s], u["k"],
                                                start=True, stop=True)
                    last.then_inc(*K.inc("scores_done"))
                if 1 <= i <= U:
                    u, b = units[i - 1], (i - 1) % 2
                    pe.wait_ge(*K.at("probs_done", i))
                    if i >= 3:
                        pe.wait_ge(*K.at("probsT_done", i - 2))
                    for c in range(len(u["v"])):
                        last = nc.tensor.transpose(K.ps[:, 4 + b, c * P:(c + 1) * P], A[:, b, c * P:(c + 1) * P], K.ident)
                    last.then_inc(*K.inc("transposed"))
                if i >= 2:
                    u, b = units[i - 2], (i - 2) % 2
                    pe.wait_ge(*K.at("probsT_done", i - 1))
                    if i >= 4:
                        pe.wait_ge(*K.at("out_kept", i - 3))
                    for c, v in enumerate(u["v"]):
                        last = nc.tensor.matmul(K.ps[u["rows"][0]:u["rows"][1], 6 + b, 0:P], v, AT[:, b, c, :],
                                                start=c == 0, stop=c == len(u["v"]) - 1)
                    last.then_inc(*K.inc("values_done"))

        @block.scalar
        def _(act):
            for i in range(U + 1):
                if i < U:
                    u, b = units[i], i % 2
                    n = u["k"].shape[-1]
                    act.wait_ge(*K.at("max_done", i + 1))
                    if i >= 2:
                        act.wait_ge(*K.at("probs_done", i - 1))
                    for s in range(passes):
                        src = E[:, b, 1, 0:n] if u["bias"] is not None else K.ps[:, 2 * b + s, 0:n]
                        nc.scalar.activation(E[:, b, s, 0:n], src, ACT.Exp, bias=stat[:, b, s, 0:1],
                                             accum_out=stat[:, b, s, 1:2]).then_inc(*K.inc("exps_done"))
                if i >= 1:
                    u, b = units[i - 1], (i - 1) % 2
                    act.wait_ge(*K.at("transposed", i))
                    if i >= 3:
                        act.wait_ge(*K.at("values_done", i - 2))
                    n = P * len(u["v"])
                    nc.scalar.activation(AT[:, b, 0:len(u["v"]), :].rearrange("p k q -> p (k q)"), K.ps[:, 4 + b, 0:n],
                                         ACT.Copy).then_inc(*K.inc("probsT_done"))

        @block.vector
        def _(dve):
            for i in range(U + 2):
                if i < U:
                    u, b = units[i], i % 2
                    n = u["k"].shape[-1]
                    dve.wait_ge(*K.at("scores_done", i + 1))
                    if i >= 2:
                        dve.wait_ge(*K.at("exps_done", passes * (i - 1)))
                    if u["bias"] is not None:
                        if n > T:
                            nc.vector.tensor_copy(E[:, b, 1, T:n], K.ps[:, 2 * b, T:n])
                        K.step(dve, nc.vector.tensor_tensor(E[:, b, 1, 0:T], K.ps[:, 2 * b, 0:T], u["bias"], ALU.add), "biased")
                    for s in range(passes):
                        src = E[:, b, 1, 0:n] if u["bias"] is not None else K.ps[:, 2 * b + s, 0:n]
                        last = nc.vector.tensor_reduce(stat[:, b, s, 0:1], src, AX, ALU.max, negate=True)
                    last.then_inc(*K.inc("max_done"))
                if 1 <= i <= U:
                    u, b = units[i - 1], (i - 1) % 2
                    n = u["k"].shape[-1]
                    dve.wait_ge(*K.at("exps_done", passes * i))
                    if i >= 3:
                        dve.wait_ge(*K.at("transposed", i - 2))
                    K.step(dve, nc.vector.reciprocal(stat[:, b, 0:passes, 2:3], stat[:, b, 0:passes, 1:2]), "dve_step")
                    for s in range(passes):
                        if u["weight"][s] is not None:
                            K.step(dve, nc.vector.tensor_tensor(stat[:, b, s, 2:3], stat[:, b, s, 2:3], u["weight"][s], ALU.mult), "dve_step")
                    last = nc.vector.tensor_scalar(A[:, b, 0:n], E[:, b, 0, 0:n], stat[:, b, 0, 2:3], None, ALU.mult)
                    for s in range(1, passes):
                        K.step(dve, last, "dve_step")
                        last = nc.vector.scalar_tensor_tensor(out=A[:, b, 0:n], in0=E[:, b, s, 0:n], scalar=stat[:, b, s, 2:3],
                                                              in1=A[:, b, 0:n], op0=ALU.mult, op1=ALU.add)
                    last.then_inc(*K.inc("probs_done"))
                if i >= 2:
                    u, b = units[i - 2], (i - 2) % 2
                    dve.wait_ge(*K.at("values_done", i - 1))
                    nc.vector.tensor_copy(u["out"], K.ps[u["rows"][0]:u["rows"][1], 6 + b, 0:P]).then_inc(*K.inc("out_kept"))
    K.end_stage()


def gated_add(K, gate, fb, n_seg):
    nc = K.nc

    def evac(side, ps, dve):
        for s in range(n_seg):
            last = nc.vector.scalar_tensor_tensor(out=K.XT[:, fb, SEGS[s]], in0=ps[:, SEGS[s]], scalar=mod(K, gate, s, fb),
                                                  in1=K.XT[:, fb, SEGS[s]], op0=ALU.mult, op1=ALU.add)
        return last
    return evac


def out_proj_stage(K, gate, n_seg):
    n = n_seg * T
    jobs = [feature_job(K, fb // 4, fb % 4 * P, P, K.HT[:, :, 0:n], None, evac=gated_add(K, gate, fb, n_seg), only="dve")
            for fb in range(KD)]
    gemm_stage(K, 2, jobs, "out_projection")


def alpha_stage(K, n):
    nc = K.nc
    with K.block("alpha") as block:
        @block.scalar
        def _(act):
            for k in range(4):
                nc.scalar.mul(K.XT[:, k, 0:n], K.XT[:, k, 0:n], ALPHA)

        @block.vector
        def _(dve):
            for k in range(4, KD):
                nc.vector.tensor_scalar(K.XT[:, k, 0:n], K.XT[:, k, 0:n], ALPHA, None, ALU.mult)
    K.end_stage()


def layer_norm_stage(K, n, g, b):
    src = [K.XT[:, k, 0:n] for k in range(KD)]
    norm_stage(K, [dict(src=src, ones=K.ones, inv=1.0 / D, eps=K.eps["ln"],
                        out=[(s, s, slice(0, n), K.col(g, k), K.col(b, k)) for k, s in enumerate(src)])],
               K.arena, centre=True)


def load_consts_stage(K, names, where, extra=()):
    at, pairs = 0, []
    for name in names:
        w = CONSTS[name]
        pairs.append((where[:, at:at + w], K.dram["consts"][:, CONST_AT[name]:CONST_AT[name] + w]))
        K.const[name] = where[:, at:at + w]
        at += w
    pairs += list(extra)
    with K.block("constants") as block:
        @block.sync
        def _(sp):
            for dst, src in pairs:
                sp.dma_start(dst, src).then_inc(*K.inc("constants_landed", 16))
            sp.wait_ge(*K.at("constants_landed", 16 * len(pairs)))
    K.end_stage()


def rope_stage(K, blocks, swap, cos, sin, tmp):
    nc, B, n = K.nc, len(blocks), T
    p = blocks[0].shape[0]
    with K.block("rope") as block:
        @block.tensor
        def _(pe):
            for i, q in enumerate(blocks):
                if i >= NBANK:
                    pe.wait_ge(*K.at("swapped_times_sin", i - NBANK + 1))
                nc.tensor.matmul(K.ps[0:p, i % NBANK, 0:n], swap, q, start=True, stop=True).then_inc(*K.inc("swapped"))

        @block.gpsimd
        def _(pool):
            for i, q in enumerate(blocks):
                pool.wait_ge(*K.at("swapped", i + 1))
                nc.gpsimd.tensor_tensor(q, q, cos, ALU.mult).then_inc(*K.inc("times_cos"))

        @block.vector
        def _(dve):
            for i, q in enumerate(blocks):
                t = tmp[0:p, i % 2 * n:(i % 2 + 1) * n]
                dve.wait_ge(*K.at("swapped", i + 1))
                K.step(dve, nc.vector.tensor_tensor(t, K.ps[0:p, i % NBANK, 0:n], sin, ALU.mult), "swapped_times_sin")
                dve.wait_ge(*K.at("times_cos", i + 1))
                K.step(dve, nc.vector.tensor_tensor(q, q, t, ALU.add), "dve_step")
    K.end_stage()


def prologue(K):
    nc, d = K.nc, K.dram
    lam_in = K.arena[:, 0:2 * 256].rearrange("p (l a n) -> p l a n", l=2, a=4)
    lam_prod = K.arena[:, 512:768].rearrange("p (l a n) -> p (l a) n", l=2, a=2)
    lam_sum = K.small[:, 24:28]
    lam_exp = K.small[:, 28:32].rearrange("p (l a) -> p l a", l=2)
    K.neg_lam = [K.small[:, 32:33], K.small[:, 33:34]]
    K.eps = {n: K.small[:, 34 + i:35 + i] for i, n in enumerate(("ln", "rms", "gn", "kk", "zero"))}
    K.subln = [K.small[:, 40:41], K.small[:, 41:42]]
    K.q_gain, K.na_gain = K.small[:, 42:43], K.small[:, 43:44]
    K.zero_wait = K.small[:, 39:40]
    sig = K.arena[:, 1024:1024 + 32].rearrange("p (b v k) -> p b v k", b=2, v=2)
    lam_init = [0.8 - 0.6 * math.exp(-0.3 * l) for l in range(DEPTH)]
    with K.block("prologue") as block:
        @block.sync
        def _(sp):
            sp.dma_start(K.cols[:, :], d["cols"]).then_inc(*K.inc("constants_landed", 16))
            sp.dma_start(K.base_consts[:, :], d["consts"][:, 0:384]).then_inc(*K.inc("constants_landed", 16))
            sp.dma_start(K.arena[:, 0:512], d["diff_lambda"].partition_broadcast(P)).then_inc(*K.inc("constants_landed", 16))
            sp.dma_start(K.XT[:, :, X], d["x"].rearrange("(k p) t -> p k t", p=P)).then_inc(*K.inc("constants_landed", 16))
            sp.dma_start(K.XT[:, :, C], d["ctx"].rearrange("(k p) t -> p k t", p=P)).then_inc(*K.inc("constants_landed", 16))
            for _ in range(RING):
                K.load_next(sp)
            sp.wait_ge(*K.at("constants_landed", 5 * 16))

        @block.gpsimd
        def _(pool):
            nc.gpsimd.memset(K.sil[:, :, :, :], 0.0).then_inc(*K.inc("cleared"))
            for n, v in (("ln", 1e-5), ("rms", 1e-6), ("gn", 64e-5), ("kk", 1e-12), ("zero", 0.0)):
                nc.gpsimd.memset(K.eps[n], v)

        @block.scalar
        def _(act):
            act.wait_ge(*K.at("constants_landed", 5 * 16))
            act.wait_ge(*K.at("cleared", 1))
            for b in range(2):
                for v in range(2):
                    nc.scalar.activation(K.sil[:, b, :, v], K.col("c", 8 * (2 * b + v), 8), ACT.Silu)
            act.wait_ge(*K.at("lam_summed", 1))
            nc.scalar.activation(lam_exp, lam_sum.rearrange("p (l a) -> p l a", l=2), ACT.Exp).then_inc(*K.inc("lam_exps"))

        @block.vector
        def _(dve):
            dve.wait_ge(*K.at("constants_landed", 5 * 16))
            for l in range(DEPTH):
                for a in range(2):
                    last = nc.vector.tensor_tensor(lam_prod[:, 2 * l + a, :], lam_in[:, l, 2 * a, :], lam_in[:, l, 2 * a + 1, :], ALU.mult)
            K.step(dve, last, "dve_step")
            nc.vector.tensor_reduce(lam_sum, lam_prod, AX, ALU.add).then_inc(*K.inc("lam_summed"))
            for l in range(DEPTH):
                nc.vector.tensor_scalar(K.subln[l], K.col(f"subln{l}"), 1.0 - lam_init[l], None, ALU.mult)
            nc.vector.tensor_scalar(K.q_gain, K.col("q_g"), 96.0 ** -0.5, None, ALU.mult)
            nc.vector.tensor_scalar(K.na_gain, K.col("na_q"), 64.0 ** -0.5, None, ALU.mult)
            dve.wait_ge(*K.at("lam_exps", 1))
            for l in range(DEPTH):
                K.step(dve, nc.vector.tensor_tensor(K.neg_lam[l], lam_exp[:, l, 1:2], lam_exp[:, l, 0:1], ALU.subtract), "dve_step")
                nc.vector.tensor_scalar(K.neg_lam[l], K.neg_lam[l], -lam_init[l], None, ALU.add)
    K.end_stage()


def first_layer(K, l):
    nc, A, HT = K.nc, K.arena, K.HT
    n_seg = 1 if l == DEPTH - 1 else 2
    n = n_seg * T
    q = A[:, 0:2048].rearrange("p (h t) -> p h t", h=4)
    k = A[:, 2048:4096].rearrange("p (h t) -> p h t", h=4)
    v = A[:, 4096:6144].rearrange("p (t e) -> p t e", t=4)
    cv = A[:, 6144:9216].rearrange("p (b t) -> p b t", b=6)
    f = A[:, 9216:10240].rearrange("p (t m) -> p t m", t=4)
    q2 = A[:, 10240:14336].rearrange("p (s h t) -> p s h t", s=2, h=4)
    tmp = A[:, 14336:16384]
    table = A[:, 16512:18432]

    mod_stage(K, K.sil[:, 0], K.col(f"b_mod{l}", 0, 48), (1, 4))
    modulate_stage(K, 0, 1, 2)
    load_consts_stage(K, ["swap1", "cos1", "sin1", "cn", "sn", "cm", "sm"], table)

    jobs = [feature_job(K, 0, h * P, P, HT[:, :, 0:n], q[:, h, 0:n], scale=0.125) for h in range(4)]
    jobs += [feature_job(K, 1, h * P, P, HT, k[:, h, :]) for h in range(4)]
    jobs += [token_job(K, 2, lambda w, i: w[:, i, :], HT, t, v[:, t, :]) for t in range(4)]
    jobs += [feature_job(K, 3, b * P, P, HT[:, :, 0:n], cv[:, b, 0:n]) for b in range(4)]
    jobs += [feature_job(K, 4, b * P, P, HT[:, :, 0:n], cv[:, 4 + b, 0:n]) for b in range(2)]
    jobs += [token_job(K, 4, lambda w, i: w[:, i, 256:512], HT, t, f[:, t, :]) for t in range(2 * n_seg)]
    gemm_stage(K, 5, jobs, "in_projection")

    rope_stage(K, [b[:, h, X] for b in (q, k) for h in range(4)], K.const["swap1"], K.const["cos1"], K.const["sin1"], tmp)
    conv_fourier_stage(K, l, n_seg, cv, f, q, q2, tmp)

    units = [dict(q=[q2[:, s, h, c * P:(c + 1) * P] for s in range(2)], k=k[:, h, 0:TT] if c < 2 else k[:, h, C],
                  v=[v[:, t, h * P:(h + 1) * P] for t in (range(4) if c < 2 else range(2, 4))], bias=None, rows=(0, P),
                  out=HT[:, h, c * P:(c + 1) * P], weight=[None, K.neg_lam[l]])
             for h in range(4) for c in range(2 * n_seg)]
    attention_stage(K, units, A[:, 6144:10240], 2, "differential_attention")
    norm_stage(K, [dict(src=[HT[:, h, 0:n]], ones=K.ones, inv=1.0 / P, eps=K.eps["ln"],
                        out=[(HT[:, h, 0:n], HT[:, h, 0:n], slice(0, n), K.subln[l], None)]) for h in range(4)], A[:, 0:3072])
    alpha_stage(K, n)
    out_proj_stage(K, 2, n_seg)
    layer_norm_stage(K, n, f"ln1_g{l}", f"ln1_b{l}")
    modulate_stage(K, 3, 4, n_seg)

    hidden = A[:, 0:16384].rearrange("p (b t) -> p b t", b=32)
    jobs = [feature_job(K, fb // 4, fb % 4 * P, P, HT[:, :, 0:n], None, evac=squared_relu(K, hidden[:, fb, 0:n])) for fb in range(32)]
    gemm_stage(K, 8, jobs, "mlp_up")
    alpha_stage(K, n)
    jobs = []
    for fb in range(KD):
        pieces = [fb // 4 * 4 + r for r in range(4)]
        c0 = fb % 4 * P
        jobs.append(dict(pieces=pieces, rows=(0, P), n=n, only="dve", evac=gated_add(K, 5, fb, n_seg),
                         mm=lambda w, c0=c0: [(w[r][:, i, c0:c0 + P], hidden[:, 8 * r + i, 0:n]) for r in range(4) for i in range(KD)]))
    gemm_stage(K, 8, jobs, "mlp_down")
    layer_norm_stage(K, n, f"ln2_g{l}", f"ln2_b{l}")


def squared_relu(K, out):
    nc = K.nc

    def evac(side, ps, eng):
        if side == "act":
            K.step(eng, nc.scalar.activation(out, ps, ACT.Relu), "act_step")
            return nc.scalar.activation(out, out, ACT.Square)
        K.step(eng, nc.vector.tensor_scalar(out, ps, 0.0, None, ALU.max), "dve_step")
        return nc.vector.tensor_tensor(out, out, out, ALU.mult)
    return evac


def conv_fourier_stage(K, l, n_seg, cv, f, q, q2, tmp):
    nc, HT = K.nc, K.HT
    n = n_seg * T
    cn = K.const["cn"].rearrange("p (t k) -> p t k", t=2)
    sn = K.const["sn"].rearrange("p (t k) -> p t k", t=2)
    first = tmp.rearrange("p (b t) -> p b t", b=4)
    with K.block("conv_fourier") as block:
        @block.tensor
        def _(pe):
            for b in range(4):
                for s in range(n_seg):
                    for t in range(2):
                        last = nc.tensor.matmul(K.ps[:, b, SEGS[s]], f[:, 2 * s + t, b % 2 * P:(b % 2 + 1) * P],
                                                (cn, sn)[b // 2][:, t, :], start=t == 0, stop=t == 1)
                last.then_inc(*K.inc("tokens_transformed"))
            for b in range(2):
                pe.wait_ge(*K.at("transform_kept", 4))
                nc.tensor.matmul(K.ps[:, 4 + b, 0:n], K.const["cm"], first[:, b, 0:n], start=True, stop=False)
                nc.tensor.matmul(K.ps[:, 4 + b, 0:n], K.const["sm"], first[:, 2 + b, 0:n], start=False, stop=True)\
                    .then_inc(*K.inc("features_transformed"))

        @block.scalar
        def _(act):
            for b in range(4):
                act.wait_ge(*K.at("tokens_transformed", b + 1))
                nc.scalar.activation(first[:, b, 0:n], K.ps[:, b, 0:n], ACT.Copy).then_inc(*K.inc("transform_kept"))
            for b in range(2):
                act.wait_ge(*K.at("features_transformed", b + 1))
                nc.scalar.activation(HT[:, 6 + b, 0:n], K.ps[:, 4 + b, 0:n], ACT.Copy)

        @block.gpsimd
        def _(pool):
            nc.gpsimd.memset(q2[64:128, 0], 0.0)
            nc.gpsimd.memset(q2[0:64, 1], 0.0)
            for s in range(2):
                nc.gpsimd.tensor_copy(q2[64 * s:64 * s + 64, s, :, 0:n], q[64 * s:64 * s + 64, :, 0:n])

        @block.vector
        def _(dve):
            for b in range(2):
                w = [K.col(f"conv_w{l}", 2 * i + b) for i in range(3)]
                z, gate, gc, y = cv[:, b, 0:n], cv[:, 2 + b, 0:n], cv[:, 4 + b, 0:n], HT[:, 4 + b, 0:n]
                K.step(dve, nc.vector.tensor_tensor(z, z, gc, ALU.mult), "dve_step")
                K.step(dve, nc.vector.tensor_scalar(y, z, w[1], K.col(f"conv_b{l}", b), ALU.mult, ALU.add), "dve_step")
                zs, ys = (a.rearrange("p (s t) -> p s t", s=n_seg) for a in (z, y))
                for tap, dst, src in ((w[0], slice(1, T), slice(0, T - 1)), (w[2], slice(0, T - 1), slice(1, T))):
                    K.step(dve, nc.vector.scalar_tensor_tensor(out=ys[:, :, dst], in0=zs[:, :, src], scalar=tap, in1=ys[:, :, dst],
                                                               op0=ALU.mult, op1=ALU.add), "dve_step")
                K.step(dve, nc.vector.tensor_tensor(y, y, gate, ALU.mult), "dve_step")
    K.end_stage()


def plan_even(K):
    K.plan("ada_w", 0)
    for name in ("ev_w_in", "w_uq", "w_ukv", "ev_w_out", "router"):
        K.plan(name, 0)
    plan_experts(K, 2)


def scaled_norm_stage(K, l, which, n_seg):
    nc = K.nc
    gain = K.col(f"norm{1 if which == 0 else 2}_g{l}", 0, KD)
    with K.block("gain") as block:
        @block.vector
        def _(dve):
            for s in range(n_seg):
                nc.vector.tensor_tensor(K.gain[:, s, :], K.modcol[:, s, 8 * (which + 1):8 * (which + 2)], gain, ALU.mult)
    K.end_stage()
    n = n_seg * T
    norm_stage(K, [dict(src=[K.XT[:, k, 0:n] for k in range(KD)], ones=K.ones, inv=1.0 / D, eps=K.eps["rms"],
                        out=[(K.HT[:, k, SEGS[s]], K.XT[:, k, SEGS[s]], SEGS[s], K.gain[:, s, k:k + 1], mod(K, which, s, k))
                             for k in range(KD) for s in range(n_seg)])], K.arena)


def even_layer(K):
    nc, A, HT = K.nc, K.arena, K.HT
    q = A[:, 0:4096].rearrange("p (h t) -> p h t", h=8)
    k = A[:, 4096:8192].rearrange("p (h t) -> p h t", h=8)
    v = A[:, 8192:10240].rearrange("p (t e) -> p t e", t=4)
    pad = A[:, 10240:12528].rearrange("p (b s t) -> p b s t", b=4, s=2)
    cq = A[:, 12528:14064].rearrange("p (b t) -> p b t", b=3)
    ckv = A[:, 14064:15088].rearrange("p (b t) -> p b t", b=2)
    kr = A[64:96, 15088:15600]
    table, tmp = A[:, 15600:16240], A[:, 16240:16752]
    a, sg = (A[:, i:i + 2048].rearrange("p (b t) -> p b t", b=4) for i in (0, 2048))

    mod_stage(K, K.sil[:, 1], K.col("ada_b0", 0, 48), (1, 4))
    load_consts_stage(K, ["swap2", "cos2", "sin2"], table, [(K.XT[:, :, C], K.dram["ctx_2"].rearrange("(k p) t -> p k t", p=P))])
    scaled_norm_stage(K, 0, 0, 2)

    jobs = [feature_job(K, 0, b * P, P, HT, cq[:, b, :]) for b in range(3)]
    jobs += [feature_job(K, 1, b * P, P, HT, ckv[:, b, :]) for b in range(2)]
    jobs += [feature_job(K, 1, 256, 32, HT, kr, p0=64)]
    jobs += [feature_job(K, 2, b * P, P, HT, a[:, b, :]) for b in range(4)]
    jobs += [feature_job(K, 3, b * P, P, HT, None, only="act",
                         evac=lambda side, ps, eng, b=b: nc.scalar.activation(sg[:, b, :], ps, ACT.Sigmoid)) for b in range(4)]
    gemm_stage(K, 4, jobs, "even_in_projection")
    gate_stage(K, a, sg, pad)
    norm_stage(K, [dict(src=[c[:, b, :] for b in range(m)], ones=K.ones, inv=1.0 / (m * P), eps=K.eps["rms"],
                        out=[(c[:, b, :], c[:, b, :], slice(0, TT), K.col(gain, b), None) for b in range(m)])
                   for c, m, gain in ((cq, 3, "q_norm"), (ckv, 2, "kv_norm"))], A[:, 0:3072])

    jobs = [feature_job(K, 0, h * 96, 96, cq, q[0:96, h, :]) for h in range(8)]
    jobs += [feature_job(K, 1, h * P, 64, ckv, k[0:64, h, :]) for h in range(8)]
    jobs += [token_job(K, 1, lambda w, i: w[:, i, :].rearrange("p (h e) -> p h e", e=P)[:, :, 64:P], ckv, t, v[:, t, :]) for t in range(4)]
    gemm_stage(K, 2, jobs, "mla_up_projection")
    with K.block("shared_rotary_key") as block:
        @block.scalar
        def _(act):
            for h in range(0, 8, 2):
                nc.scalar.activation(k[64:96, h, :], kr, ACT.Copy)

        @block.vector
        def _(dve):
            for h in range(1, 8, 2):
                nc.vector.tensor_copy(k[64:96, h, :], kr)
    K.end_stage()
    norm_stage(K, [dict(src=[b[0:96, h, :]], ones=K.ones[0:96, 0:96], inv=1.0 / 96, eps=K.eps["rms"],
                        out=[(b[0:96, h, :], b[0:96, h, :], slice(0, TT), gain[0:96], None)])
                   for b, gain in ((q, K.q_gain), (k, K.col("k_g"))) for h in range(8)], A[:, 12528:15600])
    rope_stage(K, [b[0:96, h, X] for b in (q, k) for h in range(8)], K.const["swap2"][0:96, 0:96],
               K.const["cos2"][0:96], K.const["sin2"][0:96], tmp)
    depthwise_stage(K, pad)
    conv = [HT[:, 4 + b, :] for b in range(4)]
    norm_stage(K, [dict(src=conv, ones=K.ones, inv=1.0 / 512, eps=K.eps["rms"],
                        out=[(c, c, slice(0, TT), K.col("cln_g", b), K.col("cln_b", b)) for b, c in enumerate(conv)])],
               A[:, 12528:15600], centre=True)
    with K.block("conv_silu") as block:
        @block.scalar
        def _(act):
            nc.scalar.activation(HT[:, 4:8, :], HT[:, 4:8, :], ACT.Silu)
    K.end_stage()

    units = [dict(q=[q[0:96, h, c * P:(c + 1) * P]], k=k[0:96, h, 0:TT] if c < 2 else k[0:96, h, C],
                  v=[v[:, t, h * 64:(h + 1) * 64] for t in (range(4) if c < 2 else range(2, 4))], bias=None,
                  rows=(h % 2 * 64, h % 2 * 64 + 64), out=HT[h % 2 * 64:h % 2 * 64 + 64, h // 2, c * P:(c + 1) * P], weight=[None])
             for h in range(8) for c in range(4)]
    attention_stage(K, units, A[:, 14336:18432], 1, "mla_attention")
    out_proj_stage(K, 2, 2)
    experts(K, 0, 2)


def gate_stage(K, a, sg, pad):
    nc = K.nc
    with K.block("gate") as block:
        @block.gpsimd
        def _(pool):
            nc.gpsimd.memset(pad[:, :, :, 0:15], 0.0)
            nc.gpsimd.memset(pad[:, :, :, 15 + T:30 + T], 0.0)

        @block.vector
        def _(dve):
            for b in range(4):
                nc.vector.tensor_tensor(pad[:, b, :, 15:15 + T], a[:, b, :].rearrange("p (s t) -> p s t", s=2),
                                        sg[:, b, :].rearrange("p (s t) -> p s t", s=2), ALU.mult)
    K.end_stage()


def depthwise_stage(K, pad):
    nc, taps = K.nc, 31
    y = [K.HT[:, 4 + b, :].rearrange("p (s t) -> p s t", s=2) for b in range(4)]
    with K.block("depthwise_conv") as block:
        @block.vector
        def _(dve):
            for j in range(taps):
                for b in range(4):
                    src, w = pad[:, b, :, j:j + T], K.col("dw_w", 4 * j + b)
                    if j == 0:
                        ins = nc.vector.tensor_scalar(y[b], src, w, K.col("dw_b", b), ALU.mult, ALU.add)
                    else:
                        dve.wait_ge(*K.at("tap_added", 4 * (j - 1) + b + 1))
                        ins = nc.vector.scalar_tensor_tensor(out=y[b], in0=src, scalar=w, in1=y[b], op0=ALU.mult, op1=ALU.add)
                    ins.then_inc(*K.inc("tap_added"))
    K.end_stage()


def expert_pieces(group):
    return [(m, e, h) for e in range(group) for m in ("moe_w1", "moe_w3") for h in range(2)] + \
           [("moe_w2", e, h) for h in range(2) for e in range(group)]


def plan_experts(K, group):
    l = 0 if group == 2 else 1
    for g in range(NE // group):
        for m, e, h in expert_pieces(group):
            K.stream.append((K.dram[m][l, g * group + e, h].rearrange("p n -> (p n)"), KD, 512))


def experts(K, l, n_seg):
    nc, A, HT = K.nc, K.arena, K.HT
    n, nt, M = n_seg * T, 2 * n_seg, CAP * n_seg
    group = P // M
    NG = NE // group
    xs_all = A[:, 0:NE * KD * M].rearrange("p (e k s) -> p e k s", e=NE, k=KD)
    ys = A[:, 0:NG * D].rearrange("p (g d) -> p g d", g=NG)
    h_tok = A[:, 8192:8192 + nt * D].rearrange("p (t d) -> p t d", t=nt)
    pick = A[:, 12288:12288 + nt * NE * M].rearrange("p (t e s) -> p t e s", t=nt, e=NE)
    pt = HT[:, :, :].rearrange("p k t -> p (k t)")[:, 0:NG * n].rearrange("p (g t) -> p g t", g=NG)

    scaled_norm_stage(K, l, 3, n_seg)
    B = A[:, 16384:18432]
    tri, iota = B[:, 0:128], B[:, 128:192]
    logit = B[:, 192:256].rearrange("p (t e) -> p t e", t=4)
    aff = B[:, 256:512].rearrange("p (t s) -> p t s", t=2)
    affT, left = B[0:32, 512:768], B[0:32, 768:1024]
    mask = B[:, 1024:1280]
    maskT = B[:, 1280:1344].rearrange("p (t s) -> p t s", t=2)
    place = B[:, 1344:1408].rearrange("p (t s) -> p t s", t=2)
    top = B[0:32, 1408:1416]
    peak = B[:, 1416:1420]
    load_consts_stage(K, ["tri", "iota"], B[:, 0:192])
    gemm_stage(K, 1, [token_job(K, 0, lambda w, i: w[:, i, :], HT, t, logit[:, t, :]) for t in range(nt)], "router")
    R = 16 * n_seg
    tok = lambda buf, t: buf[:, t % 2, 16 * (t // 2):16 * (t // 2) + 16]

    with K.block("routing") as block:
        @block.gpsimd
        def _(pool):
            nc.gpsimd.memset(aff, 0.0).then_inc(*K.inc("cleared"))
            nc.gpsimd.memset(mask, 0.0).then_inc(*K.inc("cleared"))
            nc.gpsimd.memset(pick, 0.0).then_inc(*K.inc("cleared"))

        @block.tensor
        def _(pe):
            for t in range(nt):
                for half in range(2):
                    for i in range(4):
                        last = nc.tensor.transpose(K.ps[:, (2 * t + half) % 4, i * P:(i + 1) * P],
                                                   HT[:, 4 * half + i, t * P:(t + 1) * P], K.ident)
                    last.then_inc(*K.inc("h_transposed"))
                    if 2 * t + half + 1 < 2 * nt and 2 * t + half >= 3:
                        pe.wait_ge(*K.at("h_kept", 2 * t + half - 2))
            pe.wait_ge(*K.at("affinities", 1))
            for t in range(2):
                last = nc.tensor.transpose(K.ps[:, 4, t * P:(t + 1) * P], aff[:, t, :], K.ident)
            last.then_inc(*K.inc("affinities_turned"))
            pe.wait_ge(*K.at("masked", 1))
            for t in range(2):
                last = nc.tensor.transpose(K.ps[:, 5, t * P:(t + 1) * P], mask[:, t * P:(t + 1) * P], K.ident)
            last.then_inc(*K.inc("mask_turned"))
            pe.wait_ge(*K.at("mask_kept", 1))
            nc.tensor.matmul(K.ps[:, 6, 0:32], tri, maskT[:, 0, :], start=True, stop=True)
            nc.tensor.matmul(K.ps[:, 7, 0:32], K.ones, maskT[:, 0, :], start=True, stop=False)
            nc.tensor.matmul(K.ps[:, 7, 0:32], tri, maskT[:, 1, :], start=False, stop=True).then_inc(*K.inc("counted"))

        @block.scalar
        def _(act):
            act.wait_ge(*K.at("shifted", 1))
            nc.scalar.activation(logit[:, 0:nt, :], logit[:, 0:nt, :], ACT.Exp).then_inc(*K.inc("logit_exps"))
            for i in range(2 * nt):
                act.wait_ge(*K.at("h_transposed", i + 1))
                nc.scalar.activation(h_tok[:, i // 2, i % 2 * 512:(i % 2 + 1) * 512], K.ps[:, i % 4, :], ACT.Copy)\
                    .then_inc(*K.inc("h_kept"))

        @block.vector
        def _(dve):
            lg = logit[:, 0:nt, :]
            pk = peak[:, 0:nt]
            bc = pk.unsqueeze(2).broadcast_to([P, nt, NE])
            K.step(dve, nc.vector.tensor_reduce(pk, lg, AX, ALU.max), "dve_step")
            nc.vector.tensor_tensor(lg, lg, bc, ALU.subtract).then_inc(*K.inc("shifted"))
            dve.wait_ge(*K.at("logit_exps", 1))
            K.step(dve, nc.vector.tensor_reduce(pk, lg, AX, ALU.add), "dve_step")
            K.step(dve, nc.vector.reciprocal(pk, pk), "dve_step")
            dve.wait_ge(*K.at("cleared", 3))
            for t in range(nt):
                last = nc.vector.tensor_scalar(tok(aff, t), logit[:, t, :], pk[:, t:t + 1], None, ALU.mult)
            last.then_inc(*K.inc("affinities"))
            dve.wait_ge(*K.at("affinities_turned", 1))
            K.step(dve, nc.vector.tensor_copy(left[0:R], K.ps[0:R, 4, 0:T]), "dve_step")
            for _ in range(CAP // 8):
                K.step(dve, nc.vector.max(top[0:R], left[0:R]), "dve_step")
                K.step(dve, nc.vector.match_replace(left[0:R], top[0:R], left[0:R], -1.0), "dve_step")
            nc.vector.tensor_scalar(mask[0:R], left[0:R], 0.0, None, ALU.is_lt).then_inc(*K.inc("masked"))
            dve.wait_ge(*K.at("mask_turned", 1))
            for t in range(2):
                last = nc.vector.tensor_copy(maskT[:, t, :], K.ps[:, 5, t * P:t * P + 32])
            last.then_inc(*K.inc("mask_kept"))
            dve.wait_ge(*K.at("counted", 1))
            dve.wait_ge(*K.at("mask_kept", 1))
            for t in range(2):
                last = nc.vector.tensor_tensor(place[:, t, :], K.ps[:, 6 + t, 0:32], maskT[:, t, :], ALU.mult)
            K.step(dve, last, "dve_step")
            for t in range(nt):
                at = CAP * (t // 2)
                nc.vector.tensor_tensor(pick[:, t, :, at:at + CAP], tok(place, t).unsqueeze(2).broadcast_to([P, NE, CAP]),
                                        iota[:, 0:CAP].unsqueeze(1).broadcast_to([P, NE, CAP]), ALU.is_equal)
    K.end_stage()

    with K.block("gather") as block:
        @block.tensor
        def _(pe):
            for i in range(n_seg * KD):
                s, k = divmod(i, KD)
                if i >= 4:
                    pe.wait_ge(*K.at("gathered_kept", i - 3))
                for t in range(2):
                    last = nc.tensor.matmul(K.ps[:, i % 4, :], h_tok[:, 2 * s + t, k * P:(k + 1) * P],
                                            pick[:, 2 * s + t, :, CAP * s:CAP * s + CAP], start=t == 0, stop=t == 1)
                last.then_inc(*K.inc("gathered"))
            for g in range(NG):
                pe.wait_ge(*K.at("weighted", 1))
                if g >= 4:
                    pe.wait_ge(*K.at("scatter_kept", g - 3))
                for t in range(nt):
                    last = nc.tensor.transpose(K.ps[:, 4 + g % 4, t * P:(t + 1) * P],
                                               pick[:, t, g * group:(g + 1) * group, :].rearrange("p e s -> p (e s)"), K.ident)
                last.then_inc(*K.inc("scatter_turned"))

        @block.scalar
        def _(act):
            for i in range(n_seg * KD):
                s, k = divmod(i, KD)
                act.wait_ge(*K.at("gathered", i + 1))
                nc.scalar.activation(xs_all[:, :, k, CAP * s:CAP * s + CAP], K.ps[:, i % 4, :].rearrange("p (e s) -> p e s", e=NE),
                                     ACT.Copy).then_inc(*K.inc("gathered_kept"))

        @block.vector
        def _(dve):
            dve.wait_ge(*K.at("gathered", n_seg * KD))
            for t in range(nt):
                at = CAP * (t // 2)
                w = pick[:, t, :, at:at + CAP]
                last = nc.vector.tensor_tensor(w, w, tok(aff, t).unsqueeze(2).broadcast_to([P, NE, CAP]), ALU.mult)
            last.then_inc(*K.inc("weighted"))
            for g in range(NG):
                dve.wait_ge(*K.at("scatter_turned", g + 1))
                nc.vector.tensor_copy(pt[:, g, :], K.ps[:, 4 + g % 4, 0:n]).then_inc(*K.inc("scatter_kept"))
    K.end_stage()
    expert_loop_stage(K, l, group, M, xs_all, ys)

    with K.block("scatter") as block:
        @block.tensor
        def _(pe):
            for k in range(KD):
                for g in range(NG):
                    last = nc.tensor.matmul(K.ps[:, k, 0:n], ys[:, g, k * P:(k + 1) * P], pt[:, g, :], start=g == 0, stop=g == NG - 1)
                last.then_inc(*K.inc("scattered"))

        @block.vector
        def _(dve):
            for k in range(KD):
                dve.wait_ge(*K.at("scattered", k + 1))
                gated_add(K, 5, k, n_seg)("dve", K.ps[:, k, 0:n], dve)
    K.end_stage()


def expert_loop_stage(K, l, group, M, xs_all, ys):
    nc, A, first = K.nc, K.arena, K.cursor
    NG, J = NE // group, group
    FW = D // J
    NC = FW // P
    order = expert_pieces(group)
    npiece = len(order)
    where = {p: i for i, p in enumerate(order)}
    xs = A[:, 8192:9216].rearrange("p (e k s) -> p e k s", e=group, k=KD)
    hid = A[:, 9216:10240].rearrange("p (b f) -> p b f", b=2)
    hidT = A[:, 10240:10240 + group * NC * P].rearrange("p (e c r) -> p e c r", e=group, c=NC)

    def slot(q):
        return K.ring[:, (first + q) % RING, :].rearrange("p (k w) -> p k w", k=KD)

    def landed(g, q):
        sem, n = K.landed(first + q)
        return sem, g * (16 * npiece // RING) + n

    def released(q):
        m, e, h = order[q]
        if m == "moe_w2":
            return "down_done", h + 1
        return "up_done", 2 * e + (1 if m == "moe_w1" else 2)

    def load(sp, g, q):
        m, e, h = order[q]
        sem = K.sem(f"slot{(first + q) % RING}_landed")
        sp.dma_start(K.ring[:, (first + q) % RING, :], K.dram[m][l, g * group + e, h]).then_inc(sem, 16)

    per = dict(up_done=2 * group, silu_done=group, hidden_done=group, hiddenT_ready=group, hiddenT_kept=group,
               down_done=2, ys_kept=2, xs_ready=group)

    def loop(eng, body):
        body(0, True)
        K.times = NG - 1
        with eng.Fori(1, NG) as g:
            body(g, False)
        K.times = 1

    def at(name, g, n):
        return K.at(name, g * per[name] + n)

    with K.block("experts") as block:
        @block.sync
        def _(sp):
            def feed(g, last):
                for q in range(npiece):
                    name, n = released(q)
                    sp.wait_ge(*at(name, g, n))
                    if q + RING < npiece:
                        load(sp, g, q + RING)
                    elif last:
                        K.load_next(sp)
                    else:
                        load(sp, g + 1, q + RING - npiece)
            with sp.Fori(0, NG - 1) as g:
                feed(g, False)
            K.issued += NG * npiece - RING
            feed(NG - 1, True)

        @block.gpsimd
        def _(pool):
            for e in range(group):
                nc.gpsimd.tensor_copy(xs[:, e], xs_all[:, e]).then_inc(*K.inc("xs_ready"))
            K.times = NG - 1
            with pool.Fori(0, NG - 1) as g:
                for e in range(group):
                    pool.wait_ge(*at("up_done", g, 2 * e + 2))
                    nc.gpsimd.tensor_copy(xs[:, e], xs_all[:, g * group + (group + e)]).then_inc(*K.inc("xs_ready"))
            K.times = 1

        @block.tensor
        def _(pe):
            def body(g, peeled):
                def turn(e):
                    pe.wait_ge(*at("hidden_done", g, e + 1))
                    if not (peeled and e < 2):
                        pe.wait_ge(*at("hiddenT_kept", g, e - 1))
                    for c in range(NC):
                        last = nc.tensor.transpose(K.ps[:, 4 + e % 2, c * P:(c + 1) * P], hid[:, e % 2, c * P:(c + 1) * P], K.ident)
                    last.then_inc(*K.inc("hiddenT_ready"))
                for e in range(group):
                    pe.wait_ge(*at("xs_ready", g, e + 1))
                    if not (peeled and e < 2):
                        pe.wait_ge(*at("hidden_done", g, e - 1))
                    for i, m in enumerate(("moe_w1", "moe_w3")):
                        for h in range(2):
                            pe.wait_ge(*landed(g, where[m, e, h]))
                        w = [slot(where[m, e, h]) for h in range(2)]
                        for k in range(KD):
                            for j in range(J):
                                c0 = j * FW % 512
                                last = nc.tensor.matmul(K.ps[M * j:M * j + M, 2 * (e % 2) + i, 0:FW], xs[:, e, k, :],
                                                        w[j * FW // 512][:, k, c0:c0 + FW], start=k == 0, stop=k == KD - 1)
                        last.then_inc(*K.inc("up_done"))
                    if e:
                        turn(e - 1)
                turn(group - 1)
                pe.wait_ge(*at("hiddenT_kept", g, group))
                for h in range(2):
                    if not peeled:
                        pe.wait_ge(*at("ys_kept", g, h - 1))
                    for e in range(group):
                        pe.wait_ge(*landed(g, where["moe_w2", e, h]))
                    for f in range(KD):
                        j, c = divmod(f, NC)
                        for e in range(group):
                            last = nc.tensor.matmul(K.ps[M * e:M * e + M, 6 + h, :], hidT[:, e, c, M * j:M * j + M],
                                                    slot(where["moe_w2", e, h])[:, f, :], start=f == 0, stop=f == KD - 1)
                    last.then_inc(*K.inc("down_done"))
            loop(pe, body)

        @block.scalar
        def _(act):
            def body(g, peeled):
                def keep(e):
                    act.wait_ge(*at("hiddenT_ready", g, e + 1))
                    if not peeled:
                        act.wait_ge(*at("down_done", g, 0))
                    nc.scalar.activation(hidT[:, e].rearrange("p c r -> p (c r)"), K.ps[:, 4 + e % 2, 0:NC * P], ACT.Copy)\
                        .then_inc(*K.inc("hiddenT_kept"))
                for e in range(group):
                    act.wait_ge(*at("up_done", g, 2 * e + 1))
                    if not (peeled and e < 2):
                        act.wait_ge(*at("hiddenT_ready", g, e - 1))
                    nc.scalar.activation(hid[:, e % 2, 0:FW], K.ps[:, 2 * (e % 2), 0:FW], ACT.Silu).then_inc(*K.inc("silu_done"))
                    if e:
                        keep(e - 1)
                keep(group - 1)
            loop(act, body)

        @block.vector
        def _(dve):
            def body(g, peeled):
                for e in range(group):
                    dve.wait_ge(*at("silu_done", g, e + 1))
                    dve.wait_ge(*at("up_done", g, 2 * e + 2))
                    nc.vector.tensor_tensor(hid[:, e % 2, 0:FW], hid[:, e % 2, 0:FW], K.ps[:, 2 * (e % 2) + 1, 0:FW], ALU.mult)\
                        .then_inc(*K.inc("hidden_done"))
                if not peeled:
                    dve.wait_ge(*at("xs_ready", g, group))
                else:
                    dve.wait_ge(*at("xs_ready", 0, group))
                for h in range(2):
                    dve.wait_ge(*at("down_done", g, h + 1))
                    nc.vector.tensor_copy(ys[:, g, h * 512:(h + 1) * 512], K.ps[:, 6 + h, :]).then_inc(*K.inc("ys_kept"))
            loop(dve, body)
    K.cursor += NG * npiece
    K.end_stage()


def plan_odd(K):
    K.plan("ada_w", 1)
    K.plan("od_w_in", 0)
    K.plan("od_w_out", 0)
    K.plan("router", 1)
    plan_experts(K, 4)


def odd_layer(K):
    nc, A, HT, XT = K.nc, K.arena, K.HT, K.XT
    mod_stage(K, K.sil[:, 1], K.col("ada_b1", 0, 48), (1, 4))
    scaled_norm_stage(K, 1, 0, 2)

    u = A[:, 0:7680].rearrange("p (b t) -> p b t", b=15)
    q = A[:, 7680:8704].rearrange("p (b t) -> p b t", b=4)
    k = A[:, 8704:10752].rearrange("p (b t) -> p b t", b=4)
    v = A[:, 10752:12800].rearrange("p (t e) -> p t e", t=4)
    q2 = A[:, 12800:14848].rearrange("p (s b t) -> p s b t", s=2, b=4)
    jobs = [feature_job(K, 0, b * P, P, HT[:, :, X], q[:, b, :]) for b in range(4)]
    jobs += [feature_job(K, 1, b * P, P, HT, k[:, b, :]) for b in range(4)]
    jobs += [token_job(K, 2, lambda w, i: w[:, i, :], HT, t, v[:, t, :]) for t in range(4)]
    jobs += [feature_job(K, 3 + b // 4, b % 4 * P, P, HT, u[:, b, :]) for b in range(15)]
    gemm_stage(K, 7, jobs, "odd_in_projection", feed=1)
    bias = HT[:, :, :].rearrange("p k t -> p (k t)").rearrange("p (c h n) -> p c h n", c=2, h=8)
    window, flip = A[:, 14848:15360].rearrange("p (c n) -> p c n", c=2), A[:, 15360:15488]
    store_u_load_bias_stage(K, u, bias, A[:, 14848:15360], flip)
    norm_stage(K, [dict(src=[b[:, i, :]], ones=K.pair, inv=1.0 / 64, eps=K.eps["rms"],
                        out=[(b[:, i, :], b[:, i, :], slice(0, b.shape[-1]), gain, None)])
                   for b, gain in ((q, K.na_gain), (k, K.col("na_k"))) for i in range(4)], A[:, 0:3072])
    with K.block("masked_bias") as block:
        @block.gpsimd
        def _(pool):
            nc.gpsimd.memset(q2[64:128, 0], 0.0)
            nc.gpsimd.memset(q2[0:64, 1], 0.0)
            for s in range(2):
                nc.gpsimd.tensor_copy(q2[64 * s:64 * s + 64, s], q[64 * s:64 * s + 64])

        @block.tensor
        def _(pe):
            for i in range(8):
                nc.tensor.matmul(K.ps[:, i, :], flip, bias[:, i // 4, i % 4 * 2:i % 4 * 2 + 2, :].rearrange("p h n -> p (h n)"),
                                 start=True, stop=True).then_inc(*K.inc("flipped"))

        @block.vector
        def _(dve):
            for i in range(8):
                dve.wait_ge(*K.at("flipped", i + 1))
                nc.vector.tensor_tensor(bias[:, i // 4, i % 4 * 2:i % 4 * 2 + 2, :], K.ps[:, i, :].rearrange("p (h n) -> p h n", h=2),
                                        window[:, i // 4, :].unsqueeze(1).broadcast_to([P, 2, T]), ALU.add)
    K.end_stage()
    units = [dict(q=[q2[:, h % 2, h // 2, c * P:(c + 1) * P]], k=k[:, h // 2, :], v=[v[:, t, h * 64:(h + 1) * 64] for t in range(4)],
                  bias=bias[:, c, h, :], rows=(h % 2 * 64, h % 2 * 64 + 64),
                  out=XT[h % 2 * 64:h % 2 * 64 + 64, h // 2, T + c * P:T + (c + 1) * P], weight=[None])
             for h in range(8) for c in range(2)]
    attention_stage(K, units, A[:, 0:4096], 1, "neighbourhood_attention")

    y = rwkv(K)
    with K.block("mixed") as block:
        @block.scalar
        def _(act):
            nc.scalar.activation(HT[:, 4:8, X], XT[:, 0:4, C], ACT.Copy)

        @block.vector
        def _(dve):
            nc.vector.tensor_tensor(HT[:, 0:4, X], y, XT[:, 4:8, C], ALU.mult)
    K.end_stage()
    out_proj_stage(K, 2, 1)
    experts(K, 1, 1)


def store_u_load_bias_stage(K, u, bias, window, flip):
    rpb = K.dram["na_rpb"]
    with K.block("bias") as block:
        @block.sync
        def _(sp):
            for s in range(2):
                sp.dma_start(K.u_dram[s].rearrange("p (b t) -> p b t", b=15), u[:, :, SEGS[s]]).then_inc(*K.inc("u_stored", 16))
            for r in range(4):
                for h in range(8):
                    src = bass.AP(rpb.tensor, h * 15 * 31 + (7 - r) * 31 + 15 - 63, [[1, 64], [31, 4], [1, 64]])
                    dst = bias[r % 2 * 64:r % 2 * 64 + 64, r // 2, h, :].rearrange("p (i j) -> p i j", i=4)
                    sp.dma_start(dst, src).then_inc(*K.inc("constants_landed", 16))
            for name, dst in (("window", window), ("flip", flip)):
                at = CONST_AT[name]
                sp.dma_start(dst, K.dram["consts"][:, at:at + CONSTS[name]]).then_inc(*K.inc("constants_landed", 16))
            sp.wait_ge(*K.at("u_stored", 32))
            sp.wait_ge(*K.at("constants_landed", 34 * 16))
    K.end_stage()


def rwkv(K):
    nc, A = K.nc, K.arena
    ring = K.ring[:, :, :].rearrange("p s n -> p (s n)")
    hf = K.HT[:, :, :].rearrange("p k t -> p (k t)")
    m = Recurrence()
    small = A[:, 14336:18432]
    four = lambda a, lo: a[:, lo:lo + 1024].rearrange("p (b t) -> p b t", b=4)
    m.r, m.k, m.v, m.kk = (four(ring, 18432 + i) for i in (0, 1024, 2048, 3072))
    m.rkv = ring[:, 18432:21504]
    m.lora = ring[:, 22528:24064].rearrange("p (w c) -> p w c", w=3)
    m.lw, m.la, m.lg = (small[:, T * i:T * i + T] for i in range(3))
    m.y = four(small, 768)
    m.state = small[:, 1792:2304].rearrange("p (d b v) -> p d b v", d=2, b=4)
    m.rhs = small[:, 2304:2816].rearrange("p (d b v) -> p d b v", d=2, b=4)
    m.g_end = small[:, 3840:3872].rearrange("p (d i) -> p d i", d=2)
    m.gate = K.XT[:, 4:8, C]
    for d, (buf, bd) in enumerate(((ring, ring[:, 14336:18432]), (A, hf))):
        w = Recurrence()
        w.ar = buf[:, 0:2048].rearrange("p (i w t) -> p i w t", i=16, w=2)
        w.bk = buf[:, 2048:4096].rearrange("p (i w t) -> p i w t", i=16, w=2)
        w.uv = buf[:, 2048:4096].rearrange("p (i h v) -> p i h v", i=16, h=2)
        w.n = buf[:, 4096:8192].rearrange("p (w i c) -> p w i c", w=2, i=16)
        w.w = buf[:, 8192:12288].rearrange("p (i h c) -> p i h c", i=16, h=2)
        w.tok = buf[:, 12288:14336].rearrange("p (i c) -> p i c", i=16)
        w.bd = bd.rearrange("p (w i c) -> p w i c", w=2, i=16)
        w.x = w.bd
        w.decay, w.rate, w.p0, w.p1, w.e2, w.keff = (four(buf, 4096 + 1024 * i) for i in range(6))
        m.of.append(w)
    m.u = A[:, 8192:12032].rearrange("p (b t) -> p b t", b=15)
    work = A[:, 4096:7168]
    load_consts_stage(K, ["causal", "level"], small[:, 2816:3840], [(m.lora.rearrange("p w c -> p (w c)"),
                      K.dram["lora"][0].rearrange("(p n) -> p n", p=P))])
    m.causal = K.const["causal"].rearrange("p (d w t) -> p d w t", d=2, w=2)
    m.level = K.const["level"].rearrange("p (d l t) -> p d l t", d=2, l=6)
    for s in (1, 0):
        rwkv_inputs(K, m, s, work)
        rwkv_rates(K, m, s)
        rwkv_scale(K, m, s)
        rwkv_products(K, m)
        rwkv_inverse(K, m)
        rwkv_chunks(K, m, s)
    with K.block("refill") as block:
        @block.sync
        def _(sp):
            for _ in range(RING):
                K.load_next(sp)
    K.end_stage()
    norm_stage(K, [dict(src=[m.y[:, b, :]], ones=K.pair, inv=1.0 / 64, eps=K.eps["gn"],
                        out=[(m.y[:, b, :], m.y[:, b, :], slice(0, T), K.col("gn_g", b), K.col("gn_b", b))]) for b in range(4)],
               work, centre=True)
    return m.y


class Recurrence:

    def __init__(self):
        self.of = []


def rwkv_inputs(K, m, s, work):
    nc = K.nc
    dst = [b[:, i, :] for b in (m.r, m.k, m.v) for i in range(4)] + [m.lw, m.la, m.lg]
    with K.block("token_shift") as block:
        @block.sync
        def _(sp):
            sp.dma_start(m.u, K.u_dram[s].rearrange("p (b t) -> p b t", b=15)).then_inc(*K.inc("u_loaded", 16))
            sp.wait_ge(*K.at("u_loaded", 16))

        @block.gpsimd
        def _(pool):
            if s == 1:
                nc.gpsimd.memset(m.state, 0.0)

        @block.vector
        def _(dve):
            tap = lambda j, b: K.col("shift_w", 15 * j + b)
            for i, (j, to, of) in enumerate(((0, slice(1, T), slice(0, T - 1)), (2, slice(0, T - 1), slice(1, T)))):
                for b in range(15):
                    dve.wait_ge(*K.at(("tap_added", "middle_tap")[i == 0], b + 1))
                    nc.vector.scalar_tensor_tensor(out=dst[b][:, to], in0=m.u[:, b, of], scalar=tap(j, b), in1=dst[b][:, to],
                                                   op0=ALU.mult, op1=ALU.add).then_inc(*K.inc("tap_added"))
            dve.wait_ge(*K.at("tap_added", 30))
            for b in range(4):
                nc.vector.tensor_scalar(m.kk[:, b, :], m.k[:, b, :], K.col("k_k", b), None, ALU.mult)

        @block.scalar
        def _(act):
            act.wait_ge(*K.at("u_loaded", 16))
            for b in range(15):
                nc.scalar.activation(dst[b], m.u[:, b, :], ACT.Copy, scale=K.col("shift_w", 15 + b)).then_inc(*K.inc("middle_tap"))
            act.wait_ge(*K.at("tap_added", 30))
            nc.scalar.activation(m.lw, m.lw, ACT.Tanh)
            nc.scalar.activation(m.lg, m.lg, ACT.Sigmoid)
    K.end_stage()
    norm_stage(K, [dict(src=[m.kk[:, b, :]], ones=K.pair, inv=1.0, eps=K.eps["kk"],
                        out=[(m.kk[:, b, :], m.kk[:, b, :], slice(0, T), None, None)]) for b in range(4)], work)


def rwkv_rates(K, m, s):
    nc = K.nc
    jobs = []
    for d in range(2):
        rows = slice(64 * d, 64 * d + 64)
        for which, src, out, bias in ((0, m.lw, m.of[d].decay, "w0"), (1, m.la, m.of[d].rate, "a0")):
            for b in range(4):
                jobs.append(dict(
                    pieces=[], rows=(0, P), n=T, only="act",
                    mm=lambda _, rows=rows, which=which, src=src, b=b: [(m.lora[rows, which, b * P:(b + 1) * P], src[rows])],
                    evac=lambda side, ps, eng, out=out, bias=bias, b=b, d=d:
                        nc.scalar.activation(out[:, b, :], ps, ACT.Sigmoid, bias=K.col(bias, 4 * d + b))))
    if s == 0:
        jobs += [dict(pieces=[], rows=(0, P), n=T, only="dve", mm=lambda _, b=b: [(m.lora[:, 2, b * P:(b + 1) * P], m.lg)],
                      evac=lambda side, ps, eng, b=b: evacuate(K, side, m.gate[:, b, :], ps)) for b in range(4)]
    gemm_stage(K, 0, jobs, "rwkv_rates")


def rwkv_scale(K, m, s):
    nc = K.nc
    by_chunk = lambda a: a.rearrange("p b (c t) -> p (b c) t", t=CH)
    r, k, kk = (by_chunk(a) for a in (m.r, m.k, m.kk))
    c = -math.exp(-0.5)

    def scale(eng, d, tag):
        w = m.of[d]
        L, p0, p1, e2, rate, keff = (by_chunk(a) for a in (w.decay, w.p0, w.p1, w.e2, w.rate, w.keff))
        done = f"cumulated_{tag}"
        for i in range(4):
            h = i % 2
            eng.memset(w.bd[64 * h:64 * h + 64, i // 2, :, 64 - 64 * h:128 - 64 * h], 0.0).then_inc(*K.inc(f"cleared_{tag}"))
        eng.wait_ge(*K.at(f"cleared_{tag}", 4))
        src = L
        for i in range(6):
            sh, dst = 1 << i, (p0, p1)[i % 2]
            lo, hi, keep = slice(0, CH - sh), slice(sh, CH), (slice(0, sh), slice(CH - sh, CH))[d]
            to, of = ((hi, lo), (lo, hi))[d]
            eng.tensor_copy(dst[:, :, keep], src[:, :, keep]).then_inc(*K.inc(done))
            eng.tensor_tensor(dst[:, :, to], src[:, :, to], src[:, :, of], ALU.add).then_inc(*K.inc(done))
            eng.wait_ge(*K.at(done, 2 * i + 2))
            src = dst
        eng.tensor_tensor(p0, p1, L, ALU.subtract).then_inc(*K.inc(done))
        for b in range(4):
            eng.tensor_scalar(w.keff[:, b, :], w.rate[:, b, :], -1.0, K.col("k_a", b), ALU.add, ALU.mult).then_inc(*K.inc(done))
        eng.wait_ge(*K.at(done, 17))
        eng.tensor_tensor(keff, keff, k, ALU.mult).then_inc(*K.inc(done))
        eng.tensor_tensor(rate, rate, kk, ALU.mult).then_inc(*K.inc(done))
        eng.wait_ge(*K.at(done, 19))
        eng.tensor_tensor(keff, keff, k, ALU.add).then_inc(*K.inc(f"effective_key_{tag}"))
        eng.tensor_scalar(rate, rate, -1.0, None, ALU.mult).then_inc(*K.inc(done))
        eng.wait_ge(*K.at(done, 20))
        eng.wait_ge(*K.at(f"effective_key_{tag}", 1))
        eng.wait_ge(*K.at(f"exps_{tag}", 3))
        eng.tensor_tensor(w.ar[:, :, 0, :], kk, p0, ALU.mult).then_inc(*K.inc(f"scaled_{tag}"))
        eng.tensor_tensor(w.bk[:, :, 0, :], rate, p1, ALU.mult).then_inc(*K.inc(f"scaled_{tag}"))
        eng.tensor_tensor(w.ar[:, :, 1, :], r, e2, ALU.mult)
        eng.tensor_tensor(w.bk[:, :, 1, :], keff, p1, ALU.mult)
        eng.tensor_copy(m.g_end[:, d].unsqueeze(2), e2[:, :, (CH - 1, 0)[d]:(CH, 1)[d]])

    with K.block("rwkv_scale") as block:
        @block.vector
        def _(dve):
            scale(nc.vector, 0, "dve")
            if s == 0:
                t, other = m.of[0].decay, m.of[1].keff
                dve.wait_ge(*K.at("effective_key_pool", 1))
                K.step(dve, nc.vector.tensor_tensor(t, m.of[0].keff, other, ALU.add), "dve_step")
                K.step(dve, nc.vector.tensor_tensor(t, t, m.r, ALU.mult), "dve_step")
                for b in range(4):
                    nc.vector.tensor_scalar(t[:, b, :], t[:, b, :], K.col("r_k", b), None, ALU.mult).then_inc(*K.inc("bonus_ready"))
                for b in range(4):
                    dve.wait_ge(*K.at("bonus_summed", b + 1))
                    nc.vector.tensor_tensor(m.y[:, b, :], K.ps[:, b, 0:T], m.v[:, b, :], ALU.mult)

        @block.gpsimd
        def _(pool):
            scale(nc.gpsimd, 1, "pool")

        @block.tensor
        def _(pe):
            if s == 0:
                for b in range(4):
                    pe.wait_ge(*K.at("bonus_ready", b + 1))
                    nc.tensor.matmul(K.ps[:, b, 0:T], K.pair, m.of[0].decay[:, b, :], start=True, stop=True).then_inc(*K.inc("bonus_summed"))

        @block.scalar
        def _(act):
            for d, tag in enumerate(("dve", "pool")):
                w = m.of[d]
                act.wait_ge(*K.at(f"cumulated_{tag}", 13))
                nc.scalar.activation(w.e2, w.p1, ACT.Exp, scale=c).then_inc(*K.inc(f"exps_{tag}"))
                nc.scalar.activation(w.p0, w.p0, ACT.Exp, scale=c).then_inc(*K.inc(f"exps_{tag}"))
                act.wait_ge(*K.at(f"exps_{tag}", 1))
                nc.scalar.activation(w.p1, w.p1, ACT.Exp, scale=-c).then_inc(*K.inc(f"exps_{tag}"))
            for d, tag in enumerate(("dve", "pool")):
                w = m.of[d]
                for i, src in enumerate((w.ar, w.bk)):
                    act.wait_ge(*K.at(f"scaled_{tag}", i + 1))
                    for h in range(2):
                        rows = slice(64 * h, 64 * h + 64)
                        nc.scalar.activation(w.bd[rows, i, :, 64 * h:64 * h + 64], src[rows, :, 0, :], ACT.Copy)
    K.end_stage()


def rwkv_products(K, m):
    nc = K.nc
    flat = lambda a: a.rearrange("p w t -> p (w t)")
    jobs = []

    def job(emit, evac, only, rows=(0, P)):
        jobs.append(dict(pieces=[], rows=rows, n=512, only=only, emit=emit, evac=evac))

    for d in range(2):
        w = m.of[d]
        mask = flat(m.causal[:, d]).unsqueeze(1).broadcast_to([P, 4, P])
        for q in range(4):
            chunks = range(4 * q, 4 * q + 4)
            for h in range(2):
                def emit(bank, w=w, h=h, chunks=chunks):
                    for i in chunks:
                        rows = slice(64 * h, 64 * h + 64)
                        last = nc.tensor.matmul(K.ps[:, bank, i % 4 * P:(i % 4 + 1) * P], flat(w.bk[rows, i]), flat(w.ar[rows, i]),
                                                start=True, stop=True)
                    return last
                job(emit, lambda side, ps, eng, w=w, q=q, h=h, mask=mask: nc.vector.tensor_tensor(
                    w.w[:, 4 * q:4 * q + 4, h, :], ps.rearrange("p (i c) -> p i c", i=4), mask, ALU.mult), "dve")
            for t in range(2):
                def emit(bank, w=w, t=t, chunks=chunks):
                    for i in chunks:
                        last = nc.tensor.matmul(K.ps[:, bank, i % 4 * P:(i % 4 + 1) * P], w.bd[:, t, i, :], w.bd[:, 1 - t, i, :],
                                                start=True, stop=True)
                    return last
                strict = m.causal[:, (1 - d, d)[t], 0, :].unsqueeze(1).broadcast_to([P, 8, CH])
                job(emit, lambda side, ps, eng, w=w, q=q, t=t, strict=strict: nc.vector.tensor_tensor(
                    w.n[:, t, 4 * q:4 * q + 4, :].rearrange("p i (h c) -> p (i h) c", h=2),
                    ps.rearrange("p (i c) -> p i c", i=8), strict, ALU.mult), "dve")

            def emit(bank, w=w, chunks=chunks):
                for i in chunks:
                    last = nc.tensor.transpose(K.ps[:, bank, i % 4 * P:(i % 4 + 1) * P], flat(w.bk[:, i]), K.ident)
                return last
            job(emit, lambda side, ps, eng, w=w, q=q: nc.scalar.activation(
                w.tok[:, 4 * q:4 * q + 4].rearrange("p i c -> p (i c)"), ps, ACT.Copy), "act")
        for q in range(4):
            def emit(bank, q=q):
                for i in range(4 * q, 4 * q + 4):
                    c0 = 2048 + CH * i - CH
                    last = nc.tensor.transpose(K.ps[:, bank, i % 4 * P:(i % 4 + 1) * P], m.rkv[:, c0:c0 + P], K.ident)
                return last
            job(emit, lambda side, ps, eng, w=w, q=q: nc.scalar.activation(
                w.uv[64:128, 4 * q:4 * q + 4].rearrange("p i h v -> p (i h v)"), ps[64:128], ACT.Copy), "act")
    gemm_stage(K, 0, jobs, "rwkv_products")


def rwkv_inverse(K, m):
    nc, levels = K.nc, 6
    jobs = []
    for i in range(1, levels):
        jobs += [(i, "z", d, q) for d in range(2) for q in range(4)]
        jobs += [(i, kind, d, q) for d in range(2) for q in range(4) for kind in (("x", "xT") if i < levels - 1 else ("xT",))]
    where = {job: j for j, job in enumerate(jobs)}
    quarter = lambda a, q: a[:, 4 * q:4 * q + 4, :]
    by_head = lambda a: a.rearrange("p i (h c) -> p (i h) c", h=2)

    with K.block("rwkv_inverse") as block:
        @block.vector
        def _(dve):
            level = lambda dd, i: m.level[:, dd, i, :].unsqueeze(1).broadcast_to([P, 8, CH])
            eye = K.ident.unsqueeze(1).broadcast_to([P, 4, P])
            for d in range(2):
                w = m.of[d]
                for q in range(4):
                    for t in range(2):
                        x = quarter(w.x[:, t], q)
                        nc.vector.tensor_tensor(by_head(x), by_head(quarter(w.n[:, t], q)), level((d, 1 - d)[t], 0), ALU.mult)\
                            .then_inc(*K.inc("first_level"))
                        dve.wait_ge(*K.at("first_level", 8 * d + 2 * q + t + 1))
                        last = nc.vector.tensor_tensor(x, x, eye, ALU.add)
                    last.then_inc(*K.inc("inverse_begun"))
            for j, (i, kind, d, q) in enumerate(jobs):
                w = m.of[d]
                ps = K.ps[:, j % NBANK, :].rearrange("p (i c) -> p i c", i=4)
                dve.wait_ge(*K.at("inverse_product", j + 1))
                if kind == "z":
                    out = quarter(w.n[:, 0], q)
                    last = nc.vector.tensor_tensor(by_head(out), by_head(ps), level(d, i), ALU.mult)
                else:
                    if kind == "x":
                        dve.wait_ge(*K.at("inverse_product", where[i, "xT", d, q] + 1))
                    x = quarter(w.x[:, 0 if kind == "x" else 1], q)
                    last = nc.vector.tensor_tensor(x, x, ps, ALU.add)
                last.then_inc(*K.inc("inverse_kept"))

        @block.tensor
        def _(pe):
            for j, (i, kind, d, q) in enumerate(jobs):
                w = m.of[d]
                if j >= NBANK:
                    pe.wait_ge(*K.at("inverse_kept", j - NBANK + 1))
                if kind == "z" and i == 1:
                    pe.wait_ge(*K.at("inverse_begun", 4 * d + q + 1))
                elif kind == "z":
                    pe.wait_ge(*K.at("inverse_kept", where[i - 1, "xT", d, q] + 1))
                else:
                    pe.wait_ge(*K.at("inverse_kept", where[i, "z", d, q] + 1))
                lhs, rhs = {"z": (w.n[:, 1], w.x[:, 0]), "x": (w.x[:, 1], w.n[:, 0]), "xT": (w.n[:, 0], w.x[:, 1])}[kind]
                for c in range(4 * q, 4 * q + 4):
                    last = nc.tensor.matmul(K.ps[:, j % NBANK, c % 4 * P:(c % 4 + 1) * P], lhs[:, c, :], rhs[:, c, :], start=True, stop=True)
                last.then_inc(*K.inc("inverse_product"))

        @block.gpsimd
        def _(pool):
            for d in range(2):
                nc.gpsimd.memset(m.of[d].uv[0:64], 0.0)
    K.end_stage()


def rwkv_chunks(K, m, s):
    nc = K.nc
    order = (range(4), range(3, -1, -1))
    heads = [(b, h) for b in range(4) for h in range(2)]
    tags = ("forward", "backward")
    out = s == 0
    steps = [(n, d) for n in range(4) for d in range(2)]
    with K.block("rwkv_chunks") as block:
        @block.tensor
        def _(pe):
            def right_sides(n, d):
                w, c = m.of[d], order[d][n]
                if n:
                    pe.wait_ge(*K.at(f"state_{tags[d]}", n))
                for b, h in heads:
                    rows, i = slice(64 * h, 64 * h + 64), 4 * b + c
                    to = K.ps[rows, 3 * d, b * CH:(b + 1) * CH]
                    nc.tensor.matmul(to, w.ar[rows, i, 0, :], m.state[rows, d, b, :], start=True, stop=False)
                    last = nc.tensor.matmul(to, w.w[:, i, h, 0:CH], w.uv[:, i, h, :], start=False, stop=True)
                last.then_inc(*K.inc("right_sides"))

            def solve(n, d):
                w, c = m.of[d], order[d][n]
                pe.wait_ge(*K.at("right_sides_kept", 2 * n + d + 1))
                for b, h in heads:
                    rows, i = slice(64 * h, 64 * h + 64), 4 * b + c
                    last = nc.tensor.matmul(K.ps[0:64, 3 * d + 1 + h, b * CH:(b + 1) * CH], w.x[rows, 1, i, 64 * h:64 * h + 64],
                                            m.rhs[rows, d, b, :], start=True, stop=True)
                last.then_inc(*K.inc("solved"))

            def advance(n, d):
                w, c = m.of[d], order[d][n]
                pe.wait_ge(*K.at("solution_kept", 2 * n + d + 1))
                for b, h in heads:
                    rows, i = slice(64 * h, 64 * h + 64), 4 * b + c
                    if out:
                        to = K.ps[rows, 3 * d, 256 + b * CH:256 + (b + 1) * CH]
                        nc.tensor.matmul(to, m.state[rows, d, b, :], w.ar[rows, i, 1, :], start=True, stop=False)
                        nc.tensor.matmul(to, w.uv[:, i, h, :], w.w[:, i, h, CH:2 * CH], start=False, stop=True)
                    last = nc.tensor.matmul(K.ps[rows, 3 * d + 1, 256 + b * CH:256 + (b + 1) * CH], w.tok[:, i, 64 * h:64 * h + 64],
                                            w.uv[:, i, h, :], start=True, stop=True)
                last.then_inc(*K.inc("chunk_done"))
            for n in range(4):
                for phase in (right_sides, solve, advance):
                    for d in range(2):
                        phase(n, d)

        @block.scalar
        def _(act):
            for j, (n, d) in enumerate(steps):
                act.wait_ge(*K.at("right_sides", j + 1))
                nc.scalar.activation(m.rhs[:, d].rearrange("p b v -> p (b v)"), K.ps[:, 3 * d, 0:256], ACT.Copy)\
                    .then_inc(*K.inc("right_sides_kept"))

        @block.vector
        def _(dve):
            for n in range(4):
                for d in range(2):
                    w, c = m.of[d], order[d][n]
                    dve.wait_ge(*K.at("solved", 2 * n + d + 1))
                    for h in range(2):
                        uv = w.uv.rearrange("p (b c) h v -> p b c h v", b=4)[0:64, :, c, h, :]
                        last = nc.vector.tensor_copy(uv, K.ps[0:64, 3 * d + 1 + h, 0:256].rearrange("p (b v) -> p b v", b=4))
                    last.then_inc(*K.inc("solution_kept"))
                for d in range(2):
                    c, S = order[d][n], m.state[:, d]
                    g = m.g_end[:, d].rearrange("p (b c) -> p b c", b=4)[:, :, c:c + 1].broadcast_to([P, 4, CH])
                    dve.wait_ge(*K.at("chunk_done", 2 * n + d + 1))
                    if out:
                        y = m.y[:, :, c * CH:(c + 1) * CH]
                        nc.vector.tensor_tensor(y, y, K.ps[:, 3 * d, 256:512].rearrange("p (b t) -> p b t", b=4), ALU.add)
                    K.step(dve, nc.vector.tensor_tensor(S, S, K.ps[:, 3 * d + 1, 256:512].rearrange("p (b v) -> p b v", b=4), ALU.add), "dve_step")
                    nc.vector.tensor_tensor(S, S, g, ALU.mult).then_inc(*K.inc(f"state_{tags[d]}"))
    K.end_stage()


def store_stage(K, out):
    with K.block("store") as block:
        @block.sync
        def _(sp):
            sp.dma_start(out.rearrange("(k p) t -> p k t", p=P), K.XT[:, :, X]).then_inc(*K.inc("output_stored", 16))
            sp.wait_ge(*K.at("output_stored", 16))
    K.end_stage()


def build_program(nc, dram, out, layers=("f0", "f1", "s0", "s1")):
    with ExitStack() as ctx:
        K = Kit(nc, ctx, dram)
        K.const, K.eps = {}, {}
        K.u_dram = nc.dram_tensor("rwkv_inputs", (2, P, 15 * T), F32, kind="Internal").ap()
        for l in range(DEPTH):
            if f"f{l}" in layers:
                for name in ("w_mod", "w_in", "w_out", "w_up", "w_down"):
                    K.plan(name, l)
        if "s0" in layers:
            plan_even(K)
        if "s1" in layers:
            plan_odd(K)
        prologue(K)
        for l in range(DEPTH):
            if f"f{l}" in layers:
                first_layer(K, l)
        if "s0" in layers:
            even_layer(K)
        if "s1" in layers:
            odd_layer(K)
        store_stage(K, out)


def tiled(w, parts):
    return np.concatenate([w[r0:r1, c0:c1].reshape((r1 - r0) // P, P, c1 - c0).transpose(1, 0, 2).ravel()
                           for r0, r1, c0, c1 in parts])


def constant_tables():
    out = {n: np.zeros((P, w), np.float64) for n, w in CONSTS.items()}
    out["ident"][:] = np.eye(P)
    out["ones"][:] = 1
    out["pair"][:64, :64] = out["pair"][64:, 64:] = 1
    t = np.arange(T)
    row, col = (t // GRID_W).astype(np.float32), (t % GRID_W).astype(np.float32)

    def rope(base, width, reps, swap, cos, sin):
        half, quarter = width // 2, width // 4
        inv = (np.float32(1.0) / np.float32(10000.0) ** (np.arange(0, half, 2, dtype=np.float32) / np.float32(half))).astype(np.float32)
        out[cos][:] = 1
        for r in range(reps):
            for i in range(width):
                j = i % half
                ang = ((row if i < half else col) * inv[j % quarter]).astype(np.float32).astype(np.float64)
                p = base + r * width + i
                out[cos][p], out[sin][p] = np.cos(ang), (-1 if j < quarter else 1) * np.sin(ang)
                out[swap][p + (quarter if j < quarter else -quarter), p] = 1
    rope(0, 64, 2, "swap1", "cos1", "sin1")
    rope(64, 32, 1, "swap2", "cos2", "sin2")
    ang = 2 * np.pi * (np.outer(t, t) % T) / T
    out["cn"][:] = (np.cos(ang) / 16).reshape(2, P, T).transpose(1, 0, 2).reshape(P, 512)
    out["sn"][:] = (np.sin(ang) / 16).reshape(2, P, T).transpose(1, 0, 2).reshape(P, 512)
    m = np.arange(64)
    ang = 2 * np.pi * (np.outer(m, m) % 64) / 64
    for g in range(2):
        s = slice(64 * g, 64 * g + 64)
        out["cm"][s, s], out["sm"][s, s] = np.cos(ang) / 8, -np.sin(ang) / 8
    out["tri"][:] = np.triu(np.ones((P, P)))
    out["iota"][:] = np.arange(1, 65)[None]
    c = np.arange(GRID_W)
    start = np.clip(c - 8, 0, GRID_W - 16)
    inside = (c[None] >= start[:, None]) & (c[None] < start[:, None] + 16)
    add = np.where(inside[t % GRID_W][:, t % GRID_W], 0.0, -1e30)
    out["window"][:] = add.reshape(2, P, T).transpose(1, 0, 2).reshape(P, 512)
    s, u = np.arange(CH)[:, None], np.arange(CH)[None]
    causal = [np.concatenate([before(s, u), ~before(u, s)], 1) for before in (np.less, np.greater)]
    out["causal"][:] = np.tile(np.concatenate(causal, 1), (2, 1))
    for i in range(6):
        b = 1 << i
        low = (s // (2 * b) == u // (2 * b)) & (s // b % 2 == 1) & (u // b % 2 == 0)
        for d, msk in enumerate((low, low.T)):
            at = (d * 6 + i) * 64
            out["level"][:, at:at + 64] = np.tile(msk, (2, 1))
    out["flip"][:] = np.kron(np.eye(2), np.eye(64)[::-1])
    return np.concatenate([out[n] for n in CONSTS], 1).astype(np.float32)


def as_columns(v):
    v = np.asarray(v, np.float32).reshape(-1)
    v = np.concatenate([v, np.zeros(-len(v) % P, np.float32)])
    return v.reshape(-1, P).T


def host_arrays(a):
    f = {k: np.asarray(v) for k, v in a.items()}
    vec = {
        "c": f["c"], "c_ctx": f["c_ctx"], "c_2": f["c_2"], "c_ctx_2": f["c_ctx_2"],
        "q_norm": f["mla_q_norm_2"], "kv_norm": f["mla_kv_norm_2"], "q_g": f["mla_q_g_2"], "k_g": f["mla_k_g_2"],
        "dw_w": f["cv_dw_w_2"], "dw_b": f["cv_dw_b_2"], "cln_g": f["cv_ln_g_2"], "cln_b": f["cv_ln_b_2"],
        "shift_w": f["rw_shift_w_2"], "w0": f["rw_w0_2"], "a0": f["rw_a0_2"], "k_k": f["rw_k_k_2"], "k_a": f["rw_k_a_2"],
        "r_k": f["rw_r_k_2"], "gn_g": f["rw_gn_g_2"], "gn_b": f["rw_gn_b_2"],
        "na_q": np.tile(f["na_q_g_2"].reshape(-1), 2), "na_k": np.tile(f["na_k_g_2"].reshape(-1), 2),
    }
    for l in range(DEPTH):
        vec |= {f"b_mod{l}": f["b_mod"][l], f"ada_b{l}": f["ada_b_2"][l], f"subln{l}": f["subln_w"][l],
                f"conv_w{l}": f["conv_w"][l], f"conv_b{l}": f["conv_b"][l],
                f"norm1_g{l}": f["norm1_g_2"][l], f"norm2_g{l}": f["norm2_g_2"][l]}
        vec |= {f"{n}{l}": f[n][l] for n in ("ln1_g", "ln1_b", "ln2_g", "ln2_b")}
    out = {"cols": np.concatenate([as_columns(vec[n]) for n in COLS], 1), "consts": constant_tables(),
           "diff_lambda": f["diff_lambda"].reshape(-1), "na_rpb": f["na_rpb_2"].reshape(-1)}
    out |= {n: np.ascontiguousarray(f[n][0].T) for n in ("x", "ctx", "ctx_2")}
    weights = {
        "w_mod": f["w_mod"], "w_in": f["w_in"], "w_out": f["w_out"], "w_up": f["w_up"], "w_down": f["w_down"],
        "ada_w": f["ada_w_2"], "ev_w_in": f["ev_w_in_2"], "ev_w_out": f["ev_w_out_2"], "w_uq": f["mla_w_uq_2"],
        "w_ukv": f["mla_w_ukv_2"], "router": f["moe_router_2"], "od_w_in": f["od_w_in_2"], "od_w_out": f["od_w_out_2"],
        "lora": np.concatenate([f["rw_w2_2"].reshape(1, P, 512), f["rw_a2_2"].reshape(1, P, 512), f["rw_g2_2"]], 1),
    }
    for n, w in weights.items():
        out[n] = np.stack([tiled(w[l], PARTS[n]) for l in range(w.shape[0])])
    for n in ("moe_w1_2", "moe_w3_2", "moe_w2_2"):
        w = f[n]
        out[n[:6]] = np.ascontiguousarray(w.reshape(DEPTH, NE, KD, P, 2, 512).transpose(0, 1, 4, 3, 2, 5)).reshape(DEPTH, NE, 2, P, SLOT)
    return {k: np.ascontiguousarray(v) for k, v in out.items()}


def kernel(**inputs):
    import concourse.bacc as bacc
    from concourse.bass_utils import run_bass_kernel_spmd

    nc = bacc.Bacc("TRN2", target_bir_lowering=False, num_devices=1)
    arrays = {f"in_{n}": a for n, a in host_arrays(inputs).items()}
    dram = {n[3:]: nc.dram_tensor(n, a.shape, mybir.dt.from_np(a.dtype), kind="ExternalInput").ap() for n, a in arrays.items()}
    out = nc.dram_tensor("out_x", (D, T), F32, kind="ExternalOutput").ap()
    build_program(nc, dram, out)
    r = run_bass_kernel_spmd(nc, [arrays], core_ids=[0])
    return np.ascontiguousarray(np.asarray(r.results[0]["out_x"]).T).reshape(1, T, D)
```

```python
import math
from contextlib import ExitStack

import numpy as np

import concourse.bass as bass
from concourse import mybir

F32 = mybir.dt.float32
ALU = mybir.AluOpType
ACT = mybir.ActivationFunctionType
AX = mybir.AxisListType.X

P = 128
D = 1024
KD = D // P
T = 256
TT = 2 * T
X, C = slice(0, T), slice(T, TT)
SEGS = (X, C)
DEPTH = 2
FF = 4 * D
RING = 6
SLOT = 4096
NBANK = 8
ALPHA = (2 * DEPTH) ** 0.25
NE = 16
CAP = 32
CH = 64
GRID_W = 64


def column_parts(w, step=512):
    rows, cols = w
    return [(0, rows, c, min(c + step, cols)) for c in range(0, cols, step)]


def ranges(rows, *cuts):
    return [(0, rows, a, b) for a, b in cuts]


PARTS = {
    "w_mod": column_parts((D, 6 * D)),
    "w_in": column_parts((D, 2560)),
    "w_out": column_parts((D, D)),
    "w_up": column_parts((D, FF)),
    "w_down": [(r, r + D, c, c + 512) for c in (0, 512) for r in range(0, FF, D)],
    "ada_w": column_parts((D, 6 * D)),
    "ev_w_in": ranges(D, (0, 384), (384, 672), (672, 1184), (1184, 1696)),
    "ev_w_out": column_parts((D, D)),
    "w_uq": ranges(384, (0, 768)),
    "w_ukv": ranges(256, (0, 1024)),
    "router": ranges(D, (0, NE)),
    "od_w_in": ranges(D, (1920, 2432), (2432, 2944), (2944, 3456), (0, 512), (512, 1024), (1024, 1536), (1536, 1920)),
    "lora": ranges(384, (0, 512)),
    "od_w_out": column_parts((D, D)),
    "moe": column_parts((D, D)),
}

COLS = {
    "c": D, "c_ctx": D, "c_2": D, "c_ctx_2": D,
    "b_mod0": 6 * D, "b_mod1": 6 * D, "ada_b0": 6 * D, "ada_b1": 6 * D,
    "subln0": P, "subln1": P,
    "conv_w0": 3 * T, "conv_w1": 3 * T, "conv_b0": T, "conv_b1": T,
    "ln1_g0": D, "ln1_b0": D, "ln2_g0": D, "ln2_b0": D,
    "ln1_g1": D, "ln1_b1": D, "ln2_g1": D, "ln2_b1": D,
    "norm1_g0": D, "norm1_g1": D, "norm2_g0": D, "norm2_g1": D,
    "q_norm": 384, "kv_norm": 256, "q_g": P, "k_g": P,
    "dw_w": 31 * 512, "dw_b": 512, "cln_g": 512, "cln_b": 512,
    "shift_w": 3 * 1920, "w0": 1024, "a0": 1024, "k_k": 512, "k_a": 512, "r_k": 512,
    "gn_g": 512, "gn_b": 512, "na_q": P, "na_k": P,
}
COL_AT, NCOL = {}, 0
for _name, _n in COLS.items():
    COL_AT[_name] = NCOL
    NCOL += _n // P

CONSTS = {
    "ident": 128, "ones": 128, "pair": 128, "swap1": 128, "cos1": 256, "sin1": 256,
    "swap2": 128, "cos2": 256, "sin2": 256, "cn": 512, "sn": 512, "cm": 128, "sm": 128,
    "tri": 128, "iota": 64, "window": 512, "causal": 256, "level": 768,
    "flip": 128,
}
CONST_AT, NCONST = {}, 0
for _name, _n in CONSTS.items():
    CONST_AT[_name] = NCONST
    NCONST += _n


class Kit:

    def __init__(self, nc, ctx, dram):
        self.nc, self.ctx, self.dram = nc, ctx, dram
        self.times = 1
        self.sems, self.given, self.base = {}, {}, {}
        self.stream, self.cursor, self.issued, self.stages = [], 0, 0, 0
        self.ring = self.sb("ring", [P, RING, SLOT])
        self.XT = self.sb("XT", [P, KD, TT])
        self.HT = self.sb("HT", [P, KD, TT])
        self.arena = self.sb("arena", [P, 18432])
        self.cols = self.sb("cols", [P, NCOL])
        self.base_consts = self.sb("base_consts", [P, 3 * 128])
        self.sil = self.sb("sil", [P, 2, KD, 32])
        self.modcol = self.sb("modcol", [P, 2, 48])
        self.gain = self.sb("gain", [P, 2, KD])
        self.small = self.sb("small", [P, 80])
        self.ps = ctx.enter_context(nc.psum_tensor("ps", [P, NBANK, 512], F32))
        self.ident = self.base_consts[:, 0:128]
        self.ones = self.base_consts[:, 128:256]
        self.pair = self.base_consts[:, 256:384]

    def sb(self, name, shape):
        return self.ctx.enter_context(self.nc.sbuf_tensor(name, shape, F32))

    def block(self, name):
        self.stages += 1
        return self.nc.Block(f"{name}_{self.stages}")

    def sem(self, name):
        if name not in self.sems:
            self.sems[name] = self.ctx.enter_context(self.nc.semaphore(name))
            self.given[name] = self.base[name] = 0
        return self.sems[name]

    def inc(self, name, n=1):
        s = self.sem(name)
        self.given[name] += n * self.times
        return s, n

    def at(self, name, n):
        return self.sem(name), self.base[name] + n

    def end_stage(self):
        self.base = dict(self.given)

    def step(self, eng, ins, name):
        s, n = self.inc(name)
        ins.then_inc(s, n)
        eng.wait_ge(s, self.given[name])

    def start_moves(self, sp, pairs):
        for dst, src in pairs:
            sp.dma_start(dst, src).then_inc(*self.inc("moved_aside", 16))

    def end_moves(self, sp, pairs):
        if pairs:
            sp.wait_ge(*self.at("moved_aside", 16 * len(pairs)))

    def constants(self, names, where):
        at, pairs = 0, []
        for name in names:
            w = CONSTS[name]
            pairs.append((where[:, at:at + w], self.dram["consts"][:, CONST_AT[name]:CONST_AT[name] + w]))
            self.const[name] = where[:, at:at + w]
            at += w
        return pairs

    def col(self, name, i=0, n=1):
        return self.cols[:, COL_AT[name] + i:COL_AT[name] + i + n]

    def plan(self, name, layer=None, parts=None):
        at = 0
        flat = self.dram[name] if layer is None else self.dram[name][layer]
        for r0, r1, c0, c1 in parts or PARTS[name]:
            n = (r1 - r0) * (c1 - c0)
            self.stream.append((flat[at:at + n], (r1 - r0) // P, c1 - c0))
            at += n

    def slot(self, i):
        _, kc, w = self.stream[i]
        return self.ring[:, i % RING, 0:kc * w].rearrange("p (k w) -> p k w", k=kc)

    def load_next(self, sp):
        i = self.issued
        if i < len(self.stream):
            src, kc, w = self.stream[i]
            sp.dma_start(self.ring[:, i % RING, 0:kc * w], src.rearrange("(p n) -> p n", p=P)).then_inc(
                self.sem(f"slot{i % RING}_landed"), 16)
        self.issued += 1

    def landed(self, i):
        return self.sem(f"slot{i % RING}_landed"), 16 * (i // RING + 1)


def evacuate(K, side, out, in_, scale=None, bias=None):
    nc = K.nc
    if side == "act":
        kw = {}
        if scale is not None:
            kw["scale"] = scale
        if bias is not None:
            kw["bias"] = bias
        return nc.scalar.activation(out, in_, ACT.Identity if kw else ACT.Copy, **kw)
    if scale is None and bias is None:
        return nc.vector.tensor_copy(out, in_)
    if bias is None:
        return nc.vector.tensor_scalar(out, in_, scale, None, ALU.mult)
    if scale is None:
        return nc.vector.tensor_scalar(out, in_, bias, None, ALU.add)
    return nc.vector.tensor_scalar(out, in_, scale, bias, ALU.mult, ALU.add)


def gemm_stage(K, npieces, jobs, name="gemm", feed=None, also=()):
    nc, first = K.nc, K.cursor
    uses = [max(j for j, job in enumerate(jobs) if i in job["pieces"]) for i in range(npieces)]
    sides = [job.get("only") or ("act", "dve")[j % 2] for j, job in enumerate(jobs)]
    turn = [sides[:j + 1].count(sides[j]) for j in range(len(jobs))]

    def bank_of(job, j):
        p0, p1 = job["rows"]
        return K.ps[p0:p1, j % NBANK, 0:job["n"]]

    with K.block(name) as block:
        @block.sync
        def _(sp):
            K.start_moves(sp, also)
            for i in range(npieces):
                if feed is None or i < feed:
                    sp.wait_ge(*K.at("products_done", uses[i] + 1))
                    K.load_next(sp)
            K.end_moves(sp, also)

        @block.tensor
        def _(pe):
            seen = set()
            for j, job in enumerate(jobs):
                for i in job["pieces"]:
                    if i not in seen:
                        seen.add(i)
                        pe.wait_ge(*K.landed(first + i))
                if j >= NBANK:
                    pe.wait_ge(*K.at(sides[j - NBANK] + "_evacuated", turn[j - NBANK]))
                if "emit" in job:
                    last = job["emit"](j % NBANK)
                else:
                    terms = job["mm"]([K.slot(first + i) for i in job["pieces"]])
                    for n, (lhsT, rhs) in enumerate(terms):
                        last = nc.tensor.matmul(bank_of(job, j), lhsT, rhs, start=n == 0, stop=n == len(terms) - 1)
                last.then_inc(*K.inc("products_done"))

        @block.scalar
        def _(act):
            for j, job in enumerate(jobs):
                if sides[j] == "act":
                    act.wait_ge(*K.at("products_done", j + 1))
                    job["evac"]("act", bank_of(job, j), act).then_inc(*K.inc("act_evacuated"))

        @block.vector
        def _(dve):
            for j, job in enumerate(jobs):
                if sides[j] == "dve":
                    dve.wait_ge(*K.at("products_done", j + 1))
                    job["evac"]("dve", bank_of(job, j), dve).then_inc(*K.inc("dve_evacuated"))
    K.cursor += npieces
    K.end_stage()


def feature_job(K, piece, c0, width, rhs, out, p0=0, scale=None, evac=None, only=None):
    n = rhs.shape[-1]
    return dict(
        pieces=[piece], rows=(p0, p0 + width), n=n, only=only,
        mm=lambda slots: [(slots[0][:, k, c0:c0 + width], rhs[:, k, :]) for k in range(slots[0].shape[1])],
        evac=evac or (lambda side, ps, eng: evacuate(K, side, out, ps, scale=scale)))


def token_job(K, piece, cols, lhs, t, out):
    return dict(
        pieces=[piece], rows=(0, P), n=out.shape[-1], only=None,
        mm=lambda slots: [(lhs[:, k, t * P:(t + 1) * P], cols(slots[0], k)) for k in range(slots[0].shape[1])],
        evac=lambda side, ps, eng: evacuate(K, side, out, ps))


def mod_stage(K, sil, bias, one_plus, also=()):
    nc, first, n = K.nc, K.cursor, 12
    rows = K.arena[:, 0:n * P].rearrange("p (n c) -> p n c", n=n)
    with K.block("modulation") as block:
        @block.sync
        def _(sp):
            K.start_moves(sp, also)
            for i in range(n):
                sp.wait_ge(*K.at("rows_done", i + 1))
                K.load_next(sp)
            K.end_moves(sp, also)

        @block.tensor
        def _(pe):
            def transpose(i):
                pe.wait_ge(*K.at("rows_kept", i + 1))
                if i >= 4:
                    pe.wait_ge(*K.at("columns_kept", i - 3))
                nc.tensor.transpose(K.ps[:, 4 + i % 4, 0:P], rows[:, i, :], K.ident).then_inc(*K.inc("columns_done"))
            for i in range(n):
                pe.wait_ge(*K.landed(first + i))
                if i >= 4:
                    pe.wait_ge(*K.at("rows_kept", i - 3))
                w = K.slot(first + i)
                for k in range(KD):
                    for j in range(4):
                        last = nc.tensor.matmul(K.ps[32 * j:32 * j + 32, i % 4, 0:P], sil[:, k, :],
                                                w[:, k, j * P:(j + 1) * P], start=k == 0, stop=k == KD - 1)
                last.then_inc(*K.inc("rows_done"))
                if i:
                    transpose(i - 1)
            transpose(n - 1)

        @block.scalar
        def _(act):
            for i in range(n):
                act.wait_ge(*K.at("rows_done", i + 1))
                nc.scalar.activation(rows[:, i, :], K.ps[:, i % 4, 0:P], ACT.Copy).then_inc(*K.inc("rows_kept"))

        @block.vector
        def _(dve):
            for i in range(n):
                dve.wait_ge(*K.at("columns_done", i + 1))
                got = K.ps[:, 4 + i % 4, 0:P].rearrange("p (j r) -> p r j", r=32)
                b = bias[:, 4 * i:4 * i + 4]
                nc.vector.tensor_tensor(K.modcol[:, 0, 4 * i:4 * i + 4], got[:, 0, :], b, ALU.add)
                nc.vector.tensor_tensor(K.modcol[:, 1, 4 * i:4 * i + 4], got[:, 1, :], b, ALU.add)\
                    .then_inc(*K.inc("columns_kept"))
            dve.wait_ge(*K.at("columns_kept", n))
            for j in one_plus:
                nc.vector.tensor_scalar(K.modcol[:, :, 8 * j:8 * j + 8], K.modcol[:, :, 8 * j:8 * j + 8],
                                        1.0, None, ALU.add)
    K.cursor += n
    K.end_stage()


def mod(K, which, seg, k):
    return K.modcol[:, seg, 8 * which + k:8 * which + k + 1]


def modulate_stage(K, shift, scale, n_seg):
    nc = K.nc
    with K.block("modulate") as block:
        @block.scalar
        def _(act):
            for k in range(0, KD, 2):
                for s in range(n_seg):
                    nc.scalar.activation(K.HT[:, k, SEGS[s]], K.XT[:, k, SEGS[s]], ACT.Identity,
                                         bias=mod(K, shift, s, k), scale=mod(K, scale, s, k))

        @block.vector
        def _(dve):
            for k in range(1, KD, 2):
                for s in range(n_seg):
                    nc.vector.tensor_scalar(K.HT[:, k, SEGS[s]], K.XT[:, k, SEGS[s]],
                                            mod(K, scale, s, k), mod(K, shift, s, k), ALU.mult, ALU.add)
    K.end_stage()


def norm_stage(K, groups, work, centre=False, also=()):
    nc = K.nc
    sq = work[:, 0:4 * TT].rearrange("p (b n) -> p b n", b=4)
    root = work[:, 4 * TT:4 * TT + 4 * P].rearrange("p (g n) -> p g n", g=4)
    means = work[:, 5 * TT:5 * TT + 4 * P].rearrange("p (g n) -> p g n", g=4)
    G = len(groups)
    firsts = [sum(len(g["src"]) for g in groups[:i]) for i in range(G + 1)]
    outs = [sum(len(g["out"]) for g in groups[:i]) for i in range(G + 1)]
    blocks = [s for grp in groups for s in grp["src"]]
    sides = ["dve" if G == 1 and not centre and b % 2 else "act" for b in range(len(blocks))]
    mean_bank = (1, 2, 5, 6)

    def sum_bank(g):
        return 3 + g % 2

    def spread_bank(g):
        return 5 + g % 3

    def square(side, b):
        s = blocks[b]
        out = sq[0:s.shape[0], b % 4, 0:s.shape[1]]
        ins = nc.scalar.activation(out, s, ACT.Square) if side == "act" else nc.vector.tensor_tensor(out, s, s, ALU.mult)
        ins.then_inc(*K.inc("squares_" + side))

    with K.block("norm") as block:
        @block.sync
        def _(sp):
            K.start_moves(sp, also)
            K.end_moves(sp, also)

        @block.tensor
        def _(pe):
            def add_up(grp, bank, c0, block, i):
                half = grp["ones"][:, 48:80]
                for c in range(4):
                    t = c * P % grp["src"][0].shape[1]
                    last = nc.tensor.matmul(K.ps[32 * c:32 * c + 32, bank, c0:c0 + P], half, block[:, t:t + P],
                                            start=i == 0, stop=i == len(grp["src"]) - 1)
                return last

            def spread(grp, rows, bank):
                for c in range(grp["src"][0].shape[1] // P):
                    for h in range(2):
                        pick = K.ident[:, 32 * c + 16 * h:32 * c + 16 * h + 1].broadcast_to([P, 64])
                        last = nc.tensor.matmul(K.ps[64 * h:64 * h + 64, bank, c * P:(c + 1) * P], pick, rows, start=True, stop=True)
                return last

            if centre:
                for g, grp in enumerate(groups):
                    for i, s in enumerate(grp["src"]):
                        last = add_up(grp, 0, g * P, s, i)
                last.then_inc(*K.inc("sums_done"))
                pe.wait_ge(*K.at("means_done", 1))
                for g in range(G):
                    spread(groups[g], means[:, g], mean_bank[g]).then_inc(*K.inc("means_spread"))
            for g in range(G + 2):
                if g < G:
                    grp = groups[g]
                    if g >= 2:
                        pe.wait_ge(*K.at("roots_done", g - 1))
                    for i, s in enumerate(grp["src"]):
                        b = firsts[g] + i
                        pe.wait_ge(*K.at("squares_" + sides[b], sides[:b + 1].count(sides[b])))
                        add_up(grp, sum_bank(g), 0, sq[0:s.shape[0], b % 4], i).then_inc(*K.inc("squares_summed"))
                if g >= 2:
                    j = g - 2
                    pe.wait_ge(*K.at("inverted", j + 1))
                    if j >= 3:
                        pe.wait_ge(*K.at("scaled", outs[j - 2]))
                    spread(groups[j], root[:, j % 4], spread_bank(j)).then_inc(*K.inc("roots_spread"))

        @block.scalar
        def _(act):
            nc.scalar.activation(K.small[:, 44:45], K.eps["zero"], ACT.Sqrt)
            if centre:
                act.wait_ge(*K.at("sums_done", 1))
                nc.scalar.mul(means[:, 0:G], K.ps[:, 0, 0:G * P].rearrange("p (g n) -> p g n", g=G), -groups[0]["inv"])\
                    .then_inc(*K.inc("means_done"))
            for g in range(G + 1):
                if g < G:
                    for b in range(firsts[g], firsts[g + 1]):
                        if sides[b] == "act":
                            if centre:
                                act.wait_ge(*K.at("centred", b + 1))
                            if b >= 4:
                                act.wait_ge(*K.at("squares_summed", b - 3))
                            square("act", b)
                if g >= 1:
                    j = g - 1
                    if j >= 4:
                        act.wait_ge(*K.at("roots_spread", j - 3))
                    act.wait_ge(*K.at("squares_summed", firsts[j + 1]))
                    nc.scalar.activation(root[:, j % 4], K.ps[:, sum_bank(j), 0:P], ACT.Sqrt, bias=groups[j]["eps"],
                                         scale=groups[j]["inv"]).then_inc(*K.inc("roots_done"))
            for i, (dst, _, _, _, bias) in enumerate(o for grp in groups for o in grp["out"]):
                if bias is not None:
                    act.wait_ge(*K.at("scaled", i + 1))
                    nc.scalar.activation(dst, dst, ACT.Identity, bias=bias)

        @block.vector
        def _(dve):
            if centre:
                for g, grp in enumerate(groups):
                    dve.wait_ge(*K.at("means_spread", g + 1))
                    for s in grp["src"]:
                        nc.vector.tensor_tensor(s, s, K.ps[0:s.shape[0], mean_bank[g], 0:s.shape[1]], ALU.add).then_inc(*K.inc("centred"))
            for b in range(len(blocks)):
                if sides[b] == "dve":
                    if b >= 4:
                        dve.wait_ge(*K.at("squares_summed", b - 3))
                    square("dve", b)
            for g in range(G + 1):
                if g < G:
                    dve.wait_ge(*K.at("roots_done", g + 1))
                    nc.vector.reciprocal(root[:, g % 4], root[:, g % 4]).then_inc(*K.inc("inverted"))
                if g >= 1:
                    j = g - 1
                    dve.wait_ge(*K.at("roots_spread", j + 1))
                    if centre and j == 0:
                        dve.wait_ge(*K.at("centred", firsts[G]))
                    for dst, src, cs, gain, _ in groups[j]["out"]:
                        r = K.ps[0:src.shape[0], spread_bank(j), cs]
                        if gain is None:
                            ins = nc.vector.tensor_tensor(dst, src, r, ALU.mult)
                        else:
                            ins = nc.vector.scalar_tensor_tensor(out=dst, in0=src, scalar=gain, in1=r, op0=ALU.mult, op1=ALU.mult)
                        ins.then_inc(*K.inc("scaled"))
    K.end_stage()


def attention_stage(K, units, work, passes, name="attention", also=()):
    nc, U = K.nc, len(units)
    nb = 3
    nt = 3 - passes
    E = work[:, 0:3072].rearrange("p (u s n) -> p u s n", u=nb, s=2)
    AT = work[:, 3072:4096].rearrange("p (u k q) -> p u k q", u=2, k=4)
    stat = K.small[:, 0:3 * 2 * nb].rearrange("p (u s c) -> p u s c", u=nb, s=2)

    def scores(i, s):
        return passes * (i % nb) + s

    def transposes(i):
        return passes * nb + i % nt

    def values(i):
        return passes * nb + nt + i % nt

    with K.block(name) as block:
        @block.sync
        def _(sp):
            K.start_moves(sp, also)
            K.end_moves(sp, also)

        @block.tensor
        def _(pe):
            for i in range(U + 3):
                if i < U:
                    u = units[i]
                    if i >= nb:
                        if u["bias"] is not None:
                            pe.wait_ge(*K.at("biased", i - nb + 1))
                        else:
                            pe.wait_ge(*K.at("exps_done", passes * (i - nb + 1)))
                    for s in range(passes):
                        last = nc.tensor.matmul(K.ps[:, scores(i, s), 0:u["k"].shape[-1]], u["q"][s], u["k"], start=True, stop=True)
                    last.then_inc(*K.inc("scores_done"))
                if 2 <= i <= U + 1:
                    j = i - 2
                    u = units[j]
                    pe.wait_ge(*K.at("probs_done", j + 1))
                    if j >= nt:
                        pe.wait_ge(*K.at("probsT_done", j - nt + 1))
                    for c in range(len(u["v"])):
                        last = nc.tensor.transpose(K.ps[:, transposes(j), c * P:(c + 1) * P], E[:, j % nb, 0, c * P:(c + 1) * P], K.ident)
                    last.then_inc(*K.inc("transposed"))
                if i >= 3:
                    j = i - 3
                    u = units[j]
                    pe.wait_ge(*K.at("probsT_done", j + 1))
                    if j >= nt:
                        pe.wait_ge(*K.at("out_kept", j - nt + 1))
                    for c, v in enumerate(u["v"]):
                        last = nc.tensor.matmul(K.ps[u["rows"][0]:u["rows"][1], values(j), 0:P], v, AT[:, j % 2, c, :],
                                                start=c == 0, stop=c == len(u["v"]) - 1)
                    last.then_inc(*K.inc("values_done"))

        @block.scalar
        def _(act):
            for i in range(U + 2):
                if i < U:
                    u, b = units[i], i % nb
                    n = u["k"].shape[-1]
                    act.wait_ge(*K.at("max_done", i + 1))
                    if i >= nb:
                        act.wait_ge(*K.at("transposed", i - nb + 1))
                    for s in range(passes):
                        src = E[:, b, 1, 0:n] if u["bias"] is not None else K.ps[:, scores(i, s), 0:n]
                        nc.scalar.activation(E[:, b, s, 0:n], src, ACT.Exp, bias=stat[:, b, s, 0:1],
                                             accum_out=stat[:, b, s, 1:2]).then_inc(*K.inc("exps_done"))
                if i >= 2:
                    j = i - 2
                    u = units[j]
                    act.wait_ge(*K.at("transposed", j + 1))
                    if j >= 2:
                        act.wait_ge(*K.at("values_done", j - 1))
                    n = P * len(u["v"])
                    nc.scalar.activation(AT[:, j % 2, 0:len(u["v"]), :].rearrange("p k q -> p (k q)"), K.ps[:, transposes(j), 0:n],
                                         ACT.Copy).then_inc(*K.inc("probsT_done"))

        @block.vector
        def _(dve):
            for i in range(U + 4):
                if i < U:
                    u, b = units[i], i % nb
                    n = u["k"].shape[-1]
                    dve.wait_ge(*K.at("scores_done", i + 1))
                    if i >= nb:
                        dve.wait_ge(*K.at("exps_done", passes * (i - nb + 1)))
                    if u["bias"] is not None:
                        if n > T:
                            nc.vector.tensor_copy(E[:, b, 1, T:n], K.ps[:, scores(i, 0), T:n])
                        K.step(dve, nc.vector.tensor_tensor(E[:, b, 1, 0:T], K.ps[:, scores(i, 0), 0:T], u["bias"], ALU.add), "biased")
                    for s in range(passes):
                        src = E[:, b, 1, 0:n] if u["bias"] is not None else K.ps[:, scores(i, s), 0:n]
                        last = nc.vector.tensor_reduce(stat[:, b, s, 0:1], src, AX, ALU.max, negate=True)
                    last.then_inc(*K.inc("max_done"))
                if i >= 4:
                    j = i - 4
                    u = units[j]
                    dve.wait_ge(*K.at("values_done", j + 1))
                    nc.vector.tensor_copy(u["out"], K.ps[u["rows"][0]:u["rows"][1], values(j), 0:P]).then_inc(*K.inc("out_kept"))
                if 1 <= i <= U:
                    j = i - 1
                    u, b = units[j], j % nb
                    n = u["k"].shape[-1]
                    dve.wait_ge(*K.at("exps_done", passes * i))
                    K.step(dve, nc.vector.reciprocal(stat[:, b, 0:passes, 2:3], stat[:, b, 0:passes, 1:2]), "dve_step")
                    for s in range(passes):
                        if u["weight"][s] is not None:
                            K.step(dve, nc.vector.tensor_tensor(stat[:, b, s, 2:3], stat[:, b, s, 2:3], u["weight"][s], ALU.mult), "dve_step")
                    probs = E[:, b, 0, 0:n]
                    last = nc.vector.tensor_scalar(probs, probs, stat[:, b, 0, 2:3], None, ALU.mult)
                    for s in range(1, passes):
                        K.step(dve, last, "dve_step")
                        last = nc.vector.scalar_tensor_tensor(out=probs, in0=E[:, b, s, 0:n], scalar=stat[:, b, s, 2:3],
                                                              in1=probs, op0=ALU.mult, op1=ALU.add)
                    last.then_inc(*K.inc("probs_done"))
    K.end_stage()


def gated_add(K, gate, fb, n_seg):
    nc = K.nc

    def evac(side, ps, dve):
        for s in range(n_seg):
            last = nc.vector.scalar_tensor_tensor(out=K.XT[:, fb, SEGS[s]], in0=ps[:, SEGS[s]], scalar=mod(K, gate, s, fb),
                                                  in1=K.XT[:, fb, SEGS[s]], op0=ALU.mult, op1=ALU.add)
        return last
    return evac


def out_proj_stage(K, gate, n_seg):
    n = n_seg * T
    jobs = [feature_job(K, fb // 4, fb % 4 * P, P, K.HT[:, :, 0:n], None, evac=gated_add(K, gate, fb, n_seg), only="dve")
            for fb in range(KD)]
    gemm_stage(K, 2, jobs, "out_projection")


def alpha_stage(K, n):
    nc = K.nc
    with K.block("alpha") as block:
        @block.scalar
        def _(act):
            for k in range(4):
                nc.scalar.mul(K.XT[:, k, 0:n], K.XT[:, k, 0:n], ALPHA)

        @block.vector
        def _(dve):
            for k in range(4, KD):
                nc.vector.tensor_scalar(K.XT[:, k, 0:n], K.XT[:, k, 0:n], ALPHA, None, ALU.mult)
    K.end_stage()


def layer_norm_stage(K, n, g, b):
    src = [K.XT[:, k, 0:n] for k in range(KD)]
    norm_stage(K, [dict(src=src, ones=K.ones, inv=1.0 / D, eps=K.eps["ln"],
                        out=[(s, s, slice(0, n), K.col(g, k), K.col(b, k)) for k, s in enumerate(src)])],
               K.arena, centre=True)


def rope_stage(K, blocks, swap, cos, sin, tmp):
    nc, B, n = K.nc, len(blocks), T
    p = blocks[0].shape[0]
    with K.block("rope") as block:
        @block.tensor
        def _(pe):
            for i, q in enumerate(blocks):
                if i >= NBANK:
                    pe.wait_ge(*K.at("swapped_times_sin", i - NBANK + 1))
                nc.tensor.matmul(K.ps[0:p, i % NBANK, 0:n], swap, q, start=True, stop=True).then_inc(*K.inc("swapped"))

        @block.gpsimd
        def _(pool):
            for i, q in enumerate(blocks):
                pool.wait_ge(*K.at("swapped", i + 1))
                nc.gpsimd.tensor_tensor(q, q, cos, ALU.mult).then_inc(*K.inc("times_cos"))

        @block.vector
        def _(dve):
            for i, q in enumerate(blocks):
                t = tmp[0:p, i % 2 * n:(i % 2 + 1) * n]
                dve.wait_ge(*K.at("swapped", i + 1))
                K.step(dve, nc.vector.tensor_tensor(t, K.ps[0:p, i % NBANK, 0:n], sin, ALU.mult), "swapped_times_sin")
                dve.wait_ge(*K.at("times_cos", i + 1))
                K.step(dve, nc.vector.tensor_tensor(q, q, t, ALU.add), "dve_step")
    K.end_stage()


def prologue(K):
    nc, d = K.nc, K.dram
    lam_in = K.arena[:, 0:2 * 256].rearrange("p (l a n) -> p l a n", l=2, a=4)
    lam_prod = K.arena[:, 512:768].rearrange("p (l a n) -> p (l a) n", l=2, a=2)
    lam_sum = K.small[:, 24:28]
    lam_exp = K.small[:, 28:32].rearrange("p (l a) -> p l a", l=2)
    K.neg_lam = [K.small[:, 32:33], K.small[:, 33:34]]
    K.eps = {n: K.small[:, 34 + i:35 + i] for i, n in enumerate(("ln", "rms", "gn", "kk", "zero"))}
    K.subln = [K.small[:, 40:41], K.small[:, 41:42]]
    K.q_gain, K.na_gain = K.small[:, 42:43], K.small[:, 43:44]
    K.zero_wait = K.small[:, 39:40]
    sig = K.arena[:, 1024:1024 + 32].rearrange("p (b v k) -> p b v k", b=2, v=2)
    lam_init = [0.8 - 0.6 * math.exp(-0.3 * l) for l in range(DEPTH)]
    with K.block("prologue") as block:
        @block.sync
        def _(sp):
            sp.dma_start(K.cols[:, :], d["cols"]).then_inc(*K.inc("constants_landed", 16))
            sp.dma_start(K.base_consts[:, :], d["consts"][:, 0:384]).then_inc(*K.inc("constants_landed", 16))
            sp.dma_start(K.arena[:, 0:512], d["diff_lambda"].partition_broadcast(P)).then_inc(*K.inc("constants_landed", 16))
            for _ in range(RING):
                K.load_next(sp)
            sp.wait_ge(*K.at("constants_landed", 3 * 16))

        @block.gpsimd
        def _(pool):
            nc.gpsimd.memset(K.sil[:, :, :, :], 0.0).then_inc(*K.inc("cleared"))
            for n, v in (("ln", 1e-5), ("rms", 1e-6), ("gn", 64e-5), ("kk", 1e-12), ("zero", 0.0)):
                nc.gpsimd.memset(K.eps[n], v)

        @block.scalar
        def _(act):
            act.wait_ge(*K.at("constants_landed", 3 * 16))
            act.wait_ge(*K.at("cleared", 1))
            for b in range(2):
                for v in range(2):
                    nc.scalar.activation(K.sil[:, b, :, v], K.col("c", 8 * (2 * b + v), 8), ACT.Silu)
            act.wait_ge(*K.at("lam_summed", 1))
            nc.scalar.activation(lam_exp, lam_sum.rearrange("p (l a) -> p l a", l=2), ACT.Exp).then_inc(*K.inc("lam_exps"))

        @block.vector
        def _(dve):
            dve.wait_ge(*K.at("constants_landed", 3 * 16))
            for l in range(DEPTH):
                for a in range(2):
                    last = nc.vector.tensor_tensor(lam_prod[:, 2 * l + a, :], lam_in[:, l, 2 * a, :], lam_in[:, l, 2 * a + 1, :], ALU.mult)
            K.step(dve, last, "dve_step")
            nc.vector.tensor_reduce(lam_sum, lam_prod, AX, ALU.add).then_inc(*K.inc("lam_summed"))
            for l in range(DEPTH):
                nc.vector.tensor_scalar(K.subln[l], K.col(f"subln{l}"), 1.0 - lam_init[l], None, ALU.mult)
            nc.vector.tensor_scalar(K.q_gain, K.col("q_g"), 96.0 ** -0.5, None, ALU.mult)
            nc.vector.tensor_scalar(K.na_gain, K.col("na_q"), 64.0 ** -0.5, None, ALU.mult)
            dve.wait_ge(*K.at("lam_exps", 1))
            for l in range(DEPTH):
                K.step(dve, nc.vector.tensor_tensor(K.neg_lam[l], lam_exp[:, l, 1:2], lam_exp[:, l, 0:1], ALU.subtract), "dve_step")
                nc.vector.tensor_scalar(K.neg_lam[l], K.neg_lam[l], -lam_init[l], None, ALU.add)
    K.end_stage()


def first_layer(K, l):
    nc, A, HT = K.nc, K.arena, K.HT
    n_seg = 1 if l == DEPTH - 1 else 2
    n = n_seg * T
    q = A[:, 0:2048].rearrange("p (h t) -> p h t", h=4)
    k = A[:, 2048:4096].rearrange("p (h t) -> p h t", h=4)
    v = A[:, 4096:6144].rearrange("p (t e) -> p t e", t=4)
    cv = A[:, 6144:9216].rearrange("p (b t) -> p b t", b=6)
    f = A[:, 9216:10240].rearrange("p (t m) -> p t m", t=4)
    q2 = A[:, 10240:14336].rearrange("p (s h t) -> p s h t", s=2, h=4)
    tmp = A[:, 14336:16384]
    table = A[:, 16512:18432]

    tokens = [(K.XT[:, :, seg], K.dram[name].rearrange("(k p) t -> p k t", p=P)) for name, seg in (("x", X), ("ctx", C))]
    mod_stage(K, K.sil[:, 0], K.col(f"b_mod{l}", 0, 48), (1, 4),
              also=K.constants(["swap1", "cos1", "sin1", "cn", "sn", "cm", "sm"], table) + (tokens if l == 0 else []))
    modulate_stage(K, 0, 1, 2)

    jobs = [feature_job(K, 0, h * P, P, HT[:, :, 0:n], q[:, h, 0:n], scale=0.125) for h in range(4)]
    jobs += [feature_job(K, 1, h * P, P, HT, k[:, h, :]) for h in range(4)]
    jobs += [token_job(K, 2, lambda w, i: w[:, i, :], HT, t, v[:, t, :]) for t in range(4)]
    jobs += [feature_job(K, 3, b * P, P, HT[:, :, 0:n], cv[:, b, 0:n]) for b in range(4)]
    jobs += [feature_job(K, 4, b * P, P, HT[:, :, 0:n], cv[:, 4 + b, 0:n]) for b in range(2)]
    jobs += [token_job(K, 4, lambda w, i: w[:, i, 256:512], HT, t, f[:, t, :]) for t in range(2 * n_seg)]
    gemm_stage(K, 5, jobs, "in_projection")

    rope_stage(K, [b[:, h, X] for b in (q, k) for h in range(4)], K.const["swap1"], K.const["cos1"], K.const["sin1"], tmp)
    conv_fourier_stage(K, l, n_seg, cv, f, q, q2, tmp)

    units = [dict(q=[q2[:, s, h, c * P:(c + 1) * P] for s in range(2)], k=k[:, h, 0:TT] if c < 2 else k[:, h, C],
                  v=[v[:, t, h * P:(h + 1) * P] for t in (range(4) if c < 2 else range(2, 4))], bias=None, rows=(0, P),
                  out=HT[:, h, c * P:(c + 1) * P], weight=[None, K.neg_lam[l]])
             for h in range(4) for c in range(2 * n_seg)]
    attention_stage(K, units, A[:, 6144:10240], 2, "differential_attention")
    norm_stage(K, [dict(src=[HT[:, h, 0:n]], ones=K.ones, inv=1.0 / P, eps=K.eps["ln"],
                        out=[(HT[:, h, 0:n], HT[:, h, 0:n], slice(0, n), K.subln[l], None)]) for h in range(4)], A[:, 0:3072])
    alpha_stage(K, n)
    out_proj_stage(K, 2, n_seg)
    layer_norm_stage(K, n, f"ln1_g{l}", f"ln1_b{l}")
    modulate_stage(K, 3, 4, n_seg)

    hidden = A[:, 0:16384].rearrange("p (b t) -> p b t", b=32)
    jobs = [feature_job(K, fb // 4, fb % 4 * P, P, HT[:, :, 0:n], None, evac=squared_relu(K, hidden[:, fb, 0:n])) for fb in range(32)]
    gemm_stage(K, 8, jobs, "mlp_up")
    alpha_stage(K, n)
    jobs = []
    for fb in range(KD):
        pieces = [fb // 4 * 4 + r for r in range(4)]
        c0 = fb % 4 * P
        jobs.append(dict(pieces=pieces, rows=(0, P), n=n, only="dve", evac=gated_add(K, 5, fb, n_seg),
                         mm=lambda w, c0=c0: [(w[r][:, i, c0:c0 + P], hidden[:, 8 * r + i, 0:n]) for r in range(4) for i in range(KD)]))
    gemm_stage(K, 8, jobs, "mlp_down")
    layer_norm_stage(K, n, f"ln2_g{l}", f"ln2_b{l}")


def squared_relu(K, out):
    nc = K.nc

    def evac(side, ps, eng):
        if side == "act":
            K.step(eng, nc.scalar.activation(out, ps, ACT.Relu), "act_step")
            return nc.scalar.activation(out, out, ACT.Square)
        K.step(eng, nc.vector.tensor_scalar(out, ps, 0.0, None, ALU.max), "dve_step")
        return nc.vector.tensor_tensor(out, out, out, ALU.mult)
    return evac


def conv_fourier_stage(K, l, n_seg, cv, f, q, q2, tmp):
    nc, HT = K.nc, K.HT
    n = n_seg * T
    cn = K.const["cn"].rearrange("p (t k) -> p t k", t=2)
    sn = K.const["sn"].rearrange("p (t k) -> p t k", t=2)
    first = tmp.rearrange("p (b t) -> p b t", b=4)
    with K.block("conv_fourier") as block:
        @block.tensor
        def _(pe):
            for b in range(4):
                for s in range(n_seg):
                    for t in range(2):
                        last = nc.tensor.matmul(K.ps[:, b, SEGS[s]], f[:, 2 * s + t, b % 2 * P:(b % 2 + 1) * P],
                                                (cn, sn)[b // 2][:, t, :], start=t == 0, stop=t == 1)
                last.then_inc(*K.inc("tokens_transformed"))
            for b in range(2):
                pe.wait_ge(*K.at("transform_kept", 4))
                nc.tensor.matmul(K.ps[:, 4 + b, 0:n], K.const["cm"], first[:, b, 0:n], start=True, stop=False)
                nc.tensor.matmul(K.ps[:, 4 + b, 0:n], K.const["sm"], first[:, 2 + b, 0:n], start=False, stop=True)\
                    .then_inc(*K.inc("features_transformed"))

        @block.scalar
        def _(act):
            for b in range(4):
                act.wait_ge(*K.at("tokens_transformed", b + 1))
                nc.scalar.activation(first[:, b, 0:n], K.ps[:, b, 0:n], ACT.Copy).then_inc(*K.inc("transform_kept"))
            for b in range(2):
                act.wait_ge(*K.at("features_transformed", b + 1))
                nc.scalar.activation(HT[:, 6 + b, 0:n], K.ps[:, 4 + b, 0:n], ACT.Copy)

        @block.gpsimd
        def _(pool):
            nc.gpsimd.memset(q2[64:128, 0], 0.0)
            nc.gpsimd.memset(q2[0:64, 1], 0.0)
            for s in range(2):
                nc.gpsimd.tensor_copy(q2[64 * s:64 * s + 64, s, :, 0:n], q[64 * s:64 * s + 64, :, 0:n])

        @block.vector
        def _(dve):
            for b in range(2):
                w = [K.col(f"conv_w{l}", 2 * i + b) for i in range(3)]
                z, gate, gc, y = cv[:, b, 0:n], cv[:, 2 + b, 0:n], cv[:, 4 + b, 0:n], HT[:, 4 + b, 0:n]
                K.step(dve, nc.vector.tensor_tensor(z, z, gc, ALU.mult), "dve_step")
                K.step(dve, nc.vector.tensor_scalar(y, z, w[1], K.col(f"conv_b{l}", b), ALU.mult, ALU.add), "dve_step")
                zs, ys = (a.rearrange("p (s t) -> p s t", s=n_seg) for a in (z, y))
                for tap, dst, src in ((w[0], slice(1, T), slice(0, T - 1)), (w[2], slice(0, T - 1), slice(1, T))):
                    K.step(dve, nc.vector.scalar_tensor_tensor(out=ys[:, :, dst], in0=zs[:, :, src], scalar=tap, in1=ys[:, :, dst],
                                                               op0=ALU.mult, op1=ALU.add), "dve_step")
                K.step(dve, nc.vector.tensor_tensor(y, y, gate, ALU.mult), "dve_step")
    K.end_stage()


def plan_even(K):
    K.plan("ada_w", 0)
    for name in ("ev_w_in", "w_uq", "w_ukv", "ev_w_out", "router"):
        K.plan(name, 0)
    plan_experts(K, 2)


def scaled_norm_stage(K, l, which, n_seg, also=()):
    nc = K.nc
    gain = K.col(f"norm{1 if which == 0 else 2}_g{l}", 0, KD)
    with K.block("gain") as block:
        @block.vector
        def _(dve):
            for s in range(n_seg):
                nc.vector.tensor_tensor(K.gain[:, s, :], K.modcol[:, s, 8 * (which + 1):8 * (which + 2)], gain, ALU.mult)
    K.end_stage()
    n = n_seg * T
    norm_stage(K, [dict(src=[K.XT[:, k, 0:n] for k in range(KD)], ones=K.ones, inv=1.0 / D, eps=K.eps["rms"],
                        out=[(K.HT[:, k, SEGS[s]], K.XT[:, k, SEGS[s]], SEGS[s], K.gain[:, s, k:k + 1], mod(K, which, s, k))
                             for k in range(KD) for s in range(n_seg)])], K.arena, also=also)


def even_layer(K):
    nc, A, HT = K.nc, K.arena, K.HT
    q = A[:, 0:4096].rearrange("p (h t) -> p h t", h=8)
    k = A[:, 4096:8192].rearrange("p (h t) -> p h t", h=8)
    v = A[:, 8192:10240].rearrange("p (t e) -> p t e", t=4)
    pad = A[:, 10240:12528].rearrange("p (b s t) -> p b s t", b=4, s=2)
    cq = A[:, 12528:14064].rearrange("p (b t) -> p b t", b=3)
    ckv = A[:, 14064:15088].rearrange("p (b t) -> p b t", b=2)
    kr = A[64:96, 15088:15600]
    table, tmp = A[:, 15600:16240], A[:, 16240:16752]
    a, sg = (A[:, i:i + 2048].rearrange("p (b t) -> p b t", b=4) for i in (0, 2048))

    mod_stage(K, K.sil[:, 1], K.col("ada_b0", 0, 48), (1, 4),
              also=K.constants(["swap2", "cos2", "sin2"], table) + [(K.XT[:, :, C], K.dram["ctx_2"].rearrange("(k p) t -> p k t", p=P))])
    scaled_norm_stage(K, 0, 0, 2)

    jobs = [feature_job(K, 0, b * P, P, HT, cq[:, b, :]) for b in range(3)]
    jobs += [feature_job(K, 1, b * P, P, HT, ckv[:, b, :]) for b in range(2)]
    jobs += [feature_job(K, 1, 256, 32, HT, kr, p0=64)]
    jobs += [feature_job(K, 2, b * P, P, HT, a[:, b, :]) for b in range(4)]
    jobs += [feature_job(K, 3, b * P, P, HT, None, only="act",
                         evac=lambda side, ps, eng, b=b: nc.scalar.activation(sg[:, b, :], ps, ACT.Sigmoid)) for b in range(4)]
    gemm_stage(K, 4, jobs, "even_in_projection")
    gate_stage(K, a, sg, pad)
    norm_stage(K, [dict(src=[c[:, b, :] for b in range(m)], ones=K.ones, inv=1.0 / (m * P), eps=K.eps["rms"],
                        out=[(c[:, b, :], c[:, b, :], slice(0, TT), K.col(gain, b), None) for b in range(m)])
                   for c, m, gain in ((cq, 3, "q_norm"), (ckv, 2, "kv_norm"))], A[:, 0:3072])

    jobs = [feature_job(K, 0, h * 96, 96, cq, q[0:96, h, :]) for h in range(8)]
    jobs += [feature_job(K, 1, h * P, 64, ckv, k[0:64, h, :]) for h in range(8)]
    jobs += [token_job(K, 1, lambda w, i: w[:, i, :].rearrange("p (h e) -> p h e", e=P)[:, :, 64:P], ckv, t, v[:, t, :]) for t in range(4)]
    gemm_stage(K, 2, jobs, "mla_up_projection")
    with K.block("shared_rotary_key") as block:
        @block.scalar
        def _(act):
            for h in range(0, 8, 2):
                nc.scalar.activation(k[64:96, h, :], kr, ACT.Copy)

        @block.vector
        def _(dve):
            for h in range(1, 8, 2):
                nc.vector.tensor_copy(k[64:96, h, :], kr)
    K.end_stage()
    norm_stage(K, [dict(src=[b[0:96, h, :]], ones=K.ones[0:96], inv=1.0 / 96, eps=K.eps["rms"],
                        out=[(b[0:96, h, :], b[0:96, h, :], slice(0, TT), gain[0:96], None)])
                   for b, gain in ((q, K.q_gain), (k, K.col("k_g"))) for h in range(8)], A[:, 12528:15600])
    rope_stage(K, [b[0:96, h, X] for b in (q, k) for h in range(8)], K.const["swap2"][0:96, 0:96],
               K.const["cos2"][0:96], K.const["sin2"][0:96], tmp)
    depthwise_stage(K, pad)
    conv = [HT[:, 4 + b, :] for b in range(4)]
    norm_stage(K, [dict(src=conv, ones=K.ones, inv=1.0 / 512, eps=K.eps["rms"],
                        out=[(c, c, slice(0, TT), K.col("cln_g", b), K.col("cln_b", b)) for b, c in enumerate(conv)])],
               A[:, 12528:15600], centre=True)
    with K.block("conv_silu") as block:
        @block.scalar
        def _(act):
            nc.scalar.activation(HT[:, 4:8, :], HT[:, 4:8, :], ACT.Silu)
    K.end_stage()

    units = [dict(q=[q[0:96, h, c * P:(c + 1) * P]], k=k[0:96, h, 0:TT] if c < 2 else k[0:96, h, C],
                  v=[v[:, t, h * 64:(h + 1) * 64] for t in (range(4) if c < 2 else range(2, 4))], bias=None,
                  rows=(h % 2 * 64, h % 2 * 64 + 64), out=HT[h % 2 * 64:h % 2 * 64 + 64, h // 2, c * P:(c + 1) * P], weight=[None])
             for h in range(8) for c in range(4)]
    attention_stage(K, units, A[:, 14336:18432], 1, "mla_attention")
    out_proj_stage(K, 2, 2)
    experts(K, 0, 2)


def gate_stage(K, a, sg, pad):
    nc = K.nc
    with K.block("gate") as block:
        @block.gpsimd
        def _(pool):
            nc.gpsimd.memset(pad[:, :, :, 0:15], 0.0)
            nc.gpsimd.memset(pad[:, :, :, 15 + T:30 + T], 0.0)

        @block.vector
        def _(dve):
            for b in range(4):
                nc.vector.tensor_tensor(pad[:, b, :, 15:15 + T], a[:, b, :].rearrange("p (s t) -> p s t", s=2),
                                        sg[:, b, :].rearrange("p (s t) -> p s t", s=2), ALU.mult)
    K.end_stage()


def depthwise_stage(K, pad):
    nc, taps = K.nc, 31
    y = [K.HT[:, 4 + b, :].rearrange("p (s t) -> p s t", s=2) for b in range(4)]
    with K.block("depthwise_conv") as block:
        @block.vector
        def _(dve):
            for j in range(taps):
                for b in range(4):
                    src, w = pad[:, b, :, j:j + T], K.col("dw_w", 4 * j + b)
                    if j == 0:
                        ins = nc.vector.tensor_scalar(y[b], src, w, K.col("dw_b", b), ALU.mult, ALU.add)
                    else:
                        dve.wait_ge(*K.at("tap_added", 4 * (j - 1) + b + 1))
                        ins = nc.vector.scalar_tensor_tensor(out=y[b], in0=src, scalar=w, in1=y[b], op0=ALU.mult, op1=ALU.add)
                    ins.then_inc(*K.inc("tap_added"))
    K.end_stage()


def expert_pieces(group):
    return [(m, e, h) for e in range(group) for m in ("moe_w1", "moe_w3") for h in range(2)] + \
           [("moe_w2", e, h) for h in range(2) for e in range(group)]


def plan_experts(K, group):
    l = 0 if group == 2 else 1
    for g in range(NE // group):
        for m, e, h in expert_pieces(group):
            K.stream.append((K.dram[m][l, g * group + e, h].rearrange("p n -> (p n)"), KD, 512))


def experts(K, l, n_seg):
    nc, A, HT = K.nc, K.arena, K.HT
    n, nt, M = n_seg * T, 2 * n_seg, CAP * n_seg
    group = P // M
    NG = NE // group
    xs_all = A[:, 0:NE * KD * M].rearrange("p (e k s) -> p e k s", e=NE, k=KD)
    ys = A[:, 0:NG * D].rearrange("p (g d) -> p g d", g=NG)
    h_tok = A[:, 8192:8192 + nt * D].rearrange("p (t d) -> p t d", t=nt)
    pick = A[:, 12288:12288 + nt * NE * M].rearrange("p (t e s) -> p t e s", t=nt, e=NE)
    pt = HT[:, :, :].rearrange("p k t -> p (k t)")[:, 0:NG * n].rearrange("p (g t) -> p g t", g=NG)

    B = A[:, 16384:18432]
    scaled_norm_stage(K, l, 3, n_seg, also=K.constants(["tri", "iota"], B[:, 0:192]))
    tri, iota = B[:, 0:128], B[:, 128:192]
    logit = B[:, 192:256].rearrange("p (t e) -> p t e", t=4)
    aff = B[:, 256:512].rearrange("p (t s) -> p t s", t=2)
    affT, left = B[0:32, 512:768], B[0:32, 768:1024]
    mask = B[:, 1024:1280]
    maskT = B[:, 1280:1344].rearrange("p (t s) -> p t s", t=2)
    place = B[:, 1344:1408].rearrange("p (t s) -> p t s", t=2)
    top = B[0:32, 1408:1416]
    peak = B[:, 1416:1420]
    router_stage(K, B[:, 1424:1552], logit, nt)
    R = 16 * n_seg
    tok = lambda buf, t: buf[:, t % 2, 16 * (t // 2):16 * (t // 2) + 16]

    with K.block("routing") as block:
        @block.gpsimd
        def _(pool):
            nc.gpsimd.memset(aff, 0.0).then_inc(*K.inc("cleared"))
            nc.gpsimd.memset(mask, 0.0).then_inc(*K.inc("cleared"))
            nc.gpsimd.memset(pick, 0.0).then_inc(*K.inc("cleared"))

        @block.tensor
        def _(pe):
            for t in range(nt):
                for half in range(2):
                    for i in range(4):
                        last = nc.tensor.transpose(K.ps[:, (2 * t + half) % 4, i * P:(i + 1) * P],
                                                   HT[:, 4 * half + i, t * P:(t + 1) * P], K.ident)
                    last.then_inc(*K.inc("h_transposed"))
                    if 2 * t + half + 1 < 2 * nt and 2 * t + half >= 3:
                        pe.wait_ge(*K.at("h_kept", 2 * t + half - 2))
            pe.wait_ge(*K.at("affinities", 1))
            for t in range(2):
                last = nc.tensor.transpose(K.ps[:, 4, t * P:(t + 1) * P], aff[:, t, :], K.ident)
            last.then_inc(*K.inc("affinities_turned"))
            pe.wait_ge(*K.at("masked", 1))
            for t in range(2):
                last = nc.tensor.transpose(K.ps[:, 5, t * P:(t + 1) * P], mask[:, t * P:(t + 1) * P], K.ident)
            last.then_inc(*K.inc("mask_turned"))
            pe.wait_ge(*K.at("mask_kept", 1))
            nc.tensor.matmul(K.ps[:, 6, 0:32], tri, maskT[:, 0, :], start=True, stop=True)
            nc.tensor.matmul(K.ps[:, 7, 0:32], K.ones, maskT[:, 0, :], start=True, stop=False)
            nc.tensor.matmul(K.ps[:, 7, 0:32], tri, maskT[:, 1, :], start=False, stop=True).then_inc(*K.inc("counted"))

        @block.scalar
        def _(act):
            act.wait_ge(*K.at("shifted", 1))
            nc.scalar.activation(logit[:, 0:nt, :], logit[:, 0:nt, :], ACT.Exp).then_inc(*K.inc("logit_exps"))
            for i in range(2 * nt):
                act.wait_ge(*K.at("h_transposed", i + 1))
                nc.scalar.activation(h_tok[:, i // 2, i % 2 * 512:(i % 2 + 1) * 512], K.ps[:, i % 4, :], ACT.Copy)\
                    .then_inc(*K.inc("h_kept"))

        @block.vector
        def _(dve):
            lg = logit[:, 0:nt, :]
            pk = peak[:, 0:nt]
            bc = pk.unsqueeze(2).broadcast_to([P, nt, NE])
            K.step(dve, nc.vector.tensor_reduce(pk, lg, AX, ALU.max), "dve_step")
            nc.vector.tensor_tensor(lg, lg, bc, ALU.subtract).then_inc(*K.inc("shifted"))
            dve.wait_ge(*K.at("logit_exps", 1))
            K.step(dve, nc.vector.tensor_reduce(pk, lg, AX, ALU.add), "dve_step")
            K.step(dve, nc.vector.reciprocal(pk, pk), "dve_step")
            dve.wait_ge(*K.at("cleared", 3))
            for t in range(nt):
                last = nc.vector.tensor_scalar(tok(aff, t), logit[:, t, :], pk[:, t:t + 1], None, ALU.mult)
            last.then_inc(*K.inc("affinities"))
            dve.wait_ge(*K.at("affinities_turned", 1))
            K.step(dve, nc.vector.tensor_copy(left[0:R], K.ps[0:R, 4, 0:T]), "dve_step")
            for _ in range(CAP // 8):
                K.step(dve, nc.vector.max(top[0:R], left[0:R]), "dve_step")
                K.step(dve, nc.vector.match_replace(left[0:R], top[0:R], left[0:R], -1.0), "dve_step")
            nc.vector.tensor_scalar(mask[0:R], left[0:R], 0.0, None, ALU.is_lt).then_inc(*K.inc("masked"))
            dve.wait_ge(*K.at("mask_turned", 1))
            for t in range(2):
                last = nc.vector.tensor_copy(maskT[:, t, :], K.ps[:, 5, t * P:t * P + 32])
            last.then_inc(*K.inc("mask_kept"))
            dve.wait_ge(*K.at("counted", 1))
            dve.wait_ge(*K.at("mask_kept", 1))
            for t in range(2):
                last = nc.vector.tensor_tensor(place[:, t, :], K.ps[:, 6 + t, 0:32], maskT[:, t, :], ALU.mult)
            K.step(dve, last, "dve_step")
            for t in range(nt):
                at = CAP * (t // 2)
                nc.vector.tensor_tensor(pick[:, t, :, at:at + CAP], tok(place, t).unsqueeze(2).broadcast_to([P, NE, CAP]),
                                        iota[:, 0:CAP].unsqueeze(1).broadcast_to([P, NE, CAP]), ALU.is_equal)
    K.end_stage()

    with K.block("gather") as block:
        @block.tensor
        def _(pe):
            for i in range(n_seg * KD):
                s, k = divmod(i, KD)
                if i >= 4:
                    pe.wait_ge(*K.at("gathered_kept", i - 3))
                for t in range(2):
                    last = nc.tensor.matmul(K.ps[:, i % 4, :], h_tok[:, 2 * s + t, k * P:(k + 1) * P],
                                            pick[:, 2 * s + t, :, CAP * s:CAP * s + CAP], start=t == 0, stop=t == 1)
                last.then_inc(*K.inc("gathered"))
            for g in range(NG):
                pe.wait_ge(*K.at("weighted", 1))
                if g >= 4:
                    pe.wait_ge(*K.at("scatter_kept", g - 3))
                for t in range(nt):
                    last = nc.tensor.transpose(K.ps[:, 4 + g % 4, t * P:(t + 1) * P],
                                               pick[:, t, g * group:(g + 1) * group, :].rearrange("p e s -> p (e s)"), K.ident)
                last.then_inc(*K.inc("scatter_turned"))

        @block.scalar
        def _(act):
            for i in range(n_seg * KD):
                s, k = divmod(i, KD)
                act.wait_ge(*K.at("gathered", i + 1))
                nc.scalar.activation(xs_all[:, :, k, CAP * s:CAP * s + CAP], K.ps[:, i % 4, :].rearrange("p (e s) -> p e s", e=NE),
                                     ACT.Copy).then_inc(*K.inc("gathered_kept"))

        @block.vector
        def _(dve):
            dve.wait_ge(*K.at("gathered", n_seg * KD))
            for t in range(nt):
                at = CAP * (t // 2)
                w = pick[:, t, :, at:at + CAP]
                last = nc.vector.tensor_tensor(w, w, tok(aff, t).unsqueeze(2).broadcast_to([P, NE, CAP]), ALU.mult)
            last.then_inc(*K.inc("weighted"))
            for g in range(NG):
                dve.wait_ge(*K.at("scatter_turned", g + 1))
                nc.vector.tensor_copy(pt[:, g, :], K.ps[:, 4 + g % 4, 0:n]).then_inc(*K.inc("scatter_kept"))
    K.end_stage()
    expert_loop_stage(K, l, group, M, xs_all, ys)

    with K.block("scatter") as block:
        @block.tensor
        def _(pe):
            for k in range(KD):
                for g in range(NG):
                    last = nc.tensor.matmul(K.ps[:, k, 0:n], ys[:, g, k * P:(k + 1) * P], pt[:, g, :], start=g == 0, stop=g == NG - 1)
                last.then_inc(*K.inc("scattered"))

        @block.vector
        def _(dve):
            for k in range(KD):
                dve.wait_ge(*K.at("scattered", k + 1))
                gated_add(K, 5, k, n_seg)("dve", K.ps[:, k, 0:n], dve)
    K.end_stage()


def router_stage(K, rows, logit, nt):
    nc, first = K.nc, K.cursor
    with K.block("router") as block:
        @block.sync
        def _(sp):
            sp.wait_ge(*K.at("logits_done", 1))
            K.load_next(sp)

        @block.tensor
        def _(pe):
            pe.wait_ge(*K.landed(first))
            w = K.slot(first)
            for k in range(KD):
                for t in range(nt):
                    last = nc.tensor.matmul(K.ps[32 * t:32 * t + NE, 0, 0:P], w[:, k, :], K.HT[:, k, t * P:(t + 1) * P],
                                            start=k == 0, stop=k == KD - 1)
            last.then_inc(*K.inc("logits_done"))
            pe.wait_ge(*K.at("logits_kept", nt))
            nc.tensor.transpose(K.ps[:, 1, 0:P], rows, K.ident).then_inc(*K.inc("logits_turned"))

        @block.vector
        def _(dve):
            K.step(dve, nc.vector.memset(rows, 0.0), "dve_step")
            dve.wait_ge(*K.at("logits_done", 1))
            for t in range(nt):
                nc.vector.tensor_copy(rows[32 * t:32 * t + NE], K.ps[32 * t:32 * t + NE, 0, 0:P]).then_inc(*K.inc("logits_kept"))
            dve.wait_ge(*K.at("logits_turned", 1))
            nc.vector.tensor_copy(logit[:, 0:nt, :], K.ps[:, 1, 0:P].rearrange("p (t e) -> p t e", e=32)[:, 0:nt, 0:NE])
    K.cursor += 1
    K.end_stage()


def expert_loop_stage(K, l, group, M, xs_all, ys):
    nc, A, first = K.nc, K.arena, K.cursor
    NG, J = NE // group, group
    FW = D // J
    NC = FW // P
    order = expert_pieces(group)
    npiece = len(order)
    where = {p: i for i, p in enumerate(order)}
    xs = A[:, 8192:9216].rearrange("p (e k s) -> p e k s", e=group, k=KD)
    hid = A[:, 9216:10240].rearrange("p (b f) -> p b f", b=2)
    hidT = A[:, 10240:10240 + group * NC * P].rearrange("p (e c r) -> p e c r", e=group, c=NC)

    def slot(q):
        return K.ring[:, (first + q) % RING, :].rearrange("p (k w) -> p k w", k=KD)

    def landed(g, q):
        sem, n = K.landed(first + q)
        return sem, g * (16 * npiece // RING) + n

    def released(q):
        m, e, h = order[q]
        if m == "moe_w2":
            return "down_done", h + 1
        return "up_done", 2 * e + (1 if m == "moe_w1" else 2)

    def load(sp, g, q):
        m, e, h = order[q]
        sem = K.sem(f"slot{(first + q) % RING}_landed")
        sp.dma_start(K.ring[:, (first + q) % RING, :], K.dram[m][l, g * group + e, h]).then_inc(sem, 16)

    per = dict(up_done=2 * group, silu_done=group, hidden_done=group, hiddenT_ready=group, hiddenT_kept=group,
               down_done=2, ys_kept=2, xs_ready=group)

    def loop(eng, body):
        body(0, True)
        K.times = NG - 1
        with eng.Fori(1, NG) as g:
            body(g, False)
        K.times = 1

    def at(name, g, n):
        return K.at(name, g * per[name] + n)

    with K.block("experts") as block:
        @block.sync
        def _(sp):
            def feed(g, last):
                for q in range(npiece):
                    name, n = released(q)
                    sp.wait_ge(*at(name, g, n))
                    if q + RING < npiece:
                        load(sp, g, q + RING)
                    elif last:
                        K.load_next(sp)
                    else:
                        load(sp, g + 1, q + RING - npiece)
            with sp.Fori(0, NG - 1) as g:
                feed(g, False)
            K.issued += NG * npiece - RING
            feed(NG - 1, True)

        @block.gpsimd
        def _(pool):
            for e in range(group):
                nc.gpsimd.tensor_copy(xs[:, e], xs_all[:, e]).then_inc(*K.inc("xs_ready"))
            K.times = NG - 1
            with pool.Fori(0, NG - 1) as g:
                for e in range(group):
                    pool.wait_ge(*at("up_done", g, 2 * e + 2))
                    nc.gpsimd.tensor_copy(xs[:, e], xs_all[:, g * group + (group + e)]).then_inc(*K.inc("xs_ready"))
            K.times = 1

        @block.tensor
        def _(pe):
            def body(g, peeled):
                def turn(e):
                    pe.wait_ge(*at("hidden_done", g, e + 1))
                    if not (peeled and e < 2):
                        pe.wait_ge(*at("hiddenT_kept", g, e - 1))
                    for c in range(NC):
                        last = nc.tensor.transpose(K.ps[:, 4 + e % 2, c * P:(c + 1) * P], hid[:, e % 2, c * P:(c + 1) * P], K.ident)
                    last.then_inc(*K.inc("hiddenT_ready"))
                for e in range(group):
                    pe.wait_ge(*at("xs_ready", g, e + 1))
                    if not (peeled and e < 2):
                        pe.wait_ge(*at("hidden_done", g, e - 1))
                    for i, m in enumerate(("moe_w1", "moe_w3")):
                        for h in range(2):
                            pe.wait_ge(*landed(g, where[m, e, h]))
                        w = [slot(where[m, e, h]) for h in range(2)]
                        for k in range(KD):
                            for j in range(J):
                                c0 = j * FW % 512
                                last = nc.tensor.matmul(K.ps[M * j:M * j + M, 2 * (e % 2) + i, 0:FW], xs[:, e, k, :],
                                                        w[j * FW // 512][:, k, c0:c0 + FW], start=k == 0, stop=k == KD - 1)
                        last.then_inc(*K.inc("up_done"))
                    if e:
                        turn(e - 1)
                turn(group - 1)
                pe.wait_ge(*at("hiddenT_kept", g, group))
                for h in range(2):
                    if not peeled:
                        pe.wait_ge(*at("ys_kept", g, h - 1))
                    for e in range(group):
                        pe.wait_ge(*landed(g, where["moe_w2", e, h]))
                    for f in range(KD):
                        j, c = divmod(f, NC)
                        for e in range(group):
                            last = nc.tensor.matmul(K.ps[M * e:M * e + M, 6 + h, :], hidT[:, e, c, M * j:M * j + M],
                                                    slot(where["moe_w2", e, h])[:, f, :], start=f == 0, stop=f == KD - 1)
                    last.then_inc(*K.inc("down_done"))
            loop(pe, body)

        @block.scalar
        def _(act):
            def body(g, peeled):
                def keep(e):
                    act.wait_ge(*at("hiddenT_ready", g, e + 1))
                    if not peeled:
                        act.wait_ge(*at("down_done", g, 0))
                    nc.scalar.activation(hidT[:, e].rearrange("p c r -> p (c r)"), K.ps[:, 4 + e % 2, 0:NC * P], ACT.Copy)\
                        .then_inc(*K.inc("hiddenT_kept"))
                for e in range(group):
                    act.wait_ge(*at("up_done", g, 2 * e + 1))
                    if not (peeled and e < 2):
                        act.wait_ge(*at("hiddenT_ready", g, e - 1))
                    nc.scalar.activation(hid[:, e % 2, 0:FW], K.ps[:, 2 * (e % 2), 0:FW], ACT.Silu).then_inc(*K.inc("silu_done"))
                    if e:
                        keep(e - 1)
                keep(group - 1)
            loop(act, body)

        @block.vector
        def _(dve):
            def body(g, peeled):
                for e in range(group):
                    dve.wait_ge(*at("silu_done", g, e + 1))
                    dve.wait_ge(*at("up_done", g, 2 * e + 2))
                    nc.vector.tensor_tensor(hid[:, e % 2, 0:FW], hid[:, e % 2, 0:FW], K.ps[:, 2 * (e % 2) + 1, 0:FW], ALU.mult)\
                        .then_inc(*K.inc("hidden_done"))
                if not peeled:
                    dve.wait_ge(*at("xs_ready", g, group))
                else:
                    dve.wait_ge(*at("xs_ready", 0, group))
                for h in range(2):
                    dve.wait_ge(*at("down_done", g, h + 1))
                    nc.vector.tensor_copy(ys[:, g, h * 512:(h + 1) * 512], K.ps[:, 6 + h, :]).then_inc(*K.inc("ys_kept"))
            loop(dve, body)
    K.cursor += NG * npiece
    K.end_stage()


def plan_odd(K):
    K.plan("ada_w", 1)
    K.plan("od_w_in", 0)
    K.plan("od_w_out", 0)
    K.plan("router", 1)
    plan_experts(K, 4)


def odd_layer(K):
    nc, A, HT, XT = K.nc, K.arena, K.HT, K.XT
    mod_stage(K, K.sil[:, 1], K.col("ada_b1", 0, 48), (1, 4))
    scaled_norm_stage(K, 1, 0, 2)

    u = A[:, 0:7680].rearrange("p (b t) -> p b t", b=15)
    q = A[:, 7680:8704].rearrange("p (b t) -> p b t", b=4)
    k = A[:, 8704:10752].rearrange("p (b t) -> p b t", b=4)
    v = A[:, 10752:12800].rearrange("p (t e) -> p t e", t=4)
    q2 = A[:, 12800:14848].rearrange("p (s b t) -> p s b t", s=2, b=4)
    jobs = [feature_job(K, 0, b * P, P, HT[:, :, X], q[:, b, :]) for b in range(4)]
    jobs += [feature_job(K, 1, b * P, P, HT, k[:, b, :]) for b in range(4)]
    jobs += [token_job(K, 2, lambda w, i: w[:, i, :], HT, t, v[:, t, :]) for t in range(4)]
    jobs += [feature_job(K, 3 + b // 4, b % 4 * P, P, HT, u[:, b, :]) for b in range(15)]
    bias = HT[:, :, :].rearrange("p k t -> p (k t)").rearrange("p (c h n) -> p c h n", c=2, h=8)
    raw = [XT[:, :, C], A[:, 15488:17536].rearrange("p (h n) -> p h n", h=8)]
    also = K.constants(["window", "flip"], A[:, 14848:15488])
    window, flip = K.const["window"].rearrange("p (c n) -> p c n", c=2), K.const["flip"]
    gemm_stage(K, 7, jobs, "odd_in_projection", feed=1, also=also + position_bias(K, raw))
    norm_stage(K, [dict(src=[b[:, i, :]], ones=K.pair, inv=1.0 / 64, eps=K.eps["rms"],
                        out=[(b[:, i, :], b[:, i, :], slice(0, b.shape[-1]), gain, None)])
                   for b, gain in ((q, K.na_gain), (k, K.col("na_k"))) for i in range(4)],
               HT[:, :, :].rearrange("p k t -> p (k t)")[:, 0:3072],
               also=[(K.u_dram[s].rearrange("p (b t) -> p b t", b=15), u[:, :, SEGS[s]]) for s in range(2)])
    with K.block("masked_bias") as block:
        @block.gpsimd
        def _(pool):
            nc.gpsimd.memset(q2[64:128, 0], 0.0)
            nc.gpsimd.memset(q2[0:64, 1], 0.0)
            for s in range(2):
                nc.gpsimd.tensor_copy(q2[64 * s:64 * s + 64, s], q[64 * s:64 * s + 64])

        @block.tensor
        def _(pe):
            for i in range(8):
                nc.tensor.matmul(K.ps[:, i, :], flip, raw[i // 4][:, i % 4 * 2:i % 4 * 2 + 2, :],
                                 start=True, stop=True).then_inc(*K.inc("flipped"))

        @block.vector
        def _(dve):
            for i in range(8):
                dve.wait_ge(*K.at("flipped", i + 1))
                nc.vector.tensor_tensor(bias[:, i // 4, i % 4 * 2:i % 4 * 2 + 2, :], K.ps[:, i, :].rearrange("p (h n) -> p h n", h=2),
                                        window[:, i // 4, :].unsqueeze(1).broadcast_to([P, 2, T]), ALU.add)
    K.end_stage()
    units = [dict(q=[q2[:, h % 2, h // 2, c * P:(c + 1) * P]], k=k[:, h // 2, :], v=[v[:, t, h * 64:(h + 1) * 64] for t in range(4)],
                  bias=bias[:, c, h, :], rows=(h % 2 * 64, h % 2 * 64 + 64),
                  out=XT[h % 2 * 64:h % 2 * 64 + 64, h // 2, T + c * P:T + (c + 1) * P], weight=[None])
             for h in range(8) for c in range(2)]
    small, lora = A[:, 14336:18432], K.ring[:, 5, 2048:3584]
    attention_stage(K, units, A[:, 0:4096], 1, "neighbourhood_attention", also=K.constants(["causal", "level"], small[:, 2816:3840]) +
                    [(lora, K.dram["lora"][0].rearrange("(p n) -> p n", p=P))])

    y = rwkv(K, small, lora.rearrange("p (w c) -> p w c", w=3))
    with K.block("mixed") as block:
        @block.scalar
        def _(act):
            nc.scalar.activation(HT[:, 4:8, X], XT[:, 0:4, C], ACT.Copy)

        @block.vector
        def _(dve):
            nc.vector.tensor_tensor(HT[:, 0:4, X], y, XT[:, 4:8, C], ALU.mult)
    K.end_stage()
    out_proj_stage(K, 2, 1)
    experts(K, 1, 1)


def position_bias(K, raw):
    rpb, pairs = K.dram["na_rpb"], []
    for r in range(4):
        for h in range(8):
            src = bass.AP(rpb.tensor, h * 15 * 31 + (7 - r) * 31 + 15 - 63, [[1, 64], [31, 4], [1, 64]])
            dst = raw[r // 2][r % 2 * 64:r % 2 * 64 + 64, h, :].rearrange("p (i j) -> p i j", i=4)
            pairs.append((dst, src))
    return pairs


def rwkv(K, small, lora):
    nc, A = K.nc, K.arena
    ring = K.ring[:, :, :].rearrange("p s n -> p (s n)")
    hf = K.HT[:, :, :].rearrange("p k t -> p (k t)")
    m = Recurrence()
    four = lambda a, lo: a[:, lo:lo + 1024].rearrange("p (b t) -> p b t", b=4)
    m.r, m.k, m.v, m.kk = (four(ring, 18432 + i) for i in (0, 1024, 2048, 3072))
    m.rkv = ring[:, 18432:21504]
    m.lora = lora
    m.lw, m.la, m.lg = (small[:, T * i:T * i + T] for i in range(3))
    m.y = four(small, 768)
    m.state = small[:, 1792:2304].rearrange("p (d b v) -> p d b v", d=2, b=4)
    m.rhs = small[:, 2304:2816].rearrange("p (d b v) -> p d b v", d=2, b=4)
    m.g_end = small[:, 3840:3872].rearrange("p (d i) -> p d i", d=2)
    m.gate = K.XT[:, 4:8, C]
    for d, (buf, bd) in enumerate(((ring, ring[:, 14336:18432]), (A, hf))):
        w = Recurrence()
        w.ar = buf[:, 0:2048].rearrange("p (i w t) -> p i w t", i=16, w=2)
        w.bk = buf[:, 2048:4096].rearrange("p (i w t) -> p i w t", i=16, w=2)
        w.uv = buf[:, 2048:4096].rearrange("p (i h v) -> p i h v", i=16, h=2)
        w.n = buf[:, 4096:8192].rearrange("p (w i c) -> p w i c", w=2, i=16)
        w.w = buf[:, 8192:12288].rearrange("p (i h c) -> p i h c", i=16, h=2)
        w.tok = buf[:, 12288:14336].rearrange("p (i c) -> p i c", i=16)
        w.bd = bd.rearrange("p (w i c) -> p w i c", w=2, i=16)
        w.x = w.bd
        w.decay, w.rate, w.p0, w.p1, w.e2, w.keff = (four(buf, 4096 + 1024 * i) for i in range(6))
        m.of.append(w)
    m.u = A[:, 8192:12032].rearrange("p (b t) -> p b t", b=15)
    work = A[:, 4096:7168]
    m.causal = K.const["causal"].rearrange("p (d w t) -> p d w t", d=2, w=2)
    m.level = K.const["level"].rearrange("p (d l t) -> p d l t", d=2, l=6)
    for s in (1, 0):
        rwkv_inputs(K, m, s, work)
        rwkv_rates(K, m, s)
        rwkv_scale(K, m, s)
        rwkv_products(K, m)
        rwkv_inverse(K, m)
        rwkv_chunks(K, m, s)
    with K.block("refill") as block:
        @block.sync
        def _(sp):
            for _ in range(RING):
                K.load_next(sp)
    K.end_stage()
    norm_stage(K, [dict(src=[m.y[:, b, :]], ones=K.pair, inv=1.0 / 64, eps=K.eps["gn"],
                        out=[(m.y[:, b, :], m.y[:, b, :], slice(0, T), K.col("gn_g", b), K.col("gn_b", b))]) for b in range(4)],
               work, centre=True)
    return m.y


class Recurrence:

    def __init__(self):
        self.of = []


def rwkv_inputs(K, m, s, work):
    nc = K.nc
    dst = [b[:, i, :] for b in (m.r, m.k, m.v) for i in range(4)] + [m.lw, m.la, m.lg]
    with K.block("token_shift") as block:
        @block.sync
        def _(sp):
            sp.dma_start(m.u, K.u_dram[s].rearrange("p (b t) -> p b t", b=15)).then_inc(*K.inc("u_loaded", 16))
            sp.wait_ge(*K.at("u_loaded", 16))

        @block.gpsimd
        def _(pool):
            if s == 1:
                nc.gpsimd.memset(m.state, 0.0)

        @block.vector
        def _(dve):
            tap = lambda j, b: K.col("shift_w", 15 * j + b)
            for i, (j, to, of) in enumerate(((0, slice(1, T), slice(0, T - 1)), (2, slice(0, T - 1), slice(1, T)))):
                for b in range(15):
                    dve.wait_ge(*K.at(("tap_added", "middle_tap")[i == 0], b + 1))
                    nc.vector.scalar_tensor_tensor(out=dst[b][:, to], in0=m.u[:, b, of], scalar=tap(j, b), in1=dst[b][:, to],
                                                   op0=ALU.mult, op1=ALU.add).then_inc(*K.inc("tap_added"))
            dve.wait_ge(*K.at("tap_added", 30))
            for b in range(4):
                nc.vector.tensor_scalar(m.kk[:, b, :], m.k[:, b, :], K.col("k_k", b), None, ALU.mult)

        @block.scalar
        def _(act):
            act.wait_ge(*K.at("u_loaded", 16))
            for b in range(15):
                nc.scalar.activation(dst[b], m.u[:, b, :], ACT.Copy, scale=K.col("shift_w", 15 + b)).then_inc(*K.inc("middle_tap"))
            act.wait_ge(*K.at("tap_added", 30))
            nc.scalar.activation(m.lw, m.lw, ACT.Tanh)
            nc.scalar.activation(m.lg, m.lg, ACT.Sigmoid)
    K.end_stage()
    norm_stage(K, [dict(src=[m.kk[:, b, :]], ones=K.pair, inv=1.0, eps=K.eps["kk"],
                        out=[(m.kk[:, b, :], m.kk[:, b, :], slice(0, T), None, None)]) for b in range(4)], work)


def rwkv_rates(K, m, s):
    nc = K.nc
    jobs = []
    for d in range(2):
        rows = slice(64 * d, 64 * d + 64)
        for which, src, out, bias in ((0, m.lw, m.of[d].decay, "w0"), (1, m.la, m.of[d].rate, "a0")):
            for b in range(4):
                jobs.append(dict(
                    pieces=[], rows=(0, P), n=T, only="act",
                    mm=lambda _, rows=rows, which=which, src=src, b=b: [(m.lora[rows, which, b * P:(b + 1) * P], src[rows])],
                    evac=lambda side, ps, eng, out=out, bias=bias, b=b, d=d:
                        nc.scalar.activation(out[:, b, :], ps, ACT.Sigmoid, bias=K.col(bias, 4 * d + b))))
    if s == 0:
        jobs += [dict(pieces=[], rows=(0, P), n=T, only="dve", mm=lambda _, b=b: [(m.lora[:, 2, b * P:(b + 1) * P], m.lg)],
                      evac=lambda side, ps, eng, b=b: evacuate(K, side, m.gate[:, b, :], ps)) for b in range(4)]
    gemm_stage(K, 0, jobs, "rwkv_rates")


def rwkv_scale(K, m, s):
    nc = K.nc
    by_chunk = lambda a: a.rearrange("p b (c t) -> p (b c) t", t=CH)
    r, k, kk = (by_chunk(a) for a in (m.r, m.k, m.kk))
    c = -math.exp(-0.5)

    reset = m.of[0].keff.rearrange("p b t -> p (b t)")

    def clear(eng, d, tag):
        for i in range(4):
            h = i % 2
            eng.memset(m.of[d].bd[64 * h:64 * h + 64, i // 2, :, 64 - 64 * h:128 - 64 * h], 0.0).then_inc(*K.inc(f"cleared_{tag}"))
        eng.wait_ge(*K.at(f"cleared_{tag}", 4))

    def scale(eng, d, tag):
        w = m.of[d]
        p0, p1, e2, rate, keff = (by_chunk(a) for a in (w.p0, w.p1, w.e2, w.rate, w.keff))
        done = f"{tag}_step"
        for b in range(4):
            last = eng.tensor_scalar(w.keff[:, b, :], w.rate[:, b, :], -1.0, K.col("k_a", b), ALU.add, ALU.mult)
        K.step(eng, last, done)
        eng.tensor_tensor(rate, rate, kk, ALU.mult)
        K.step(eng, eng.tensor_tensor(keff, keff, k, ALU.mult), done)
        eng.tensor_scalar(rate, rate, -1.0, None, ALU.mult)
        K.step(eng, eng.tensor_tensor(keff, keff, k, ALU.add), f"effective_key_{tag}")
        eng.wait_ge(*K.at(f"exps_{tag}", 3))
        eng.tensor_tensor(w.ar[:, :, 0, :], kk, p0, ALU.mult).then_inc(*K.inc(f"scaled_{tag}"))
        eng.tensor_tensor(w.bk[:, :, 0, :], rate, p1, ALU.mult).then_inc(*K.inc(f"scaled_{tag}"))
        eng.tensor_tensor(w.bk[:, :, 1, :], keff, p1, ALU.mult)

    with K.block("rwkv_scale") as block:
        @block.vector
        def _(dve):
            dve.wait_ge(*K.at("reset_ready", 2))
            for d in range(2):
                L, p1 = (a.rearrange("p b t -> p (b t)")[:, ::(1, -1)[d]] for a in (m.of[d].decay, m.of[d].p1))
                nc.vector.tensor_tensor_scan(p1, reset, L, 0.0, ALU.mult, ALU.add).then_inc(*K.inc("cumulated"))
            for d in range(2):
                dve.wait_ge(*K.at("cumulated", d + 1))
                nc.vector.tensor_tensor(m.of[d].p0, m.of[d].p1, m.of[d].decay, ALU.subtract).then_inc(*K.inc("cumulated_before"))
            clear(nc.vector, 0, "dve")
            scale(nc.vector, 0, "dve")
            for d, tag in enumerate(("dve", "pool")):
                e2 = by_chunk(m.of[d].e2)
                dve.wait_ge(*K.at(f"exps_{tag}", 1))
                nc.vector.tensor_tensor(m.of[d].ar[:, :, 1, :], r, e2, ALU.mult)
                nc.vector.tensor_copy(m.g_end[:, d].unsqueeze(2), e2[:, :, (CH - 1, 0)[d]:(CH, 1)[d]])
            if s == 0:
                t, other = m.of[0].decay, m.of[1].keff
                dve.wait_ge(*K.at("cumulated_before", 1))
                dve.wait_ge(*K.at("effective_key_pool", 1))
                K.step(dve, nc.vector.tensor_tensor(t, m.of[0].keff, other, ALU.add), "dve_step")
                K.step(dve, nc.vector.tensor_tensor(t, t, m.r, ALU.mult), "dve_step")
                for b in range(4):
                    nc.vector.tensor_scalar(t[:, b, :], t[:, b, :], K.col("r_k", b), None, ALU.mult).then_inc(*K.inc("bonus_ready"))
                for b in range(4):
                    dve.wait_ge(*K.at("bonus_summed", b + 1))
                    nc.vector.tensor_tensor(m.y[:, b, :], K.ps[:, b, 0:T], m.v[:, b, :], ALU.mult)

        @block.gpsimd
        def _(pool):
            by_token = reset.rearrange("p (i t) -> p i t", t=CH)
            nc.gpsimd.memset(by_token[:, :, 0:1], 0.0).then_inc(*K.inc("reset_ready"))
            nc.gpsimd.memset(by_token[:, :, 1:CH], 1.0).then_inc(*K.inc("reset_ready"))
            pool.wait_ge(*K.at("reset_ready", 2))
            clear(nc.gpsimd, 1, "pool")
            scale(nc.gpsimd, 1, "pool")

        @block.tensor
        def _(pe):
            if s == 0:
                for b in range(4):
                    pe.wait_ge(*K.at("bonus_ready", b + 1))
                    nc.tensor.matmul(K.ps[:, b, 0:T], K.pair, m.of[0].decay[:, b, :], start=True, stop=True).then_inc(*K.inc("bonus_summed"))

        @block.scalar
        def _(act):
            for d, tag in enumerate(("dve", "pool")):
                w = m.of[d]
                act.wait_ge(*K.at("cumulated_before", d + 1))
                nc.scalar.activation(w.e2, w.p1, ACT.Exp, scale=c).then_inc(*K.inc(f"exps_{tag}"))
                nc.scalar.activation(w.p0, w.p0, ACT.Exp, scale=c).then_inc(*K.inc(f"exps_{tag}"))
                act.wait_ge(*K.at(f"exps_{tag}", 1))
                nc.scalar.activation(w.p1, w.p1, ACT.Exp, scale=-c).then_inc(*K.inc(f"exps_{tag}"))
            for d, tag in enumerate(("dve", "pool")):
                w = m.of[d]
                for i, src in enumerate((w.ar, w.bk)):
                    act.wait_ge(*K.at(f"scaled_{tag}", i + 1))
                    for h in range(2):
                        rows = slice(64 * h, 64 * h + 64)
                        nc.scalar.activation(w.bd[rows, i, :, 64 * h:64 * h + 64], src[rows, :, 0, :], ACT.Copy)
    K.end_stage()


def rwkv_products(K, m):
    nc = K.nc
    flat = lambda a: a.rearrange("p w t -> p (w t)")
    jobs = []

    def job(emit, evac, only, rows=(0, P)):
        jobs.append(dict(pieces=[], rows=rows, n=512, only=only, emit=emit, evac=evac))

    for d in range(2):
        w = m.of[d]
        mask = flat(m.causal[:, d]).unsqueeze(1).broadcast_to([P, 4, P])
        for q in range(4):
            chunks = range(4 * q, 4 * q + 4)
            for h in range(2):
                def emit(bank, w=w, h=h, chunks=chunks):
                    for i in chunks:
                        rows = slice(64 * h, 64 * h + 64)
                        last = nc.tensor.matmul(K.ps[:, bank, i % 4 * P:(i % 4 + 1) * P], flat(w.bk[rows, i]), flat(w.ar[rows, i]),
                                                start=True, stop=True)
                    return last
                job(emit, lambda side, ps, eng, w=w, q=q, h=h, mask=mask: nc.vector.tensor_tensor(
                    w.w[:, 4 * q:4 * q + 4, h, :], ps.rearrange("p (i c) -> p i c", i=4), mask, ALU.mult), "dve")
            for t in range(2):
                def emit(bank, w=w, t=t, chunks=chunks):
                    for i in chunks:
                        last = nc.tensor.matmul(K.ps[:, bank, i % 4 * P:(i % 4 + 1) * P], w.bd[:, t, i, :], w.bd[:, 1 - t, i, :],
                                                start=True, stop=True)
                    return last
                strict = m.causal[:, (1 - d, d)[t], 0, :].unsqueeze(1).broadcast_to([P, 8, CH])
                job(emit, lambda side, ps, eng, w=w, q=q, t=t, strict=strict: nc.vector.tensor_tensor(
                    w.n[:, t, 4 * q:4 * q + 4, :].rearrange("p i (h c) -> p (i h) c", h=2),
                    ps.rearrange("p (i c) -> p i c", i=8), strict, ALU.mult), "dve")

            def emit(bank, w=w, chunks=chunks):
                for i in chunks:
                    last = nc.tensor.transpose(K.ps[:, bank, i % 4 * P:(i % 4 + 1) * P], flat(w.bk[:, i]), K.ident)
                return last
            job(emit, lambda side, ps, eng, w=w, q=q: nc.scalar.activation(
                w.tok[:, 4 * q:4 * q + 4].rearrange("p i c -> p (i c)"), ps, ACT.Copy), "act")
        for q in range(4):
            def emit(bank, q=q):
                for i in range(4 * q, 4 * q + 4):
                    c0 = 2048 + CH * i - CH
                    last = nc.tensor.transpose(K.ps[:, bank, i % 4 * P:(i % 4 + 1) * P], m.rkv[:, c0:c0 + P], K.ident)
                return last
            job(emit, lambda side, ps, eng, w=w, q=q: nc.scalar.activation(
                w.uv[64:128, 4 * q:4 * q + 4].rearrange("p i h v -> p (i h v)"), ps[64:128], ACT.Copy), "act")
    gemm_stage(K, 0, jobs, "rwkv_products")


def rwkv_inverse(K, m):
    nc, levels = K.nc, 6
    jobs = []
    for i in range(1, levels):
        jobs += [(i, "z", d, q) for d in range(2) for q in range(4)]
        jobs += [(i, kind, d, q) for d in range(2) for q in range(4) for kind in (("x", "xT") if i < levels - 1 else ("xT",))]
    where = {job: j for j, job in enumerate(jobs)}
    quarter = lambda a, q: a[:, 4 * q:4 * q + 4, :]
    by_head = lambda a: a.rearrange("p i (h c) -> p (i h) c", h=2)

    with K.block("rwkv_inverse") as block:
        @block.vector
        def _(dve):
            level = lambda dd, i: m.level[:, dd, i, :].unsqueeze(1).broadcast_to([P, 8, CH])
            eye = K.ident.unsqueeze(1).broadcast_to([P, 4, P])
            for d in range(2):
                w = m.of[d]
                for q in range(4):
                    for t in range(2):
                        x = quarter(w.x[:, t], q)
                        nc.vector.tensor_tensor(by_head(x), by_head(quarter(w.n[:, t], q)), level((d, 1 - d)[t], 0), ALU.mult)\
                            .then_inc(*K.inc("first_level"))
                        dve.wait_ge(*K.at("first_level", 8 * d + 2 * q + t + 1))
                        last = nc.vector.tensor_tensor(x, x, eye, ALU.add)
                    last.then_inc(*K.inc("inverse_begun"))
            for j, (i, kind, d, q) in enumerate(jobs):
                w = m.of[d]
                ps = K.ps[:, j % NBANK, :].rearrange("p (i c) -> p i c", i=4)
                dve.wait_ge(*K.at("inverse_product", j + 1))
                if kind == "z":
                    out = quarter(w.n[:, 0], q)
                    last = nc.vector.tensor_tensor(by_head(out), by_head(ps), level(d, i), ALU.mult)
                else:
                    if kind == "x":
                        dve.wait_ge(*K.at("inverse_product", where[i, "xT", d, q] + 1))
                    x = quarter(w.x[:, 0 if kind == "x" else 1], q)
                    last = nc.vector.tensor_tensor(x, x, ps, ALU.add)
                last.then_inc(*K.inc("inverse_kept"))

        @block.tensor
        def _(pe):
            for j, (i, kind, d, q) in enumerate(jobs):
                w = m.of[d]
                if j >= NBANK:
                    pe.wait_ge(*K.at("inverse_kept", j - NBANK + 1))
                if kind == "z" and i == 1:
                    pe.wait_ge(*K.at("inverse_begun", 4 * d + q + 1))
                elif kind == "z":
                    pe.wait_ge(*K.at("inverse_kept", where[i - 1, "xT", d, q] + 1))
                else:
                    pe.wait_ge(*K.at("inverse_kept", where[i, "z", d, q] + 1))
                lhs, rhs = {"z": (w.n[:, 1], w.x[:, 0]), "x": (w.x[:, 1], w.n[:, 0]), "xT": (w.n[:, 0], w.x[:, 1])}[kind]
                for c in range(4 * q, 4 * q + 4):
                    last = nc.tensor.matmul(K.ps[:, j % NBANK, c % 4 * P:(c % 4 + 1) * P], lhs[:, c, :], rhs[:, c, :], start=True, stop=True)
                last.then_inc(*K.inc("inverse_product"))

        @block.gpsimd
        def _(pool):
            for d in range(2):
                nc.gpsimd.memset(m.of[d].uv[0:64], 0.0)
    K.end_stage()


def rwkv_chunks(K, m, s):
    nc = K.nc
    order = (range(4), range(3, -1, -1))
    heads = [(b, h) for b in range(4) for h in range(2)]
    tags = ("forward", "backward")
    out = s == 0
    steps = [(n, d) for n in range(4) for d in range(2)]
    with K.block("rwkv_chunks") as block:
        @block.tensor
        def _(pe):
            def right_sides(n, d):
                w, c = m.of[d], order[d][n]
                if n:
                    pe.wait_ge(*K.at(f"state_{tags[d]}", n))
                for b, h in heads:
                    rows, i = slice(64 * h, 64 * h + 64), 4 * b + c
                    to = K.ps[rows, 3 * d, b * CH:(b + 1) * CH]
                    nc.tensor.matmul(to, w.ar[rows, i, 0, :], m.state[rows, d, b, :], start=True, stop=False)
                    last = nc.tensor.matmul(to, w.w[:, i, h, 0:CH], w.uv[:, i, h, :], start=False, stop=True)
                last.then_inc(*K.inc("right_sides"))

            def solve(n, d):
                w, c = m.of[d], order[d][n]
                pe.wait_ge(*K.at("right_sides_kept", 2 * n + d + 1))
                for b, h in heads:
                    rows, i = slice(64 * h, 64 * h + 64), 4 * b + c
                    last = nc.tensor.matmul(K.ps[0:64, 3 * d + 1 + h, b * CH:(b + 1) * CH], w.x[rows, 1, i, 64 * h:64 * h + 64],
                                            m.rhs[rows, d, b, :], start=True, stop=True)
                last.then_inc(*K.inc("solved"))

            def advance(n, d):
                w, c = m.of[d], order[d][n]
                pe.wait_ge(*K.at("solution_kept", 2 * n + d + 1))
                for b, h in heads:
                    rows, i = slice(64 * h, 64 * h + 64), 4 * b + c
                    if out:
                        to = K.ps[rows, 3 * d, 256 + b * CH:256 + (b + 1) * CH]
                        nc.tensor.matmul(to, m.state[rows, d, b, :], w.ar[rows, i, 1, :], start=True, stop=False)
                        nc.tensor.matmul(to, w.uv[:, i, h, :], w.w[:, i, h, CH:2 * CH], start=False, stop=True)
                    last = nc.tensor.matmul(K.ps[rows, 3 * d + 1, 256 + b * CH:256 + (b + 1) * CH], w.tok[:, i, 64 * h:64 * h + 64],
                                            w.uv[:, i, h, :], start=True, stop=True)
                last.then_inc(*K.inc("chunk_done"))
            for n in range(4):
                for phase in (right_sides, solve, advance):
                    for d in range(2):
                        phase(n, d)

        @block.scalar
        def _(act):
            for j, (n, d) in enumerate(steps):
                act.wait_ge(*K.at("right_sides", j + 1))
                nc.scalar.activation(m.rhs[:, d].rearrange("p b v -> p (b v)"), K.ps[:, 3 * d, 0:256], ACT.Copy)\
                    .then_inc(*K.inc("right_sides_kept"))

        @block.vector
        def _(dve):
            for n in range(4):
                for d in range(2):
                    w, c = m.of[d], order[d][n]
                    dve.wait_ge(*K.at("solved", 2 * n + d + 1))
                    for h in range(2):
                        uv = w.uv.rearrange("p (b c) h v -> p b c h v", b=4)[0:64, :, c, h, :]
                        last = nc.vector.tensor_copy(uv, K.ps[0:64, 3 * d + 1 + h, 0:256].rearrange("p (b v) -> p b v", b=4))
                    last.then_inc(*K.inc("solution_kept"))
                for d in range(2):
                    c, S = order[d][n], m.state[:, d]
                    g = m.g_end[:, d].rearrange("p (b c) -> p b c", b=4)[:, :, c:c + 1].broadcast_to([P, 4, CH])
                    dve.wait_ge(*K.at("chunk_done", 2 * n + d + 1))
                    if out:
                        y = m.y[:, :, c * CH:(c + 1) * CH]
                        nc.vector.tensor_tensor(y, y, K.ps[:, 3 * d, 256:512].rearrange("p (b t) -> p b t", b=4), ALU.add)
                    K.step(dve, nc.vector.tensor_tensor(S, S, K.ps[:, 3 * d + 1, 256:512].rearrange("p (b v) -> p b v", b=4), ALU.add), "dve_step")
                    nc.vector.tensor_tensor(S, S, g, ALU.mult).then_inc(*K.inc(f"state_{tags[d]}"))
    K.end_stage()


def store_stage(K, out):
    with K.block("store") as block:
        @block.sync
        def _(sp):
            sp.dma_start(out.rearrange("(k p) t -> p k t", p=P), K.XT[:, :, X]).then_inc(*K.inc("output_stored", 16))
            sp.wait_ge(*K.at("output_stored", 16))
    K.end_stage()


def build_program(nc, dram, out, layers=("f0", "f1", "s0", "s1")):
    with ExitStack() as ctx:
        K = Kit(nc, ctx, dram)
        K.const, K.eps = {}, {}
        K.u_dram = nc.dram_tensor("rwkv_inputs", (2, P, 15 * T), F32, kind="Internal").ap()
        for l in range(DEPTH):
            if f"f{l}" in layers:
                for name in ("w_mod", "w_in", "w_out", "w_up", "w_down"):
                    K.plan(name, l)
        if "s0" in layers:
            plan_even(K)
        if "s1" in layers:
            plan_odd(K)
        prologue(K)
        for l in range(DEPTH):
            if f"f{l}" in layers:
                first_layer(K, l)
        if "s0" in layers:
            even_layer(K)
        if "s1" in layers:
            odd_layer(K)
        store_stage(K, out)


def tiled(w, parts):
    return np.concatenate([w[r0:r1, c0:c1].reshape((r1 - r0) // P, P, c1 - c0).transpose(1, 0, 2).ravel()
                           for r0, r1, c0, c1 in parts])


def constant_tables():
    out = {n: np.zeros((P, w), np.float64) for n, w in CONSTS.items()}
    out["ident"][:] = np.eye(P)
    out["ones"][:] = 1
    out["pair"][:64, :64] = out["pair"][64:, 64:] = 1
    t = np.arange(T)
    row, col = (t // GRID_W).astype(np.float32), (t % GRID_W).astype(np.float32)

    def rope(base, width, reps, swap, cos, sin):
        half, quarter = width // 2, width // 4
        inv = (np.float32(1.0) / np.float32(10000.0) ** (np.arange(0, half, 2, dtype=np.float32) / np.float32(half))).astype(np.float32)
        out[cos][:] = 1
        for r in range(reps):
            for i in range(width):
                j = i % half
                ang = ((row if i < half else col) * inv[j % quarter]).astype(np.float32).astype(np.float64)
                p = base + r * width + i
                out[cos][p], out[sin][p] = np.cos(ang), (-1 if j < quarter else 1) * np.sin(ang)
                out[swap][p + (quarter if j < quarter else -quarter), p] = 1
    rope(0, 64, 2, "swap1", "cos1", "sin1")
    rope(64, 32, 1, "swap2", "cos2", "sin2")
    ang = 2 * np.pi * (np.outer(t, t) % T) / T
    out["cn"][:] = (np.cos(ang) / 16).reshape(2, P, T).transpose(1, 0, 2).reshape(P, 512)
    out["sn"][:] = (np.sin(ang) / 16).reshape(2, P, T).transpose(1, 0, 2).reshape(P, 512)
    m = np.arange(64)
    ang = 2 * np.pi * (np.outer(m, m) % 64) / 64
    for g in range(2):
        s = slice(64 * g, 64 * g + 64)
        out["cm"][s, s], out["sm"][s, s] = np.cos(ang) / 8, -np.sin(ang) / 8
    out["tri"][:] = np.triu(np.ones((P, P)))
    out["iota"][:] = np.arange(1, 65)[None]
    c = np.arange(GRID_W)
    start = np.clip(c - 8, 0, GRID_W - 16)
    inside = (c[None] >= start[:, None]) & (c[None] < start[:, None] + 16)
    add = np.where(inside[t % GRID_W][:, t % GRID_W], 0.0, -1e30)
    out["window"][:] = add.reshape(2, P, T).transpose(1, 0, 2).reshape(P, 512)
    s, u = np.arange(CH)[:, None], np.arange(CH)[None]
    causal = [np.concatenate([before(s, u), ~before(u, s)], 1) for before in (np.less, np.greater)]
    out["causal"][:] = np.tile(np.concatenate(causal, 1), (2, 1))
    for i in range(6):
        b = 1 << i
        low = (s // (2 * b) == u // (2 * b)) & (s // b % 2 == 1) & (u // b % 2 == 0)
        for d, msk in enumerate((low, low.T)):
            at = (d * 6 + i) * 64
            out["level"][:, at:at + 64] = np.tile(msk, (2, 1))
    out["flip"][:] = np.kron(np.eye(2), np.eye(64)[::-1])
    return np.concatenate([out[n] for n in CONSTS], 1).astype(np.float32)


def as_columns(v):
    v = np.asarray(v, np.float32).reshape(-1)
    v = np.concatenate([v, np.zeros(-len(v) % P, np.float32)])
    return v.reshape(-1, P).T


def host_arrays(a):
    f = {k: np.asarray(v) for k, v in a.items()}
    vec = {
        "c": f["c"], "c_ctx": f["c_ctx"], "c_2": f["c_2"], "c_ctx_2": f["c_ctx_2"],
        "q_norm": f["mla_q_norm_2"], "kv_norm": f["mla_kv_norm_2"], "q_g": f["mla_q_g_2"], "k_g": f["mla_k_g_2"],
        "dw_w": f["cv_dw_w_2"], "dw_b": f["cv_dw_b_2"], "cln_g": f["cv_ln_g_2"], "cln_b": f["cv_ln_b_2"],
        "shift_w": f["rw_shift_w_2"], "w0": f["rw_w0_2"], "a0": f["rw_a0_2"], "k_k": f["rw_k_k_2"], "k_a": f["rw_k_a_2"],
        "r_k": f["rw_r_k_2"], "gn_g": f["rw_gn_g_2"], "gn_b": f["rw_gn_b_2"],
        "na_q": np.tile(f["na_q_g_2"].reshape(-1), 2), "na_k": np.tile(f["na_k_g_2"].reshape(-1), 2),
    }
    for l in range(DEPTH):
        vec |= {f"b_mod{l}": f["b_mod"][l], f"ada_b{l}": f["ada_b_2"][l], f"subln{l}": f["subln_w"][l],
                f"conv_w{l}": f["conv_w"][l], f"conv_b{l}": f["conv_b"][l],
                f"norm1_g{l}": f["norm1_g_2"][l], f"norm2_g{l}": f["norm2_g_2"][l]}
        vec |= {f"{n}{l}": f[n][l] for n in ("ln1_g", "ln1_b", "ln2_g", "ln2_b")}
    out = {"cols": np.concatenate([as_columns(vec[n]) for n in COLS], 1), "consts": constant_tables(),
           "diff_lambda": f["diff_lambda"].reshape(-1), "na_rpb": f["na_rpb_2"].reshape(-1)}
    out |= {n: np.ascontiguousarray(f[n][0].T) for n in ("x", "ctx", "ctx_2")}
    weights = {
        "w_mod": f["w_mod"], "w_in": f["w_in"], "w_out": f["w_out"], "w_up": f["w_up"], "w_down": f["w_down"],
        "ada_w": f["ada_w_2"], "ev_w_in": f["ev_w_in_2"], "ev_w_out": f["ev_w_out_2"], "w_uq": f["mla_w_uq_2"],
        "w_ukv": f["mla_w_ukv_2"], "router": f["moe_router_2"], "od_w_in": f["od_w_in_2"], "od_w_out": f["od_w_out_2"],
        "lora": np.concatenate([f["rw_w2_2"].reshape(1, P, 512), f["rw_a2_2"].reshape(1, P, 512), f["rw_g2_2"]], 1),
    }
    for n, w in weights.items():
        out[n] = np.stack([tiled(w[l], PARTS[n]) for l in range(w.shape[0])])
    for n in ("moe_w1_2", "moe_w3_2", "moe_w2_2"):
        w = f[n]
        out[n[:6]] = np.ascontiguousarray(w.reshape(DEPTH, NE, KD, P, 2, 512).transpose(0, 1, 4, 3, 2, 5)).reshape(DEPTH, NE, 2, P, SLOT)
    return {k: np.ascontiguousarray(v) for k, v in out.items()}


def kernel(**inputs):
    import concourse.bacc as bacc
    from concourse.bass_utils import run_bass_kernel_spmd

    nc = bacc.Bacc("TRN2", target_bir_lowering=False, num_devices=1)
    arrays = {f"in_{n}": a for n, a in host_arrays(inputs).items()}
    dram = {n[3:]: nc.dram_tensor(n, a.shape, mybir.dt.from_np(a.dtype), kind="ExternalInput").ap() for n, a in arrays.items()}
    out = nc.dram_tensor("out_x", (D, T), F32, kind="ExternalOutput").ap()
    build_program(nc, dram, out)
    r = run_bass_kernel_spmd(nc, [arrays], core_ids=[0])
    return np.ascontiguousarray(np.asarray(r.results[0]["out_x"]).T).reshape(1, T, D)
```

```python
import math
from contextlib import ExitStack

import numpy as np

import concourse.bass as bass
from concourse import mybir

F32 = mybir.dt.float32
ALU = mybir.AluOpType
ACT = mybir.ActivationFunctionType
AX = mybir.AxisListType.X

P = 128
D = 1024
KD = D // P
T = 256
TT = 2 * T
X, C = slice(0, T), slice(T, TT)
SEGS = (X, C)
DEPTH = 2
FF = 4 * D
RING = 6
SLOT = 4096
NBANK = 8
ALPHA = (2 * DEPTH) ** 0.25
EARLY = 4
NE = 16
CAP = 32
CH = 64
GRID_W = 64


def column_parts(w, step=512):
    rows, cols = w
    return [(0, rows, c, min(c + step, cols)) for c in range(0, cols, step)]


def ranges(rows, *cuts):
    return [(0, rows, a, b) for a, b in cuts]


PARTS = {
    "w_mod": column_parts((D, 6 * D)),
    "w_in": column_parts((D, 2560)),
    "w_out": column_parts((D, D)),
    "w_up": column_parts((D, FF)),
    "w_down": [(r, r + D, c, c + 512) for c in (0, 512) for r in range(0, FF, D)],
    "ada_w": column_parts((D, 6 * D)),
    "ev_w_in": ranges(D, (0, 384), (384, 672), (672, 1184), (1184, 1696)),
    "ev_w_out": column_parts((D, D)),
    "w_uq": ranges(384, (0, 768)),
    "w_ukv": ranges(256, (0, 1024)),
    "router": ranges(D, (0, NE)),
    "od_w_in": ranges(D, (1920, 2432), (2432, 2944), (2944, 3456), (0, 512), (512, 1024), (1024, 1536), (1536, 1920)),
    "lora": ranges(384, (0, 512)),
    "od_w_out": column_parts((D, D)),
    "moe": column_parts((D, D)),
}

COLS = {
    "c": D, "c_ctx": D, "c_2": D, "c_ctx_2": D,
    "b_mod0": 6 * D, "b_mod1": 6 * D, "ada_b0": 6 * D, "ada_b1": 6 * D,
    "subln0": P, "subln1": P,
    "conv_w0": 3 * T, "conv_w1": 3 * T, "conv_b0": T, "conv_b1": T,
    "ln1_g0": D, "ln1_b0": D, "ln2_g0": D, "ln2_b0": D,
    "ln1_g1": D, "ln1_b1": D, "ln2_g1": D, "ln2_b1": D,
    "norm1_g0": D, "norm1_g1": D, "norm2_g0": D, "norm2_g1": D,
    "q_norm": 384, "kv_norm": 256, "q_g": P, "k_g": P,
    "dw_w": 31 * 512, "dw_b": 512, "cln_g": 512, "cln_b": 512,
    "shift_w": 3 * 1920, "w0": 1024, "a0": 1024, "k_k": 512, "k_a": 512, "r_k": 512,
    "gn_g": 512, "gn_b": 512, "na_q": P, "na_k": P,
}
COL_AT, NCOL = {}, 0
for _name, _n in COLS.items():
    COL_AT[_name] = NCOL
    NCOL += _n // P

CONSTS = {
    "ident": 128, "ones": 128, "pair": 128, "swap1": 128, "cos1": 256, "sin1": 256,
    "swap2": 128, "cos2": 256, "sin2": 256, "cn": 512, "sn": 512, "cm": 128, "sm": 128,
    "tri": 128, "iota": 64, "window": 512, "causal": 256, "level": 768,
    "flip": 128,
}
CONST_AT, NCONST = {}, 0
for _name, _n in CONSTS.items():
    CONST_AT[_name] = NCONST
    NCONST += _n


class Kit:

    def __init__(self, nc, ctx, dram):
        self.nc, self.ctx, self.dram = nc, ctx, dram
        self.times = 1
        self.sems, self.given, self.base = {}, {}, {}
        self.stream, self.cursor, self.issued, self.stages = [], 0, 0, 0
        self.ring = self.sb("ring", [P, RING, SLOT])
        self.XT = self.sb("XT", [P, KD, TT])
        self.HT = self.sb("HT", [P, KD, TT])
        self.arena = self.sb("arena", [P, 18432])
        self.cols = self.sb("cols", [P, NCOL])
        self.base_consts = self.sb("base_consts", [P, 3 * 128])
        self.sil = self.sb("sil", [P, 2, KD, 32])
        self.modcol = self.sb("modcol", [P, 2, 48])
        self.gain = self.sb("gain", [P, 2, KD])
        self.small = self.sb("small", [P, 80])
        self.ps = ctx.enter_context(nc.psum_tensor("ps", [P, NBANK, 512], F32))
        self.ident = self.base_consts[:, 0:128]
        self.ones = self.base_consts[:, 128:256]
        self.pair = self.base_consts[:, 256:384]

    def sb(self, name, shape):
        return self.ctx.enter_context(self.nc.sbuf_tensor(name, shape, F32))

    def block(self, name):
        self.stages += 1
        return self.nc.Block(f"{name}_{self.stages}")

    def sem(self, name):
        if name not in self.sems:
            self.sems[name] = self.ctx.enter_context(self.nc.semaphore(name))
            self.given[name] = self.base[name] = 0
        return self.sems[name]

    def inc(self, name, n=1):
        s = self.sem(name)
        self.given[name] += n * self.times
        return s, n

    def at(self, name, n):
        return self.sem(name), self.base[name] + n

    def end_stage(self):
        self.base = dict(self.given)

    def step(self, eng, ins, name):
        s, n = self.inc(name)
        ins.then_inc(s, n)
        eng.wait_ge(s, self.given[name])

    def start_moves(self, sp, pairs):
        for dst, src in pairs:
            sp.dma_start(dst, src).then_inc(*self.inc("moved_aside", 16))

    def end_moves(self, sp, pairs):
        if pairs:
            sp.wait_ge(*self.at("moved_aside", 16 * len(pairs)))

    def constants(self, names, where):
        at, pairs = 0, []
        for name in names:
            w = CONSTS[name]
            pairs.append((where[:, at:at + w], self.dram["consts"][:, CONST_AT[name]:CONST_AT[name] + w]))
            self.const[name] = where[:, at:at + w]
            at += w
        return pairs

    def col(self, name, i=0, n=1):
        return self.cols[:, COL_AT[name] + i:COL_AT[name] + i + n]

    def plan(self, name, layer, first=0, last=None):
        at = 0
        for i, (r0, r1, c0, c1) in enumerate(PARTS[name][:last]):
            n = (r1 - r0) * (c1 - c0)
            if i >= first:
                self.stream.append((self.dram[name][layer][at:at + n], (r1 - r0) // P, c1 - c0))
            at += n

    def slot(self, i):
        _, kc, w = self.stream[i]
        return self.ring[:, i % RING, 0:kc * w].rearrange("p (k w) -> p k w", k=kc)

    def load_next(self, sp):
        self.load(sp, self.issued)
        self.issued += 1

    def load(self, sp, i):
        if i < len(self.stream):
            src, kc, w = self.stream[i]
            sp.dma_start(self.ring[:, i % RING, 0:kc * w], src.rearrange("(p n) -> p n", p=P)).then_inc(
                self.sem(f"slot{i % RING}_landed"), 16)

    def landed(self, i):
        return self.sem(f"slot{i % RING}_landed"), 16 * (i // RING + 1)


def evacuate(K, side, out, in_, scale=None, bias=None):
    nc = K.nc
    if side == "act":
        kw = {}
        if scale is not None:
            kw["scale"] = scale
        if bias is not None:
            kw["bias"] = bias
        return nc.scalar.activation(out, in_, ACT.Identity if kw else ACT.Copy, **kw)
    if scale is None and bias is None:
        return nc.vector.tensor_copy(out, in_)
    if bias is None:
        return nc.vector.tensor_scalar(out, in_, scale, None, ALU.mult)
    if scale is None:
        return nc.vector.tensor_scalar(out, in_, bias, None, ALU.add)
    return nc.vector.tensor_scalar(out, in_, scale, bias, ALU.mult, ALU.add)


def gemm_stage(K, npieces, jobs, name="gemm", feed=None, also=(), before=None):
    nc, first = K.nc, K.cursor
    uses = [max(j for j, job in enumerate(jobs) if i in job["pieces"]) for i in range(npieces)]
    sides = [job.get("only") or ("act", "dve")[j % 2] for j, job in enumerate(jobs)]
    turn = [sides[:j + 1].count(sides[j]) for j in range(len(jobs))]

    def bank_of(job, j):
        p0, p1 = job["rows"]
        return K.ps[p0:p1, j % NBANK, 0:job["n"]]

    with K.block(name) as block:
        @block.sync
        def _(sp):
            K.start_moves(sp, also)
            for i in range(npieces):
                if feed is None or i < feed:
                    sp.wait_ge(*K.at("products_done", uses[i] + 1))
                    K.load_next(sp)
            K.end_moves(sp, also)

        @block.tensor
        def _(pe):
            seen = set()

            def await_piece(i):
                if i not in seen:
                    seen.add(i)
                    pe.wait_ge(*K.landed(first + i))
            for j, job in enumerate(jobs):
                pieces = job["pieces"]
                if j >= NBANK:
                    pe.wait_ge(*K.at(sides[j - NBANK] + "_evacuated", turn[j - NBANK]))
                if "emit" in job:
                    last = job["emit"](j % NBANK)
                else:
                    terms = job["mm"]([K.slot(first + i) for i in job["pieces"]])
                    for n, (lhsT, rhs) in enumerate(terms):
                        if pieces:
                            await_piece(pieces[n * len(pieces) // len(terms)])
                        if j == 0 and before and before["ready"] and n < KD:
                            pe.wait_ge(*before["ready"](n))
                        last = nc.tensor.matmul(bank_of(job, j), lhsT, rhs, start=n == 0, stop=n == len(terms) - 1)
                last.then_inc(*K.inc("products_done"))

        @block.scalar
        def _(act):
            if before:
                before["act"](act)
            for j, job in enumerate(jobs):
                if sides[j] == "act":
                    act.wait_ge(*K.at("products_done", j + 1))
                    job["evac"]("act", bank_of(job, j), act).then_inc(*K.inc("act_evacuated"))

        @block.vector
        def _(dve):
            if before:
                before["dve"](dve)
            for j, job in enumerate(jobs):
                if sides[j] == "dve":
                    dve.wait_ge(*K.at("products_done", j + 1))
                    job["evac"]("dve", bank_of(job, j), dve).then_inc(*K.inc("dve_evacuated"))
        @block.gpsimd
        def _(pool):
            if before and "pool" in before:
                before["pool"](pool)
    K.cursor += npieces
    K.end_stage()


def feature_job(K, piece, c0, width, rhs, out, p0=0, scale=None, evac=None, only=None):
    n = rhs.shape[-1]
    return dict(
        pieces=[piece], rows=(p0, p0 + width), n=n, only=only,
        mm=lambda slots: [(slots[0][:, k, c0:c0 + width], rhs[:, k, :]) for k in range(slots[0].shape[1])],
        evac=evac or (lambda side, ps, eng: evacuate(K, side, out, ps, scale=scale)))


def token_job(K, piece, cols, lhs, t, out):
    return dict(
        pieces=[piece], rows=(0, P), n=out.shape[-1], only=None,
        mm=lambda slots: [(lhs[:, k, t * P:(t + 1) * P], cols(slots[0], k)) for k in range(slots[0].shape[1])],
        evac=lambda side, ps, eng: evacuate(K, side, out, ps))


def mod_stage(K, sil, bias, late, also=()):
    nc, first = K.nc, K.cursor
    p0, p1 = ((0, EARLY), (EARLY, 12))[late]
    n = p1 - p0
    rows = K.arena[:, 0:n * P].rearrange("p (n c) -> p n c", n=n)
    with K.block("modulation") as block:
        @block.sync
        def _(sp):
            K.start_moves(sp, also)
            while K.issued < first + RING:
                K.load_next(sp)
            for i in range(n):
                sp.wait_ge(*K.at("rows_done", i + 1))
                K.load_next(sp)
            K.end_moves(sp, also)

        @block.tensor
        def _(pe):
            def transpose(i):
                pe.wait_ge(*K.at("rows_kept", i + 1))
                if i >= 4:
                    pe.wait_ge(*K.at("columns_kept", i - 3))
                nc.tensor.transpose(K.ps[:, 4 + i % 4, 0:P], rows[:, i, :], K.ident).then_inc(*K.inc("columns_done"))
            for i in range(n):
                pe.wait_ge(*K.landed(first + i))
                if i >= 4:
                    pe.wait_ge(*K.at("rows_kept", i - 3))
                w = K.slot(first + i)
                for k in range(KD):
                    for j in range(4):
                        last = nc.tensor.matmul(K.ps[32 * j:32 * j + 32, i % 4, 0:P], sil[:, k, :],
                                                w[:, k, j * P:(j + 1) * P], start=k == 0, stop=k == KD - 1)
                last.then_inc(*K.inc("rows_done"))
                if i:
                    transpose(i - 1)
            transpose(n - 1)

        @block.scalar
        def _(act):
            for i in range(n):
                act.wait_ge(*K.at("rows_done", i + 1))
                nc.scalar.activation(rows[:, i, :], K.ps[:, i % 4, 0:P], ACT.Copy).then_inc(*K.inc("rows_kept"))

        @block.vector
        def _(dve):
            for i in range(n):
                dve.wait_ge(*K.at("columns_done", i + 1))
                got = K.ps[:, 4 + i % 4, 0:P].rearrange("p (j r) -> p r j", r=32)
                at = slice(4 * (p0 + i), 4 * (p0 + i) + 4)
                nc.vector.tensor_tensor(K.modcol[:, 0, at], got[:, 0, :], bias[:, at], ALU.add)
                nc.vector.tensor_tensor(K.modcol[:, 1, at], got[:, 1, :], bias[:, at], ALU.add)\
                    .then_inc(*K.inc("columns_kept"))
            dve.wait_ge(*K.at("columns_kept", n))
            j = (1, 4)[late]
            nc.vector.tensor_scalar(K.modcol[:, :, 8 * j:8 * j + 8], K.modcol[:, :, 8 * j:8 * j + 8], 1.0, None, ALU.add)
    K.cursor += n
    K.end_stage()


def mod(K, which, seg, k):
    return K.modcol[:, seg, 8 * which + k:8 * which + k + 1]


def modulating(K, shift, scale, n_seg):
    nc = K.nc

    def act_part(act):
        for k in range(0, KD, 2):
            for s in range(n_seg):
                last = nc.scalar.activation(K.HT[:, k, SEGS[s]], K.XT[:, k, SEGS[s]], ACT.Identity,
                                            bias=mod(K, shift, s, k), scale=mod(K, scale, s, k))
            last.then_inc(*K.inc("even_modulated"))

    def dve_part(dve):
        for k in range(1, KD, 2):
            for s in range(n_seg):
                last = nc.vector.tensor_scalar(K.HT[:, k, SEGS[s]], K.XT[:, k, SEGS[s]],
                                               mod(K, scale, s, k), mod(K, shift, s, k), ALU.mult, ALU.add)
            last.then_inc(*K.inc("odd_modulated"))
    return dict(act=act_part, dve=dve_part, ready=lambda k: K.at(("even_modulated", "odd_modulated")[k % 2], k // 2 + 1))


def norm_stage(K, groups, work, centre=False, also=(), after=ACT.Identity, vector_work=None):
    nc = K.nc
    sq = work[:, 0:4 * TT].rearrange("p (b n) -> p b n", b=4)
    root = work[:, 4 * TT:4 * TT + 4 * P].rearrange("p (g n) -> p g n", g=4)
    means = work[:, 5 * TT:5 * TT + 4 * P].rearrange("p (g n) -> p g n", g=4)
    G = len(groups)
    firsts = [sum(len(g["src"]) for g in groups[:i]) for i in range(G + 1)]
    outs = [sum(len(g["out"]) for g in groups[:i]) for i in range(G + 1)]
    blocks = [s for grp in groups for s in grp["src"]]
    sides = ["dve" if G == 1 and not centre and b % 2 else "act" for b in range(len(blocks))]
    mean_bank = (1, 2, 5, 6)

    def sum_bank(g):
        return 3 + g % 2

    def spread_bank(g):
        return 5 + g % 3

    def square(side, b):
        s = blocks[b]
        out = sq[0:s.shape[0], b % 4, 0:s.shape[1]]
        ins = nc.scalar.activation(out, s, ACT.Square) if side == "act" else nc.vector.tensor_tensor(out, s, s, ALU.mult)
        ins.then_inc(*K.inc("squares_" + side))

    with K.block("norm") as block:
        @block.sync
        def _(sp):
            K.start_moves(sp, also)
            K.end_moves(sp, also)

        @block.tensor
        def _(pe):
            def add_up(grp, bank, c0, block, i):
                half = grp["ones"][:, 48:80]
                for c in range(4):
                    t = c * P % grp["src"][0].shape[1]
                    last = nc.tensor.matmul(K.ps[32 * c:32 * c + 32, bank, c0:c0 + P], half, block[:, t:t + P],
                                            start=i == 0, stop=i == len(grp["src"]) - 1)
                return last

            def spread(grp, rows, bank):
                for c in range(grp["src"][0].shape[1] // P):
                    for h in range(2):
                        pick = K.ident[:, 32 * c + 16 * h:32 * c + 16 * h + 1].broadcast_to([P, 64])
                        last = nc.tensor.matmul(K.ps[64 * h:64 * h + 64, bank, c * P:(c + 1) * P], pick, rows, start=True, stop=True)
                return last

            if centre:
                for g, grp in enumerate(groups):
                    for i, s in enumerate(grp["src"]):
                        last = add_up(grp, 0, g * P, s, i)
                last.then_inc(*K.inc("sums_done"))
                pe.wait_ge(*K.at("means_done", 1))
                for g in range(G):
                    spread(groups[g], means[:, g], mean_bank[g]).then_inc(*K.inc("means_spread"))
            for g in range(G + 2):
                if g < G:
                    grp = groups[g]
                    if g >= 2:
                        pe.wait_ge(*K.at("roots_done", g - 1))
                    for i, s in enumerate(grp["src"]):
                        b = firsts[g] + i
                        pe.wait_ge(*K.at("squares_" + sides[b], sides[:b + 1].count(sides[b])))
                        add_up(grp, sum_bank(g), 0, sq[0:s.shape[0], b % 4], i).then_inc(*K.inc("squares_summed"))
                if g >= 2:
                    j = g - 2
                    pe.wait_ge(*K.at("inverted", j + 1))
                    if j >= 3:
                        pe.wait_ge(*K.at("scaled", outs[j - 2]))
                    spread(groups[j], root[:, j % 4], spread_bank(j)).then_inc(*K.inc("roots_spread"))

        @block.scalar
        def _(act):
            nc.scalar.activation(K.small[:, 44:45], K.eps["zero"], ACT.Sqrt)
            if centre:
                act.wait_ge(*K.at("sums_done", 1))
                nc.scalar.mul(means[:, 0:G], K.ps[:, 0, 0:G * P].rearrange("p (g n) -> p g n", g=G), -groups[0]["inv"])\
                    .then_inc(*K.inc("means_done"))
            for g in range(G + 1):
                if g < G:
                    for b in range(firsts[g], firsts[g + 1]):
                        if sides[b] == "act":
                            if centre:
                                act.wait_ge(*K.at("centred", b + 1))
                            if b >= 4:
                                act.wait_ge(*K.at("squares_summed", b - 3))
                            square("act", b)
                if g >= 1:
                    j = g - 1
                    if j >= 4:
                        act.wait_ge(*K.at("roots_spread", j - 3))
                    act.wait_ge(*K.at("squares_summed", firsts[j + 1]))
                    nc.scalar.activation(root[:, j % 4], K.ps[:, sum_bank(j), 0:P], ACT.Sqrt, bias=groups[j]["eps"],
                                         scale=groups[j]["inv"]).then_inc(*K.inc("roots_done"))
            for i, (dst, _, _, _, bias) in enumerate(o for grp in groups for o in grp["out"]):
                if bias is not None:
                    act.wait_ge(*K.at("scaled", i + 1))
                    nc.scalar.activation(dst, dst, after, bias=bias)

        @block.vector
        def _(dve):
            if vector_work:
                vector_work(dve)
            if centre:
                for g, grp in enumerate(groups):
                    dve.wait_ge(*K.at("means_spread", g + 1))
                    for s in grp["src"]:
                        nc.vector.tensor_tensor(s, s, K.ps[0:s.shape[0], mean_bank[g], 0:s.shape[1]], ALU.add).then_inc(*K.inc("centred"))
            for b in range(len(blocks)):
                if sides[b] == "dve":
                    if b >= 4:
                        dve.wait_ge(*K.at("squares_summed", b - 3))
                    square("dve", b)
            for g in range(G + 1):
                if g < G:
                    dve.wait_ge(*K.at("roots_done", g + 1))
                    nc.vector.reciprocal(root[:, g % 4], root[:, g % 4]).then_inc(*K.inc("inverted"))
                if g >= 1:
                    j = g - 1
                    dve.wait_ge(*K.at("roots_spread", j + 1))
                    if centre and j == 0:
                        dve.wait_ge(*K.at("centred", firsts[G]))
                    for dst, src, cs, gain, _ in groups[j]["out"]:
                        r = K.ps[0:src.shape[0], spread_bank(j), cs]
                        if gain is None:
                            ins = nc.vector.tensor_tensor(dst, src, r, ALU.mult)
                        else:
                            ins = nc.vector.scalar_tensor_tensor(out=dst, in0=src, scalar=gain, in1=r, op0=ALU.mult, op1=ALU.mult)
                        ins.then_inc(*K.inc("scaled"))
    K.end_stage()


def attention_stage(K, units, work, passes, name="attention", also=()):
    nc, U = K.nc, len(units)
    nb = 3
    nt = 3 - passes
    E = work[:, 0:3072].rearrange("p (u s n) -> p u s n", u=nb, s=2)
    AT = work[:, 3072:4096].rearrange("p (u k q) -> p u k q", u=2, k=4)
    stat = K.small[:, 0:3 * 2 * nb].rearrange("p (u s c) -> p u s c", u=nb, s=2)

    def scores(i, s):
        return passes * (i % nb) + s

    def transposes(i):
        return passes * nb + i % nt

    def values(i):
        return passes * nb + nt + i % nt

    with K.block(name) as block:
        @block.sync
        def _(sp):
            K.start_moves(sp, also)
            K.end_moves(sp, also)

        @block.tensor
        def _(pe):
            for i in range(U + 3):
                if i < U:
                    u = units[i]
                    if i >= nb:
                        if u["bias"] is not None:
                            pe.wait_ge(*K.at("biased", i - nb + 1))
                        else:
                            pe.wait_ge(*K.at("exps_done", passes * (i - nb + 1)))
                    for s in range(passes):
                        last = nc.tensor.matmul(K.ps[:, scores(i, s), 0:u["k"].shape[-1]], u["q"][s], u["k"], start=True, stop=True)
                    last.then_inc(*K.inc("scores_done"))
                if 2 <= i <= U + 1:
                    j = i - 2
                    u = units[j]
                    pe.wait_ge(*K.at("probs_done", j + 1))
                    if j >= nt:
                        pe.wait_ge(*K.at("probsT_done", j - nt + 1))
                    for c in range(len(u["v"])):
                        last = nc.tensor.transpose(K.ps[:, transposes(j), c * P:(c + 1) * P], E[:, j % nb, 0, c * P:(c + 1) * P], K.ident)
                    last.then_inc(*K.inc("transposed"))
                if i >= 3:
                    j = i - 3
                    u = units[j]
                    pe.wait_ge(*K.at("probsT_done", j + 1))
                    if j >= nt:
                        pe.wait_ge(*K.at("out_kept", j - nt + 1))
                    for c, v in enumerate(u["v"]):
                        last = nc.tensor.matmul(K.ps[u["rows"][0]:u["rows"][1], values(j), 0:P], v, AT[:, j % 2, c, :],
                                                start=c == 0, stop=c == len(u["v"]) - 1)
                    last.then_inc(*K.inc("values_done"))

        @block.scalar
        def _(act):
            for i in range(U + 2):
                if i < U:
                    u, b = units[i], i % nb
                    n = u["k"].shape[-1]
                    act.wait_ge(*K.at("max_done", i + 1))
                    if i >= nb:
                        act.wait_ge(*K.at("transposed", i - nb + 1))
                    for s in range(passes):
                        src = E[:, b, 1, 0:n] if u["bias"] is not None else K.ps[:, scores(i, s), 0:n]
                        nc.scalar.activation(E[:, b, s, 0:n], src, ACT.Exp, bias=stat[:, b, s, 0:1],
                                             accum_out=stat[:, b, s, 1:2]).then_inc(*K.inc("exps_done"))
                if i >= 2:
                    j = i - 2
                    u = units[j]
                    act.wait_ge(*K.at("transposed", j + 1))
                    if j >= 2:
                        act.wait_ge(*K.at("values_done", j - 1))
                    n = P * len(u["v"])
                    nc.scalar.activation(AT[:, j % 2, 0:len(u["v"]), :].rearrange("p k q -> p (k q)"), K.ps[:, transposes(j), 0:n],
                                         ACT.Copy).then_inc(*K.inc("probsT_done"))

        @block.vector
        def _(dve):
            for i in range(U + 4):
                if i < U:
                    u, b = units[i], i % nb
                    n = u["k"].shape[-1]
                    dve.wait_ge(*K.at("scores_done", i + 1))
                    if i >= nb:
                        dve.wait_ge(*K.at("exps_done", passes * (i - nb + 1)))
                    if u["bias"] is not None:
                        if n > T:
                            nc.vector.tensor_copy(E[:, b, 1, T:n], K.ps[:, scores(i, 0), T:n])
                        K.step(dve, nc.vector.tensor_tensor(E[:, b, 1, 0:T], K.ps[:, scores(i, 0), 0:T], u["bias"], ALU.add), "biased")
                    for s in range(passes):
                        src = E[:, b, 1, 0:n] if u["bias"] is not None else K.ps[:, scores(i, s), 0:n]
                        last = nc.vector.tensor_reduce(stat[:, b, s, 0:1], src, AX, ALU.max, negate=True)
                    last.then_inc(*K.inc("max_done"))
                if i >= 4:
                    j = i - 4
                    u = units[j]
                    dve.wait_ge(*K.at("values_done", j + 1))
                    nc.vector.tensor_copy(u["out"], K.ps[u["rows"][0]:u["rows"][1], values(j), 0:P]).then_inc(*K.inc("out_kept"))
                if 1 <= i <= U:
                    j = i - 1
                    u, b = units[j], j % nb
                    n = u["k"].shape[-1]
                    dve.wait_ge(*K.at("exps_done", passes * i))
                    K.step(dve, nc.vector.reciprocal(stat[:, b, 0:passes, 2:3], stat[:, b, 0:passes, 1:2]), "dve_step")
                    for s in range(passes):
                        if u["weight"][s] is not None:
                            K.step(dve, nc.vector.tensor_tensor(stat[:, b, s, 2:3], stat[:, b, s, 2:3], u["weight"][s], ALU.mult), "dve_step")
                    probs = E[:, b, 0, 0:n]
                    last = nc.vector.tensor_scalar(probs, probs, stat[:, b, 0, 2:3], None, ALU.mult)
                    for s in range(1, passes):
                        K.step(dve, last, "dve_step")
                        last = nc.vector.scalar_tensor_tensor(out=probs, in0=E[:, b, s, 0:n], scalar=stat[:, b, s, 2:3],
                                                              in1=probs, op0=ALU.mult, op1=ALU.add)
                    last.then_inc(*K.inc("probs_done"))
    K.end_stage()


def gated_add(K, gate, fb, n_seg):
    nc = K.nc

    def evac(side, ps, dve):
        for s in range(n_seg):
            last = nc.vector.scalar_tensor_tensor(out=K.XT[:, fb, SEGS[s]], in0=ps[:, SEGS[s]], scalar=mod(K, gate, s, fb),
                                                  in1=K.XT[:, fb, SEGS[s]], op0=ALU.mult, op1=ALU.add)
        return last
    return evac


def out_proj_stage(K, gate, n_seg, before=None):
    n = n_seg * T
    jobs = [feature_job(K, fb // 4, fb % 4 * P, P, K.HT[:, :, 0:n], None, evac=gated_add(K, gate, fb, n_seg), only="dve")
            for fb in range(KD)]
    gemm_stage(K, 2, jobs, "out_projection", before=before)


def clear_other_halves(K, q2):
    nc = K.nc

    def work(pool):
        nc.gpsimd.memset(q2[64:128, 0], 0.0)
        nc.gpsimd.memset(q2[0:64, 1], 0.0)
    return work


def times_alpha(K, n):
    nc = K.nc

    def act_part(act):
        for k in range(KD):
            nc.scalar.mul(K.XT[:, k, 0:n], K.XT[:, k, 0:n], ALPHA).then_inc(*K.inc("times_alpha"))
    return dict(act=act_part, dve=lambda dve: dve.wait_ge(*K.at("times_alpha", KD)), ready=None)


def layer_norm_stage(K, n, g, b):
    src = [K.XT[:, k, 0:n] for k in range(KD)]
    norm_stage(K, [dict(src=src, ones=K.ones, inv=1.0 / D, eps=K.eps["ln"],
                        out=[(s, s, slice(0, n), K.col(g, k), K.col(b, k)) for k, s in enumerate(src)])],
               K.arena, centre=True)


def rope_stage(K, blocks, swap, cos, sin, tmp):
    nc, B, n = K.nc, len(blocks), T
    p = blocks[0].shape[0]
    with K.block("rope") as block:
        @block.tensor
        def _(pe):
            for i, q in enumerate(blocks):
                if i >= NBANK:
                    pe.wait_ge(*K.at("swapped_times_sin", i - NBANK + 1))
                nc.tensor.matmul(K.ps[0:p, i % NBANK, 0:n], swap, q, start=True, stop=True).then_inc(*K.inc("swapped"))

        @block.gpsimd
        def _(pool):
            for i, q in enumerate(blocks):
                pool.wait_ge(*K.at("swapped", i + 1))
                nc.gpsimd.tensor_tensor(q, q, cos, ALU.mult).then_inc(*K.inc("times_cos"))

        @block.vector
        def _(dve):
            for i in range(len(blocks) + 1):
                if i < len(blocks):
                    if i >= 2:
                        dve.wait_ge(*K.at("rotated", i - 1))
                    dve.wait_ge(*K.at("swapped", i + 1))
                    nc.vector.tensor_tensor(tmp[0:p, i % 2 * n:(i % 2 + 1) * n], K.ps[0:p, i % NBANK, 0:n], sin, ALU.mult)\
                        .then_inc(*K.inc("swapped_times_sin"))
                if i:
                    q, t = blocks[i - 1], tmp[0:p, (i - 1) % 2 * n:((i - 1) % 2 + 1) * n]
                    dve.wait_ge(*K.at("swapped_times_sin", i))
                    dve.wait_ge(*K.at("times_cos", i))
                    nc.vector.tensor_tensor(q, q, t, ALU.add).then_inc(*K.inc("rotated"))
    K.end_stage()


def prologue(K):
    nc, d = K.nc, K.dram
    lam_in = K.arena[:, 0:2 * 256].rearrange("p (l a n) -> p l a n", l=2, a=4)
    lam_prod = K.arena[:, 512:768].rearrange("p (l a n) -> p (l a) n", l=2, a=2)
    lam_sum = K.small[:, 24:28]
    lam_exp = K.small[:, 28:32].rearrange("p (l a) -> p l a", l=2)
    K.neg_lam = [K.small[:, 32:33], K.small[:, 33:34]]
    K.eps = {n: K.small[:, 34 + i:35 + i] for i, n in enumerate(("ln", "rms", "gn", "kk", "zero"))}
    K.subln = [K.small[:, 40:41], K.small[:, 41:42]]
    K.q_gain, K.na_gain = K.small[:, 42:43], K.small[:, 43:44]
    sig = K.arena[:, 1024:1024 + 32].rearrange("p (b v k) -> p b v k", b=2, v=2)
    lam_init = [0.8 - 0.6 * math.exp(-0.3 * l) for l in range(DEPTH)]
    with K.block("prologue") as block:
        @block.sync
        def _(sp):
            sp.dma_start(K.cols[:, :], d["cols"]).then_inc(*K.inc("constants_landed", 16))
            sp.dma_start(K.base_consts[:, :], d["consts"][:, 0:384]).then_inc(*K.inc("constants_landed", 16))
            sp.dma_start(K.arena[:, 0:512], d["diff_lambda"].partition_broadcast(P)).then_inc(*K.inc("constants_landed", 16))
            for _ in range(EARLY):
                K.load_next(sp)
            sp.wait_ge(*K.at("constants_landed", 3 * 16))

        @block.gpsimd
        def _(pool):
            nc.gpsimd.memset(K.sil[:, :, :, :], 0.0).then_inc(*K.inc("cleared"))
            for n, v in (("ln", 1e-5), ("rms", 1e-6), ("gn", 64e-5), ("kk", 1e-12), ("zero", 0.0)):
                nc.gpsimd.memset(K.eps[n], v)

        @block.scalar
        def _(act):
            act.wait_ge(*K.at("constants_landed", 3 * 16))
            act.wait_ge(*K.at("cleared", 1))
            for b in range(2):
                for v in range(2):
                    nc.scalar.activation(K.sil[:, b, :, v], K.col("c", 8 * (2 * b + v), 8), ACT.Silu)
            act.wait_ge(*K.at("lam_summed", 1))
            nc.scalar.activation(lam_exp, lam_sum.rearrange("p (l a) -> p l a", l=2), ACT.Exp).then_inc(*K.inc("lam_exps"))

        @block.vector
        def _(dve):
            dve.wait_ge(*K.at("constants_landed", 3 * 16))
            for l in range(DEPTH):
                for a in range(2):
                    last = nc.vector.tensor_tensor(lam_prod[:, 2 * l + a, :], lam_in[:, l, 2 * a, :], lam_in[:, l, 2 * a + 1, :], ALU.mult)
            K.step(dve, last, "dve_step")
            nc.vector.tensor_reduce(lam_sum, lam_prod, AX, ALU.add).then_inc(*K.inc("lam_summed"))
            for l in range(DEPTH):
                nc.vector.tensor_scalar(K.subln[l], K.col(f"subln{l}"), 1.0 - lam_init[l], None, ALU.mult)
            nc.vector.tensor_scalar(K.q_gain, K.col("q_g"), 96.0 ** -0.5, None, ALU.mult)
            nc.vector.tensor_scalar(K.na_gain, K.col("na_q"), 64.0 ** -0.5, None, ALU.mult)
            dve.wait_ge(*K.at("lam_exps", 1))
            for l in range(DEPTH):
                K.step(dve, nc.vector.tensor_tensor(K.neg_lam[l], lam_exp[:, l, 1:2], lam_exp[:, l, 0:1], ALU.subtract), "dve_step")
                nc.vector.tensor_scalar(K.neg_lam[l], K.neg_lam[l], -lam_init[l], None, ALU.add)
    K.end_stage()


def first_layer(K, l):
    nc, A, HT = K.nc, K.arena, K.HT
    n_seg = 1 if l == DEPTH - 1 else 2
    n = n_seg * T
    q = A[:, 0:2048].rearrange("p (h t) -> p h t", h=4)
    k = A[:, 2048:4096].rearrange("p (h t) -> p h t", h=4)
    v = A[:, 4096:6144].rearrange("p (t e) -> p t e", t=4)
    cv = A[:, 6144:9216].rearrange("p (b t) -> p b t", b=6)
    f = A[:, 9216:10240].rearrange("p (t m) -> p t m", t=4)
    q2 = A[:, 10240:14336].rearrange("p (s h t) -> p s h t", s=2, h=4)
    tmp = A[:, 14336:16384]
    table = A[:, 16512:18432]

    tokens = [(K.XT[:, :, seg], K.dram[name].rearrange("(k p) t -> p k t", p=P)) for name, seg in (("x", X), ("ctx", C))]
    mod_stage(K, K.sil[:, 0], K.col(f"b_mod{l}", 0, 48), 0,
              also=K.constants(["swap1", "cos1", "sin1", "cn", "sn", "cm", "sm"], table) + (tokens if l == 0 else []))

    jobs = [feature_job(K, 0, h * P, P, HT[:, :, 0:n], q[:, h, 0:n], scale=0.125) for h in range(4)]
    jobs += [feature_job(K, 1, h * P, P, HT, k[:, h, :]) for h in range(4)]
    jobs += [token_job(K, 2, lambda w, i: w[:, i, :], HT, t, v[:, t, :]) for t in range(4)]
    jobs += [feature_job(K, 3, b * P, P, HT[:, :, 0:n], cv[:, b, 0:n]) for b in range(4)]
    jobs += [feature_job(K, 4, b * P, P, HT[:, :, 0:n], cv[:, 4 + b, 0:n]) for b in range(2)]
    jobs += [token_job(K, 4, lambda w, i: w[:, i, 256:512], HT, t, f[:, t, :]) for t in range(2 * n_seg)]
    gemm_stage(K, 5, jobs, "in_projection", before=dict(modulating(K, 0, 1, 2), pool=clear_other_halves(K, q2)))

    rope_stage(K, [b[:, h, X] for b in (q, k) for h in range(4)], K.const["swap1"], K.const["cos1"], K.const["sin1"], tmp)
    conv_fourier_stage(K, l, n_seg, cv, f, q, q2, tmp)

    units = [dict(q=[q2[:, s, h, c * P:(c + 1) * P] for s in range(2)], k=k[:, h, 0:TT] if c < 2 else k[:, h, C],
                  v=[v[:, t, h * P:(h + 1) * P] for t in (range(4) if c < 2 else range(2, 4))], bias=None, rows=(0, P),
                  out=HT[:, h, c * P:(c + 1) * P], weight=[None, K.neg_lam[l]])
             for h in range(4) for c in range(2 * n_seg)]
    attention_stage(K, units, A[:, 6144:10240], 2, "differential_attention")
    norm_stage(K, [dict(src=[HT[:, h, 0:n]], ones=K.ones, inv=1.0 / P, eps=K.eps["ln"],
                        out=[(HT[:, h, 0:n], HT[:, h, 0:n], slice(0, n), K.subln[l], None)]) for h in range(4)], A[:, 0:3072])
    mod_stage(K, K.sil[:, 0], K.col(f"b_mod{l}", 0, 48), 1)
    out_proj_stage(K, 2, n_seg, before=times_alpha(K, n))
    layer_norm_stage(K, n, f"ln1_g{l}", f"ln1_b{l}")

    hidden = A[:, 0:16384].rearrange("p (b t) -> p b t", b=32)
    jobs = [feature_job(K, fb // 4, fb % 4 * P, P, HT[:, :, 0:n], None, evac=squared_relu(K, hidden[:, fb, 0:n])) for fb in range(32)]
    gemm_stage(K, 8, jobs, "mlp_up", before=modulating(K, 3, 4, n_seg))
    jobs = []
    for fb in range(KD):
        pieces = [fb // 4 * 4 + r for r in range(4)]
        c0 = fb % 4 * P
        jobs.append(dict(pieces=pieces, rows=(0, P), n=n, only="dve", evac=gated_add(K, 5, fb, n_seg),
                         mm=lambda w, c0=c0: [(w[r][:, i, c0:c0 + P], hidden[:, 8 * r + i, 0:n]) for r in range(4) for i in range(KD)]))
    gemm_stage(K, 8, jobs, "mlp_down", before=times_alpha(K, n))
    layer_norm_stage(K, n, f"ln2_g{l}", f"ln2_b{l}")


def squared_relu(K, out):
    nc = K.nc

    def evac(side, ps, eng):
        if side == "act":
            K.step(eng, nc.scalar.activation(out, ps, ACT.Relu), "act_step")
            return nc.scalar.activation(out, out, ACT.Square)
        K.step(eng, nc.vector.tensor_scalar(out, ps, 0.0, None, ALU.max), "dve_step")
        return nc.vector.tensor_tensor(out, out, out, ALU.mult)
    return evac


def conv_fourier_stage(K, l, n_seg, cv, f, q, q2, tmp):
    nc, HT = K.nc, K.HT
    n = n_seg * T
    cn = K.const["cn"].rearrange("p (t k) -> p t k", t=2)
    sn = K.const["sn"].rearrange("p (t k) -> p t k", t=2)
    first = tmp.rearrange("p (b t) -> p b t", b=4)
    with K.block("conv_fourier") as block:
        @block.tensor
        def _(pe):
            for b in range(4):
                for s in range(n_seg):
                    for t in range(2):
                        last = nc.tensor.matmul(K.ps[:, b, SEGS[s]], f[:, 2 * s + t, b % 2 * P:(b % 2 + 1) * P],
                                                (cn, sn)[b // 2][:, t, :], start=t == 0, stop=t == 1)
                last.then_inc(*K.inc("tokens_transformed"))
            for b in range(2):
                pe.wait_ge(*K.at("transform_kept", 4))
                nc.tensor.matmul(K.ps[:, 4 + b, 0:n], K.const["cm"], first[:, b, 0:n], start=True, stop=False)
                nc.tensor.matmul(K.ps[:, 4 + b, 0:n], K.const["sm"], first[:, 2 + b, 0:n], start=False, stop=True)\
                    .then_inc(*K.inc("features_transformed"))

        @block.scalar
        def _(act):
            nc.scalar.activation(q2[64:128, 1, :, 0:n], q[64:128, :, 0:n], ACT.Copy)
            for b in range(4):
                act.wait_ge(*K.at("tokens_transformed", b + 1))
                nc.scalar.activation(first[:, b, 0:n], K.ps[:, b, 0:n], ACT.Copy).then_inc(*K.inc("transform_kept"))
            for b in range(2):
                act.wait_ge(*K.at("features_transformed", b + 1))
                nc.scalar.activation(HT[:, 6 + b, 0:n], K.ps[:, 4 + b, 0:n], ACT.Copy)

        @block.gpsimd
        def _(pool):
            nc.gpsimd.tensor_copy(q2[0:64, 0, :, 0:n], q[0:64, :, 0:n])

        @block.vector
        def _(dve):
            for b in range(2):
                w = [K.col(f"conv_w{l}", 2 * i + b) for i in range(3)]
                z, gate, gc, y = cv[:, b, 0:n], cv[:, 2 + b, 0:n], cv[:, 4 + b, 0:n], HT[:, 4 + b, 0:n]
                K.step(dve, nc.vector.tensor_tensor(z, z, gc, ALU.mult), "dve_step")
                K.step(dve, nc.vector.tensor_scalar(y, z, w[1], K.col(f"conv_b{l}", b), ALU.mult, ALU.add), "dve_step")
                zs, ys = (a.rearrange("p (s t) -> p s t", s=n_seg) for a in (z, y))
                for tap, dst, src in ((w[0], slice(1, T), slice(0, T - 1)), (w[2], slice(0, T - 1), slice(1, T))):
                    K.step(dve, nc.vector.scalar_tensor_tensor(out=ys[:, :, dst], in0=zs[:, :, src], scalar=tap, in1=ys[:, :, dst],
                                                               op0=ALU.mult, op1=ALU.add), "dve_step")
                K.step(dve, nc.vector.tensor_tensor(y, y, gate, ALU.mult), "dve_step")
    K.end_stage()


def plan_even(K):
    K.plan("ada_w", 0, 0, EARLY)
    for name in ("ev_w_in", "w_uq", "w_ukv"):
        K.plan(name, 0)
    K.plan("ada_w", 0, EARLY)
    K.plan("ev_w_out", 0)
    K.plan("router", 0)
    plan_experts(K, 2)


def scaled_norm_stage(K, l, which, n_seg, also=()):
    nc = K.nc
    gain = K.col(f"norm{1 if which == 0 else 2}_g{l}", 0, KD)
    with K.block("gain") as block:
        @block.vector
        def _(dve):
            for s in range(n_seg):
                nc.vector.tensor_tensor(K.gain[:, s, :], K.modcol[:, s, 8 * (which + 1):8 * (which + 2)], gain, ALU.mult)
    K.end_stage()
    n = n_seg * T
    norm_stage(K, [dict(src=[K.XT[:, k, 0:n] for k in range(KD)], ones=K.ones, inv=1.0 / D, eps=K.eps["rms"],
                        out=[(K.HT[:, k, SEGS[s]], K.XT[:, k, SEGS[s]], SEGS[s], K.gain[:, s, k:k + 1], mod(K, which, s, k))
                             for k in range(KD) for s in range(n_seg)])], K.arena, also=also)


def even_layer(K):
    nc, A, HT = K.nc, K.arena, K.HT
    q = A[:, 0:4096].rearrange("p (h t) -> p h t", h=8)
    k = A[:, 4096:8192].rearrange("p (h t) -> p h t", h=8)
    v = A[:, 8192:10240].rearrange("p (t e) -> p t e", t=4)
    pad = A[:, 10240:12528].rearrange("p (b s t) -> p b s t", b=4, s=2)
    cq = A[:, 12528:14064].rearrange("p (b t) -> p b t", b=3)
    ckv = A[:, 14064:15088].rearrange("p (b t) -> p b t", b=2)
    kr = A[64:96, 15088:15600]
    table, tmp = A[:, 15600:16240], A[:, 16240:16752]
    a, sg = (A[:, i:i + 2048].rearrange("p (b t) -> p b t", b=4) for i in (0, 2048))

    mod_stage(K, K.sil[:, 1], K.col("ada_b0", 0, 48), 0,
              also=K.constants(["swap2", "cos2", "sin2"], table) + [(K.XT[:, :, C], K.dram["ctx_2"].rearrange("(k p) t -> p k t", p=P))])
    scaled_norm_stage(K, 0, 0, 2)

    jobs = [feature_job(K, 0, b * P, P, HT, cq[:, b, :]) for b in range(3)]
    jobs += [feature_job(K, 1, b * P, P, HT, ckv[:, b, :]) for b in range(2)]
    jobs += [feature_job(K, 1, 256, 32, HT, kr, p0=64)]
    jobs += [feature_job(K, 2, b * P, P, HT, a[:, b, :]) for b in range(4)]
    jobs += [feature_job(K, 3, b * P, P, HT, None, only="act",
                         evac=lambda side, ps, eng, b=b: nc.scalar.activation(sg[:, b, :], ps, ACT.Sigmoid)) for b in range(4)]

    def clear_borders(pool):
        nc.gpsimd.memset(pad[:, :, :, 0:15], 0.0)
        nc.gpsimd.memset(pad[:, :, :, 15 + T:30 + T], 0.0)
    gemm_stage(K, 4, jobs, "even_in_projection", before=dict(act=lambda act: None, dve=lambda dve: None, ready=None, pool=clear_borders))

    def gate(dve):
        for b in range(4):
            nc.vector.tensor_tensor(pad[:, b, :, 15:15 + T], a[:, b, :].rearrange("p (s t) -> p s t", s=2),
                                    sg[:, b, :].rearrange("p (s t) -> p s t", s=2), ALU.mult)
    norm_stage(K, [dict(src=[c[:, b, :] for b in range(m)], ones=K.ones, inv=1.0 / (m * P), eps=K.eps["rms"],
                        out=[(c[:, b, :], c[:, b, :], slice(0, TT), K.col(gain, b), None) for b in range(m)])
                   for c, m, gain in ((cq, 3, "q_norm"), (ckv, 2, "kv_norm"))], A[:, 4096:7168], vector_work=gate)

    jobs = [feature_job(K, 0, h * 96, 96, cq, q[0:96, h, :]) for h in range(8)]
    jobs += [feature_job(K, 1, h * P, 64, ckv, k[0:64, h, :]) for h in range(8)]
    jobs += [token_job(K, 1, lambda w, i: w[:, i, :].rearrange("p (h e) -> p h e", e=P)[:, :, 64:P], ckv, t, v[:, t, :]) for t in range(4)]
    for job in jobs:
        job["only"] = "act"

    def shared_key(act):
        for h in range(8):
            nc.scalar.activation(k[64:96, h, :], kr, ACT.Copy)
    gemm_stage(K, 2, jobs, "mla_up_projection", before=dict(dve=depthwise_taps(K, pad, range(16)), act=shared_key, ready=None))
    norm_stage(K, [dict(src=[b[0:96, h, :]], ones=K.ones[0:96], inv=1.0 / 96, eps=K.eps["rms"],
                        out=[(b[0:96, h, :], b[0:96, h, :], slice(0, TT), gain[0:96], None)])
                   for b, gain in ((q, K.q_gain), (k, K.col("k_g"))) for h in range(8)], A[:, 12528:15600])
    rope_stage(K, [b[0:96, h, X] for b in (q, k) for h in range(8)], K.const["swap2"][0:96, 0:96],
               K.const["cos2"][0:96], K.const["sin2"][0:96], tmp)
    depthwise_stage(K, pad, range(16, 24), range(24, 31), A[:, 12528:13552])
    conv = [HT[:, 4 + b, :] for b in range(4)]
    norm_stage(K, [dict(src=conv, ones=K.ones, inv=1.0 / 512, eps=K.eps["rms"],
                        out=[(c, c, slice(0, TT), K.col("cln_g", b), K.col("cln_b", b)) for b, c in enumerate(conv)])],
               A[:, 12528:15600], centre=True, after=ACT.Silu)

    units = [dict(q=[q[0:96, h, c * P:(c + 1) * P]], k=k[0:96, h, 0:TT] if c < 2 else k[0:96, h, C],
                  v=[v[:, t, h * 64:(h + 1) * 64] for t in (range(4) if c < 2 else range(2, 4))], bias=None,
                  rows=(h % 2 * 64, h % 2 * 64 + 64), out=HT[h % 2 * 64:h % 2 * 64 + 64, h // 2, c * P:(c + 1) * P], weight=[None])
             for h in range(8) for c in range(4)]
    attention_stage(K, units, A[:, 14336:18432], 1, "mla_attention")
    mod_stage(K, K.sil[:, 1], K.col("ada_b0", 0, 48), 1)
    out_proj_stage(K, 2, 2)
    experts(K, 0, 2)


def depthwise_taps(K, pad, taps):
    nc = K.nc
    y = [K.HT[:, 4 + b, :].rearrange("p (s t) -> p s t", s=2) for b in range(4)]

    def work(dve):
        for i, j in enumerate(taps):
            for b in range(4):
                src, w = pad[:, b, :, j:j + T], K.col("dw_w", 4 * j + b)
                if j == 0:
                    ins = nc.vector.tensor_scalar(y[b], src, w, K.col("dw_b", b), ALU.mult, ALU.add)
                else:
                    if i:
                        dve.wait_ge(*K.at("tap_added", 4 * (i - 1) + b + 1))
                    ins = nc.vector.scalar_tensor_tensor(out=y[b], in0=src, scalar=w, in1=y[b], op0=ALU.mult, op1=ALU.add)
                ins.then_inc(*K.inc("tap_added"))
    return work


def depthwise_stage(K, pad, vector_taps, tensor_taps, work):
    nc = K.nc
    diag = work.rearrange("p (n c) -> p n c", n=8)
    pairs = [(b, j) for b in range(4) for j in tensor_taps]
    nt = len(tensor_taps)
    with K.block("depthwise_conv") as block:
        @block.scalar
        def _(act):
            for i, (b, j) in enumerate(pairs):
                if i >= 8:
                    act.wait_ge(*K.at("diagonal_used", i - 7))
                nc.scalar.activation(diag[:, i % 8], K.ident, ACT.Copy, scale=K.col("dw_w", 4 * j + b)).then_inc(*K.inc("diagonal_ready"))

        @block.tensor
        def _(pe):
            for i, (b, j) in enumerate(pairs):
                pe.wait_ge(*K.at("diagonal_ready", i + 1))
                nc.tensor.matmul(K.ps[:, b, :], diag[:, i % 8], pad[:, b, :, j:j + T], start=j == tensor_taps[0],
                                 stop=j == tensor_taps[-1]).then_inc(*K.inc("diagonal_used"))

        @block.vector
        def _(dve):
            depthwise_taps(K, pad, vector_taps)(dve)
            for b in range(4):
                dve.wait_ge(*K.at("tap_added", 4 * len(vector_taps) - 3 + b))
                dve.wait_ge(*K.at("diagonal_used", nt * (b + 1)))
                nc.vector.tensor_tensor(K.HT[:, 4 + b, :], K.HT[:, 4 + b, :], K.ps[:, b, :], ALU.add)
    K.end_stage()


def expert_pieces(group):
    return [(m, e, h) for e in range(group) for m in ("moe_w1", "moe_w3") for h in range(2)] + \
           [("moe_w2", e, h) for h in range(2) for e in range(group)]


def plan_experts(K, group):
    l = 0 if group == 2 else 1
    for g in range(NE // group):
        for m, e, h in expert_pieces(group):
            K.stream.append((K.dram[m][l, g * group + e, h].rearrange("p n -> (p n)"), KD, 512))


def experts(K, l, n_seg):
    nc, A, HT = K.nc, K.arena, K.HT
    n, nt, M = n_seg * T, 2 * n_seg, CAP * n_seg
    group = P // M
    NG = NE // group
    xs_all = A[:, 0:NE * KD * M].rearrange("p (e k s) -> p e k s", e=NE, k=KD)
    NQ = NE // 4
    ys = A[:, 0:NG * D].rearrange("p (q s d) -> p q s d", q=NQ, s=n_seg)
    h_tok = A[:, 8192:8192 + nt * D].rearrange("p (t d) -> p t d", t=nt)
    pick = A[:, 12288:12288 + nt * NE * M].rearrange("p (t e s) -> p t e s", t=nt, e=NE)
    pt = HT[:, :, :].rearrange("p k t -> p (k t)")[:, 0:NQ * n].rearrange("p (q t) -> p q t", q=NQ)

    B = A[:, 16384:18432]
    scaled_norm_stage(K, l, 3, n_seg, also=K.constants(["tri", "iota"], B[:, 0:192]))
    tri, iota = B[:, 0:128], B[:, 128:192]
    logit = B[:, 192:256].rearrange("p (t e) -> p t e", t=4)
    aff = B[:, 256:512].rearrange("p (t s) -> p t s", t=2)
    affT, left = B[0:32, 512:768], B[0:32, 768:1024]
    mask = B[:, 1024:1280]
    maskT = B[:, 1280:1344].rearrange("p (t s) -> p t s", t=2)
    place = B[:, 1344:1408].rearrange("p (t s) -> p t s", t=2)
    top = B[0:32, 1408:1416]
    peak = B[:, 1416:1420]
    router_stage(K, B[:, 1424:1552], logit, nt)
    R = 16 * n_seg
    tok = lambda buf, t: buf[:, t % 2, 16 * (t // 2):16 * (t // 2) + 16]

    with K.block("routing") as block:
        @block.gpsimd
        def _(pool):
            nc.gpsimd.memset(aff, 0.0).then_inc(*K.inc("cleared"))
            nc.gpsimd.memset(mask, 0.0).then_inc(*K.inc("cleared"))
            nc.gpsimd.memset(pick, 0.0).then_inc(*K.inc("cleared"))

        @block.tensor
        def _(pe):
            for t in range(nt):
                for half in range(2):
                    for i in range(4):
                        last = nc.tensor.transpose(K.ps[:, (2 * t + half) % 4, i * P:(i + 1) * P],
                                                   HT[:, 4 * half + i, t * P:(t + 1) * P], K.ident)
                    last.then_inc(*K.inc("h_transposed"))
                    if 2 * t + half + 1 < 2 * nt and 2 * t + half >= 3:
                        pe.wait_ge(*K.at("h_kept", 2 * t + half - 2))
            pe.wait_ge(*K.at("affinities", 1))
            for t in range(2):
                last = nc.tensor.transpose(K.ps[:, 4, t * P:(t + 1) * P], aff[:, t, :], K.ident)
            last.then_inc(*K.inc("affinities_turned"))
            pe.wait_ge(*K.at("masked", 1))
            for t in range(2):
                last = nc.tensor.transpose(K.ps[:, 5, t * P:(t + 1) * P], mask[:, t * P:(t + 1) * P], K.ident)
            last.then_inc(*K.inc("mask_turned"))
            pe.wait_ge(*K.at("mask_kept", 1))
            nc.tensor.matmul(K.ps[:, 6, 0:32], tri, maskT[:, 0, :], start=True, stop=True)
            nc.tensor.matmul(K.ps[:, 7, 0:32], K.ones, maskT[:, 0, :], start=True, stop=False)
            nc.tensor.matmul(K.ps[:, 7, 0:32], tri, maskT[:, 1, :], start=False, stop=True).then_inc(*K.inc("counted"))

        @block.scalar
        def _(act):
            act.wait_ge(*K.at("shifted", 1))
            nc.scalar.activation(logit[:, 0:nt, :], logit[:, 0:nt, :], ACT.Exp).then_inc(*K.inc("logit_exps"))
            for i in range(2 * nt):
                act.wait_ge(*K.at("h_transposed", i + 1))
                nc.scalar.activation(h_tok[:, i // 2, i % 2 * 512:(i % 2 + 1) * 512], K.ps[:, i % 4, :], ACT.Copy)\
                    .then_inc(*K.inc("h_kept"))

        @block.vector
        def _(dve):
            lg = logit[:, 0:nt, :]
            pk = peak[:, 0:nt]
            bc = pk.unsqueeze(2).broadcast_to([P, nt, NE])
            K.step(dve, nc.vector.tensor_reduce(pk, lg, AX, ALU.max), "dve_step")
            nc.vector.tensor_tensor(lg, lg, bc, ALU.subtract).then_inc(*K.inc("shifted"))
            dve.wait_ge(*K.at("logit_exps", 1))
            K.step(dve, nc.vector.tensor_reduce(pk, lg, AX, ALU.add), "dve_step")
            K.step(dve, nc.vector.reciprocal(pk, pk), "dve_step")
            dve.wait_ge(*K.at("cleared", 3))
            for t in range(nt):
                last = nc.vector.tensor_scalar(tok(aff, t), logit[:, t, :], pk[:, t:t + 1], None, ALU.mult)
            last.then_inc(*K.inc("affinities"))
            dve.wait_ge(*K.at("affinities_turned", 1))
            K.step(dve, nc.vector.tensor_copy(left[0:R], K.ps[0:R, 4, 0:T]), "dve_step")
            for _ in range(CAP // 8):
                K.step(dve, nc.vector.max(top[0:R], left[0:R]), "dve_step")
                K.step(dve, nc.vector.match_replace(left[0:R], top[0:R], left[0:R], -1.0), "dve_step")
            nc.vector.tensor_scalar(mask[0:R], left[0:R], 0.0, None, ALU.is_lt).then_inc(*K.inc("masked"))
            dve.wait_ge(*K.at("mask_turned", 1))
            for t in range(2):
                last = nc.vector.tensor_copy(maskT[:, t, :], K.ps[:, 5, t * P:t * P + 32])
            last.then_inc(*K.inc("mask_kept"))
            dve.wait_ge(*K.at("counted", 1))
            dve.wait_ge(*K.at("mask_kept", 1))
            for t in range(2):
                last = nc.vector.tensor_tensor(place[:, t, :], K.ps[:, 6 + t, 0:32], maskT[:, t, :], ALU.mult)
            K.step(dve, last, "dve_step")
            for t in range(nt):
                at = CAP * (t // 2)
                nc.vector.tensor_tensor(pick[:, t, :, at:at + CAP], tok(place, t).unsqueeze(2).broadcast_to([P, NE, CAP]),
                                        iota[:, 0:CAP].unsqueeze(1).broadcast_to([P, NE, CAP]), ALU.is_equal)
    K.end_stage()

    with K.block("gather") as block:
        @block.tensor
        def _(pe):
            for i in range(n_seg * KD):
                s, k = divmod(i, KD)
                if i >= 4:
                    pe.wait_ge(*K.at("gathered_kept", i - 3))
                for t in range(2):
                    last = nc.tensor.matmul(K.ps[:, i % 4, :], h_tok[:, 2 * s + t, k * P:(k + 1) * P],
                                            pick[:, 2 * s + t, :, CAP * s:CAP * s + CAP], start=t == 0, stop=t == 1)
                last.then_inc(*K.inc("gathered"))
            pe.wait_ge(*K.at("weighted", 1))
            for q in range(NQ):
                for t in range(nt):
                    for e in range(4):
                        at = CAP * (t // 2)
                        last = nc.tensor.matmul(K.ps[32 * e:32 * e + 32, 4 + q, t * P:(t + 1) * P], pick[:, t, 4 * q + e, at:at + CAP],
                                                K.ident, start=True, stop=True)
                last.then_inc(*K.inc("scatter_turned"))

        @block.scalar
        def _(act):
            for i in range(n_seg * KD):
                s, k = divmod(i, KD)
                act.wait_ge(*K.at("gathered", i + 1))
                nc.scalar.activation(xs_all[:, :, k, CAP * s:CAP * s + CAP], K.ps[:, i % 4, :].rearrange("p (e s) -> p e s", e=NE),
                                     ACT.Copy).then_inc(*K.inc("gathered_kept"))

        @block.vector
        def _(dve):
            dve.wait_ge(*K.at("gathered", n_seg * KD))
            for t in range(nt):
                at = CAP * (t // 2)
                w = pick[:, t, :, at:at + CAP]
                last = nc.vector.tensor_tensor(w, w, tok(aff, t).unsqueeze(2).broadcast_to([P, NE, CAP]), ALU.mult)
            last.then_inc(*K.inc("weighted"))
            for q in range(NQ):
                dve.wait_ge(*K.at("scatter_turned", q + 1))
                nc.vector.tensor_copy(pt[:, q, :], K.ps[:, 4 + q, 0:n])
    K.end_stage()
    expert_loop_stage(K, l, group, M, n_seg, xs_all, ys)

    with K.block("scatter") as block:
        @block.tensor
        def _(pe):
            for k in range(KD):
                for s in range(n_seg):
                    for q in range(NQ):
                        last = nc.tensor.matmul(K.ps[:, k, SEGS[s]], ys[:, q, s, k * P:(k + 1) * P], pt[:, q, SEGS[s]],
                                                start=q == 0, stop=q == NQ - 1)
                last.then_inc(*K.inc("scattered"))

        @block.vector
        def _(dve):
            for k in range(KD):
                dve.wait_ge(*K.at("scattered", k + 1))
                gated_add(K, 5, k, n_seg)("dve", K.ps[:, k, 0:n], dve)
    K.end_stage()


def router_stage(K, rows, logit, nt):
    nc, first = K.nc, K.cursor
    with K.block("router") as block:
        @block.sync
        def _(sp):
            sp.wait_ge(*K.at("logits_done", 1))
            K.load_next(sp)

        @block.tensor
        def _(pe):
            pe.wait_ge(*K.landed(first))
            w = K.slot(first)
            for k in range(KD):
                for t in range(nt):
                    last = nc.tensor.matmul(K.ps[32 * t:32 * t + NE, 0, 0:P], w[:, k, :], K.HT[:, k, t * P:(t + 1) * P],
                                            start=k == 0, stop=k == KD - 1)
            last.then_inc(*K.inc("logits_done"))
            pe.wait_ge(*K.at("logits_kept", nt))
            nc.tensor.transpose(K.ps[:, 1, 0:P], rows, K.ident).then_inc(*K.inc("logits_turned"))

        @block.vector
        def _(dve):
            K.step(dve, nc.vector.memset(rows, 0.0), "dve_step")
            dve.wait_ge(*K.at("logits_done", 1))
            for t in range(nt):
                nc.vector.tensor_copy(rows[32 * t:32 * t + NE], K.ps[32 * t:32 * t + NE, 0, 0:P]).then_inc(*K.inc("logits_kept"))
            dve.wait_ge(*K.at("logits_turned", 1))
            nc.vector.tensor_copy(logit[:, 0:nt, :], K.ps[:, 1, 0:P].rearrange("p (t e) -> p t e", e=32)[:, 0:nt, 0:NE])
    K.cursor += 1
    K.end_stage()


def expert_loop_stage(K, l, group, M, n_seg, xs_all, ys):
    nc, A, first = K.nc, K.arena, K.cursor
    NG, J = NE // group, group
    FW = D // J
    NC = FW // P
    order = expert_pieces(group)
    npiece = len(order)
    where = {p: i for i, p in enumerate(order)}
    xs = A[:, 8192:9216].rearrange("p (e k s) -> p e k s", e=group, k=KD)
    hid = A[:, 9216:10240].rearrange("p (b f) -> p b f", b=2)
    hidT = A[:, 10240:10240 + group * NC * P].rearrange("p (e c r) -> p e c r", e=group, c=NC)

    def slot(q):
        return K.ring[:, (first + q) % RING, :].rearrange("p (k w) -> p k w", k=KD)

    def landed(g, q):
        sem, n = K.landed(first + q)
        return sem, g * (16 * npiece // RING) + n

    def released(q):
        m, e, h = order[q]
        if m == "moe_w2":
            return "down_done", h + 1
        return "up_done", 2 * e + (1 if m == "moe_w1" else 2)

    def load(sp, g, q):
        m, e, h = order[q]
        sem = K.sem(f"slot{(first + q) % RING}_landed")
        sp.dma_start(K.ring[:, (first + q) % RING, :], K.dram[m][l, g * group + e, h]).then_inc(sem, 16)

    per = dict(up_done=2 * group, silu_done=group, hidden_done=group, hiddenT_ready=group, hiddenT_kept=group,
               down_done=2, ys_kept=2, xs_ready=group)

    def loop(eng, body):
        body(0, True)
        K.times = NG - 1
        with eng.Fori(1, NG) as g:
            body(g, False)
        K.times = 1

    def at(name, g, n):
        return K.at(name, g * per[name] + n)

    with K.block("experts") as block:
        @block.sync
        def _(sp):
            def feed(g, last):
                for q in range(npiece):
                    name, n = released(q)
                    sp.wait_ge(*at(name, g, n))
                    if q + RING < npiece:
                        load(sp, g, q + RING)
                    elif last:
                        K.load_next(sp)
                    else:
                        load(sp, g + 1, q + RING - npiece)
            with sp.Fori(0, NG - 1) as g:
                feed(g, False)
            K.issued += NG * npiece - RING
            feed(NG - 1, True)

        @block.gpsimd
        def _(pool):
            for e in range(group):
                nc.gpsimd.tensor_copy(xs[:, e], xs_all[:, e]).then_inc(*K.inc("xs_ready"))
            K.times = NG - 1
            with pool.Fori(0, NG - 1) as g:
                for e in range(group):
                    pool.wait_ge(*at("up_done", g, 2 * e + 2))
                    nc.gpsimd.tensor_copy(xs[:, e], xs_all[:, g * group + (group + e)]).then_inc(*K.inc("xs_ready"))
            K.times = 1

        @block.tensor
        def _(pe):
            def body(g, peeled):
                def turn(e):
                    pe.wait_ge(*at("hidden_done", g, e + 1))
                    if not (peeled and e < 2):
                        pe.wait_ge(*at("hiddenT_kept", g, e - 1))
                    for c in range(NC):
                        last = nc.tensor.transpose(K.ps[:, 4 + e % 2, c * P:(c + 1) * P], hid[:, e % 2, c * P:(c + 1) * P], K.ident)
                    last.then_inc(*K.inc("hiddenT_ready"))
                for e in range(group):
                    pe.wait_ge(*at("xs_ready", g, e + 1))
                    if not (peeled and e < 2):
                        pe.wait_ge(*at("hidden_done", g, e - 1))
                    for i, m in enumerate(("moe_w1", "moe_w3")):
                        for h in range(2):
                            pe.wait_ge(*landed(g, where[m, e, h]))
                        w = [slot(where[m, e, h]) for h in range(2)]
                        for k in range(KD):
                            for j in range(J):
                                c0 = j * FW % 512
                                last = nc.tensor.matmul(K.ps[M * j:M * j + M, 2 * (e % 2) + i, 0:FW], xs[:, e, k, :],
                                                        w[j * FW // 512][:, k, c0:c0 + FW], start=k == 0, stop=k == KD - 1)
                        last.then_inc(*K.inc("up_done"))
                    if e:
                        turn(e - 1)
                turn(group - 1)
                pe.wait_ge(*at("hiddenT_kept", g, group))
                for h in range(2):
                    if not peeled:
                        pe.wait_ge(*at("ys_kept", g, h - 1))
                    for e in range(group):
                        pe.wait_ge(*landed(g, where["moe_w2", e, h]))
                    for f in range(KD):
                        j, c = divmod(f, NC)
                        for e in range(group):
                            last = nc.tensor.matmul(K.ps[M * e:M * e + M, 6 + h, :], hidT[:, e, c, M * j:M * j + M],
                                                    slot(where["moe_w2", e, h])[:, f, :], start=f == 0, stop=f == KD - 1)
                    last.then_inc(*K.inc("down_done"))
            loop(pe, body)

        @block.scalar
        def _(act):
            def body(g, peeled):
                def keep(e):
                    act.wait_ge(*at("hiddenT_ready", g, e + 1))
                    if not peeled:
                        act.wait_ge(*at("down_done", g, 0))
                    nc.scalar.activation(hidT[:, e].rearrange("p c r -> p (c r)"), K.ps[:, 4 + e % 2, 0:NC * P], ACT.Copy)\
                        .then_inc(*K.inc("hiddenT_kept"))
                for e in range(group):
                    act.wait_ge(*at("up_done", g, 2 * e + 1))
                    if not (peeled and e < 2):
                        act.wait_ge(*at("hiddenT_ready", g, e - 1))
                    nc.scalar.activation(hid[:, e % 2, 0:FW], K.ps[:, 2 * (e % 2), 0:FW], ACT.Silu).then_inc(*K.inc("silu_done"))
                    if e:
                        keep(e - 1)
                keep(group - 1)
            loop(act, body)

        @block.vector
        def _(dve):
            def body(q, g, rows):
                for e in range(group):
                    dve.wait_ge(*at("silu_done", g, e + 1))
                    dve.wait_ge(*at("up_done", g, 2 * e + 2))
                    nc.vector.tensor_tensor(hid[:, e % 2, 0:FW], hid[:, e % 2, 0:FW], K.ps[:, 2 * (e % 2) + 1, 0:FW], ALU.mult)\
                        .then_inc(*K.inc("hidden_done"))
                dve.wait_ge(*at("xs_ready", q * n_seg + (n_seg - 1), group))
                for h in range(2):
                    dve.wait_ge(*at("down_done", g, h + 1))
                    for e in range(group):
                        for c in range(n_seg):
                            r0, p0 = rows + CAP * e, M * e + CAP * c
                            last = nc.vector.tensor_copy(ys[r0:r0 + CAP, q, c, h * 512:(h + 1) * 512], K.ps[p0:p0 + CAP, 6 + h, :])
                    last.then_inc(*K.inc("ys_kept"))
            K.times = NE // 4
            with dve.Fori(0, NE // 4) as q:
                for i in range(n_seg):
                    body(q, q * n_seg + i, CAP * group * i)
            K.times = 1
    K.cursor += NG * npiece
    K.end_stage()


def plan_odd(K):
    K.plan("ada_w", 1, 0, EARLY)
    K.plan("od_w_in", 0)
    K.plan("ada_w", 1, EARLY)
    K.plan("od_w_out", 0)
    K.plan("router", 1)
    plan_experts(K, 4)


def odd_layer(K):
    nc, A, HT, XT = K.nc, K.arena, K.HT, K.XT
    mod_stage(K, K.sil[:, 1], K.col("ada_b1", 0, 48), 0)
    scaled_norm_stage(K, 1, 0, 2)

    u = A[:, 0:7680].rearrange("p (b t) -> p b t", b=15)
    q = A[:, 7680:8704].rearrange("p (b t) -> p b t", b=4)
    k = A[:, 8704:10752].rearrange("p (b t) -> p b t", b=4)
    v = A[:, 10752:12800].rearrange("p (t e) -> p t e", t=4)
    q2 = A[:, 12800:14848].rearrange("p (s b t) -> p s b t", s=2, b=4)
    jobs = [feature_job(K, 0, b * P, P, HT[:, :, X], q[:, b, :]) for b in range(4)]
    jobs += [feature_job(K, 1, b * P, P, HT, k[:, b, :]) for b in range(4)]
    jobs += [token_job(K, 2, lambda w, i: w[:, i, :], HT, t, v[:, t, :]) for t in range(4)]
    jobs += [feature_job(K, 3 + b // 4, b % 4 * P, P, HT, u[:, b, :]) for b in range(15)]
    bias = HT[:, :, :].rearrange("p k t -> p (k t)").rearrange("p (c h n) -> p c h n", c=2, h=8)
    raw = [XT[:, :, C], A[:, 15488:17536].rearrange("p (h n) -> p h n", h=8)]
    also = K.constants(["window", "flip"], A[:, 14848:15488])
    window, flip = K.const["window"].rearrange("p (c n) -> p c n", c=2), K.const["flip"]
    gemm_stage(K, 7, jobs, "odd_in_projection", feed=1, also=also + position_bias(K, raw),
               before=dict(act=lambda act: None, dve=lambda dve: None, ready=None, pool=clear_other_halves(K, q2)))
    norm_stage(K, [dict(src=[b[:, i, :]], ones=K.pair, inv=1.0 / 64, eps=K.eps["rms"],
                        out=[(b[:, i, :], b[:, i, :], slice(0, b.shape[-1]), gain, None)])
                   for b, gain in ((q, K.na_gain), (k, K.col("na_k"))) for i in range(4)],
               HT[:, :, :].rearrange("p k t -> p (k t)")[:, 0:3072],
               also=[(K.u_dram[s].rearrange("p (b t) -> p b t", b=15), u[:, :, SEGS[s]]) for s in range(2)])
    with K.block("masked_bias") as block:
        @block.gpsimd
        def _(pool):
            nc.gpsimd.tensor_copy(q2[0:64, 0], q[0:64])

        @block.scalar
        def _(act):
            nc.scalar.activation(q2[64:128, 1], q[64:128], ACT.Copy)

        @block.tensor
        def _(pe):
            for i in range(8):
                nc.tensor.matmul(K.ps[:, i, :], flip, raw[i // 4][:, i % 4 * 2:i % 4 * 2 + 2, :],
                                 start=True, stop=True).then_inc(*K.inc("flipped"))

        @block.vector
        def _(dve):
            for i in range(8):
                dve.wait_ge(*K.at("flipped", i + 1))
                nc.vector.tensor_tensor(bias[:, i // 4, i % 4 * 2:i % 4 * 2 + 2, :], K.ps[:, i, :].rearrange("p (h n) -> p h n", h=2),
                                        window[:, i // 4, :].unsqueeze(1).broadcast_to([P, 2, T]), ALU.add)
    K.end_stage()
    units = [dict(q=[q2[:, h % 2, h // 2, c * P:(c + 1) * P]], k=k[:, h // 2, :], v=[v[:, t, h * 64:(h + 1) * 64] for t in range(4)],
                  bias=bias[:, c, h, :], rows=(h % 2 * 64, h % 2 * 64 + 64),
                  out=XT[h % 2 * 64:h % 2 * 64 + 64, h // 2, T + c * P:T + (c + 1) * P], weight=[None])
             for h in range(8) for c in range(2)]
    small, lora = A[:, 14336:18432], K.ring[:, 5, 2048:3584]
    attention_stage(K, units, A[:, 0:4096], 1, "neighbourhood_attention", also=K.constants(["causal", "level"], small[:, 2816:3840]) +
                    [(lora, K.dram["lora"][0].rearrange("(p n) -> p n", p=P))])

    y = rwkv(K, small, lora.rearrange("p (w c) -> p w c", w=3))
    with K.block("mixed") as block:
        @block.scalar
        def _(act):
            nc.scalar.activation(HT[:, 4:8, X], XT[:, 0:4, C], ACT.Copy)

        @block.vector
        def _(dve):
            nc.vector.tensor_tensor(HT[:, 0:4, X], y, XT[:, 4:8, C], ALU.mult)
    K.end_stage()
    mod_stage(K, K.sil[:, 1], K.col("ada_b1", 0, 48), 1)
    out_proj_stage(K, 2, 1)
    experts(K, 1, 1)


def position_bias(K, raw):
    rpb, pairs = K.dram["na_rpb"], []
    for r in range(4):
        for h in range(8):
            src = bass.AP(rpb.tensor, h * 15 * 31 + (7 - r) * 31 + 15 - 63, [[1, 64], [31, 4], [1, 64]])
            dst = raw[r // 2][r % 2 * 64:r % 2 * 64 + 64, h, :].rearrange("p (i j) -> p i j", i=4)
            pairs.append((dst, src))
    return pairs


def rwkv(K, small, lora):
    nc, A = K.nc, K.arena
    ring = K.ring[:, :, :].rearrange("p s n -> p (s n)")
    hf = K.HT[:, :, :].rearrange("p k t -> p (k t)")
    m = Recurrence()
    four = lambda a, lo: a[:, lo:lo + 1024].rearrange("p (b t) -> p b t", b=4)
    m.r, m.k, m.v, m.kk = (four(ring, 18432 + i) for i in (0, 1024, 2048, 3072))
    m.rkv = ring[:, 18432:21504]
    m.lora = lora
    m.y = four(small, 768)
    m.lw, m.la, m.lg = m.y[:, 0], m.y[:, 1], small[:, 2 * T:3 * T]
    m.low = [a.rearrange("p (d t) -> p d t", d=2) for a in (small[:, 0:2 * T], ring[:, 24064:24576])]
    m.state = small[:, 1792:2304].rearrange("p (d b v) -> p d b v", d=2, b=4)
    m.rhs = small[:, 2304:2816].rearrange("p (d b v) -> p d b v", d=2, b=4)
    m.g_end = small[:, 3840:3872].rearrange("p (d i) -> p d i", d=2)
    m.idle_slots = (1, 5)
    m.gate = K.XT[:, 4:8, C]
    for d, (buf, bd) in enumerate(((ring, ring[:, 14336:18432]), (A, hf))):
        w = Recurrence()
        w.ar = buf[:, 0:2048].rearrange("p (i w t) -> p i w t", i=16, w=2)
        w.bk = buf[:, 2048:4096].rearrange("p (i w t) -> p i w t", i=16, w=2)
        w.uv = buf[:, 2048:4096].rearrange("p (i h v) -> p i h v", i=16, h=2)
        w.n = buf[:, 4096:8192].rearrange("p (w i c) -> p w i c", w=2, i=16)
        w.w = buf[:, 8192:12288].rearrange("p (i h c) -> p i h c", i=16, h=2)
        w.tok = buf[:, 12288:14336].rearrange("p (i c) -> p i c", i=16)
        w.bd = bd.rearrange("p (w i c) -> p w i c", w=2, i=16)
        w.x = w.bd
        w.decay, w.rate, w.p0, w.p1, w.e2, w.keff = (four(buf, 4096 + 1024 * i) for i in range(6))
        m.of.append(w)
    m.u = A[:, 8192:12032].rearrange("p (b t) -> p b t", b=15)
    work = A[:, 4096:7168]
    m.causal = K.const["causal"].rearrange("p (d w t) -> p d w t", d=2, w=2)
    m.level = K.const["level"].rearrange("p (d l t) -> p d l t", d=2, l=6)
    for s in (1, 0):
        rwkv_inputs(K, m, s, work)
        rwkv_rates(K, m, s)
        rwkv_scale(K, m, s)
        rwkv_products(K, m)
        rwkv_inverse(K, m)
        rwkv_chunks(K, m, s)
    with K.block("refill") as block:
        @block.sync
        def _(sp):
            for i in range(K.issued, K.issued + RING):
                if i % RING not in m.idle_slots:
                    K.load(sp, i)
    K.issued += RING
    K.end_stage()
    norm_stage(K, [dict(src=[m.y[:, b, :]], ones=K.pair, inv=1.0 / 64, eps=K.eps["gn"],
                        out=[(m.y[:, b, :], m.y[:, b, :], slice(0, T), K.col("gn_g", b), K.col("gn_b", b))]) for b in range(4)],
               work, centre=True)
    return m.y


class Recurrence:

    def __init__(self):
        self.of = []


def rwkv_inputs(K, m, s, work):
    nc = K.nc
    dst = [b[:, i, :] for b in (m.r, m.k, m.v) for i in range(4)] + [m.lw, m.la, m.lg]
    with K.block("token_shift") as block:
        @block.sync
        def _(sp):
            for i in range(3):
                sp.dma_start(m.u[:, 5 * i:5 * i + 5], K.u_dram[s].rearrange("p (b t) -> p b t", b=15)[:, 5 * i:5 * i + 5])\
                    .then_inc(*K.inc(f"u_loaded_{i}", 16))
            for i in range(3):
                sp.wait_ge(*K.at(f"u_loaded_{i}", 16))

        @block.gpsimd
        def _(pool):
            if s == 1:
                nc.gpsimd.memset(m.state, 0.0).then_inc(*K.inc("state_cleared"))
                pool.wait_ge(*K.at("state_cleared", 1))
                for low in m.low:
                    for d in range(2):
                        nc.gpsimd.memset(low[64 - 64 * d:128 - 64 * d, d], 0.0)

        @block.vector
        def _(dve):
            tap = lambda j, b: K.col("shift_w", 15 * j + b)
            for i, (j, to, of) in enumerate(((0, slice(1, T), slice(0, T - 1)), (2, slice(0, T - 1), slice(1, T)))):
                for b in range(15):
                    dve.wait_ge(*K.at(("tap_added", "middle_tap")[i == 0], b + 1))
                    nc.vector.scalar_tensor_tensor(out=dst[b][:, to], in0=m.u[:, b, of], scalar=tap(j, b), in1=dst[b][:, to],
                                                   op0=ALU.mult, op1=ALU.add).then_inc(*K.inc("tap_added"))
            dve.wait_ge(*K.at("tap_added", 30))
            for b in range(4):
                nc.vector.tensor_scalar(m.kk[:, b, :], m.k[:, b, :], K.col("k_k", b), None, ALU.mult)

        @block.scalar
        def _(act):
            for b in range(15):
                if b % 5 == 0:
                    act.wait_ge(*K.at(f"u_loaded_{b // 5}", 16))
                nc.scalar.activation(dst[b], m.u[:, b, :], ACT.Copy, scale=K.col("shift_w", 15 + b)).then_inc(*K.inc("middle_tap"))
            act.wait_ge(*K.at("tap_added", 30))
            for d in range(2):
                rows = slice(64 * d, 64 * d + 64)
                nc.scalar.activation(m.low[1][rows, d], m.la[rows], ACT.Copy)
                nc.scalar.activation(m.low[0][rows, d], m.lw[rows], ACT.Tanh)
            nc.scalar.activation(m.lg, m.lg, ACT.Sigmoid)
    K.end_stage()
    norm_stage(K, [dict(src=[m.kk[:, b, :]], ones=K.pair, inv=1.0, eps=K.eps["kk"],
                        out=[(m.kk[:, b, :], m.kk[:, b, :], slice(0, T), None, None)]) for b in range(4)], work)


def rwkv_rates(K, m, s):
    nc = K.nc
    jobs = []
    for which, bias in enumerate(("w0", "a0")):
        for b in range(4):
            def evac(side, ps, eng, outs=[(w.decay, w.rate)[which] for w in m.of], bias=bias, b=b):
                for d in range(2):
                    last = nc.scalar.activation(outs[d][:, b, :], ps[:, d * T:(d + 1) * T], ACT.Sigmoid, bias=K.col(bias, 4 * d + b))
                return last
            jobs.append(dict(pieces=[], rows=(0, P), n=TT, only="act", evac=evac,
                             mm=lambda _, which=which, b=b: [(m.lora[:, which, b * P:(b + 1) * P], m.low[which].rearrange("p d t -> p (d t)"))]))
    if s == 0:
        jobs += [dict(pieces=[], rows=(0, P), n=T, only="dve", mm=lambda _, b=b: [(m.lora[:, 2, b * P:(b + 1) * P], m.lg)],
                      evac=lambda side, ps, eng, b=b: evacuate(K, side, m.gate[:, b, :], ps)) for b in range(4)]
    gemm_stage(K, 0, jobs, "rwkv_rates")


def rwkv_scale(K, m, s):
    nc = K.nc
    by_chunk = lambda a: a.rearrange("p b (c t) -> p (b c) t", t=CH)
    r, k, kk = (by_chunk(a) for a in (m.r, m.k, m.kk))
    c = -math.exp(-0.5)

    reset = m.of[0].keff.rearrange("p b t -> p (b t)")

    def other_blocks(d):
        return [m.of[d].bd[64 * h:64 * h + 64, i, :, 64 - 64 * h:128 - 64 * h] for i in range(2) for h in range(2)]

    def scale(eng, d, tag):
        w = m.of[d]
        p0, p1, e2, rate, keff = (by_chunk(a) for a in (w.p0, w.p1, w.e2, w.rate, w.keff))
        done = f"{tag}_step"
        for b in range(4):
            last = eng.tensor_scalar(w.keff[:, b, :], w.rate[:, b, :], -1.0, K.col("k_a", b), ALU.add, ALU.mult)
        K.step(eng, last, done)
        eng.tensor_tensor(rate, rate, kk, ALU.mult)
        K.step(eng, eng.tensor_tensor(keff, keff, k, ALU.mult), done)
        eng.tensor_scalar(rate, rate, -1.0, None, ALU.mult)
        K.step(eng, eng.tensor_tensor(keff, keff, k, ALU.add), f"effective_key_{tag}")
        eng.wait_ge(*K.at(f"exps_{tag}", 3))
        eng.tensor_tensor(w.ar[:, :, 0, :], kk, p0, ALU.mult).then_inc(*K.inc(f"scaled_{tag}"))
        eng.tensor_tensor(w.bk[:, :, 0, :], rate, p1, ALU.mult).then_inc(*K.inc(f"scaled_{tag}"))
        eng.tensor_tensor(w.bk[:, :, 1, :], keff, p1, ALU.mult)

    with K.block("rwkv_scale") as block:
        @block.vector
        def _(dve):
            dve.wait_ge(*K.at("reset_ready", 2))
            for d in range(2):
                L, p1 = (a.rearrange("p b t -> p (b t)")[:, ::(1, -1)[d]] for a in (m.of[d].decay, m.of[d].p1))
                nc.vector.tensor_tensor_scan(p1, reset, L, 0.0, ALU.mult, ALU.add).then_inc(*K.inc("cumulated"))
            for d in range(2):
                dve.wait_ge(*K.at("cumulated", d + 1))
                nc.vector.tensor_tensor(m.of[d].p0, m.of[d].p1, m.of[d].decay, ALU.subtract).then_inc(*K.inc("cumulated_before"))
            for zeros in other_blocks(0):
                nc.vector.memset(zeros, 0.0)
            scale(nc.vector, 0, "dve")
            for d, tag in enumerate(("dve", "pool")):
                e2 = by_chunk(m.of[d].e2)
                dve.wait_ge(*K.at(f"exps_{tag}", 1))
                nc.vector.tensor_tensor(m.of[d].ar[:, :, 1, :], r, e2, ALU.mult)
                nc.vector.tensor_copy(m.g_end[:, d].unsqueeze(2), e2[:, :, (CH - 1, 0)[d]:(CH, 1)[d]])
            if s == 0:
                t, other = m.of[0].decay, m.of[1].keff
                dve.wait_ge(*K.at("cumulated_before", 1))
                dve.wait_ge(*K.at("effective_key_pool", 1))
                K.step(dve, nc.vector.tensor_tensor(t, m.of[0].keff, other, ALU.add), "dve_step")
                K.step(dve, nc.vector.tensor_tensor(t, t, m.r, ALU.mult), "dve_step")
                for b in range(4):
                    nc.vector.tensor_scalar(t[:, b, :], t[:, b, :], K.col("r_k", b), None, ALU.mult).then_inc(*K.inc("bonus_ready"))
                for b in range(4):
                    dve.wait_ge(*K.at("bonus_summed", b + 1))
                    nc.vector.tensor_tensor(m.y[:, b, :], K.ps[:, b, 0:T], m.v[:, b, :], ALU.mult)

        @block.gpsimd
        def _(pool):
            by_token = reset.rearrange("p (i t) -> p i t", t=CH)
            nc.gpsimd.memset(by_token[:, :, 0:1], 0.0).then_inc(*K.inc("reset_ready"))
            nc.gpsimd.memset(by_token[:, :, 1:CH], 1.0).then_inc(*K.inc("reset_ready"))
            scale(nc.gpsimd, 1, "pool")

        @block.tensor
        def _(pe):
            if s == 0:
                for b in range(4):
                    pe.wait_ge(*K.at("bonus_ready", b + 1))
                    nc.tensor.matmul(K.ps[:, b, 0:T], K.pair, m.of[0].decay[:, b, :], start=True, stop=True).then_inc(*K.inc("bonus_summed"))

        @block.scalar
        def _(act):
            for i, zeros in enumerate(other_blocks(1)):
                h = i % 2
                nc.scalar.activation(zeros, K.eps["zero"][64 * h:64 * h + 64].unsqueeze(2).broadcast_to([64, 16, 64]), ACT.Copy)
            for d, tag in enumerate(("dve", "pool")):
                w = m.of[d]
                act.wait_ge(*K.at("cumulated_before", d + 1))
                nc.scalar.activation(w.e2, w.p1, ACT.Exp, scale=c).then_inc(*K.inc(f"exps_{tag}"))
                nc.scalar.activation(w.p0, w.p0, ACT.Exp, scale=c).then_inc(*K.inc(f"exps_{tag}"))
                act.wait_ge(*K.at(f"exps_{tag}", 1))
                nc.scalar.activation(w.p1, w.p1, ACT.Exp, scale=-c).then_inc(*K.inc(f"exps_{tag}"))
            for d, tag in enumerate(("dve", "pool")):
                w = m.of[d]
                for i, src in enumerate((w.ar, w.bk)):
                    act.wait_ge(*K.at(f"scaled_{tag}", i + 1))
                    for h in range(2):
                        rows = slice(64 * h, 64 * h + 64)
                        nc.scalar.activation(w.bd[rows, i, :, 64 * h:64 * h + 64], src[rows, :, 0, :], ACT.Copy)
    K.end_stage()


def rwkv_products(K, m):
    nc = K.nc
    flat = lambda a: a.rearrange("p w t -> p (w t)")
    jobs = []

    def job(emit, evac, only, rows=(0, P)):
        jobs.append(dict(pieces=[], rows=rows, n=512, only=only, emit=emit, evac=evac))

    for d in range(2):
        w = m.of[d]
        mask = flat(m.causal[:, d]).unsqueeze(1).broadcast_to([P, 4, P])
        for q in range(4):
            chunks = range(4 * q, 4 * q + 4)
            for h in range(2):
                def emit(bank, w=w, h=h, chunks=chunks):
                    for i in chunks:
                        rows = slice(64 * h, 64 * h + 64)
                        last = nc.tensor.matmul(K.ps[:, bank, i % 4 * P:(i % 4 + 1) * P], flat(w.bk[rows, i]), flat(w.ar[rows, i]),
                                                start=True, stop=True)
                    return last
                job(emit, lambda side, ps, eng, w=w, q=q, h=h, mask=mask: nc.vector.tensor_tensor(
                    w.w[:, 4 * q:4 * q + 4, h, :], ps.rearrange("p (i c) -> p i c", i=4), mask, ALU.mult), "dve")
            for t in range(2):
                def emit(bank, w=w, t=t, chunks=chunks):
                    for i in chunks:
                        last = nc.tensor.matmul(K.ps[:, bank, i % 4 * P:(i % 4 + 1) * P], w.bd[:, t, i, :], w.bd[:, 1 - t, i, :],
                                                start=True, stop=True)
                    return last
                strict = m.causal[:, (1 - d, d)[t], 0, :].unsqueeze(1).broadcast_to([P, 8, CH])
                job(emit, lambda side, ps, eng, w=w, q=q, t=t, strict=strict: nc.vector.tensor_tensor(
                    w.n[:, t, 4 * q:4 * q + 4, :].rearrange("p i (h c) -> p (i h) c", h=2),
                    ps.rearrange("p (i c) -> p i c", i=8), strict, ALU.mult), "dve")

            def emit(bank, w=w, chunks=chunks):
                for i in chunks:
                    last = nc.tensor.transpose(K.ps[:, bank, i % 4 * P:(i % 4 + 1) * P], flat(w.bk[:, i]), K.ident)
                return last
            job(emit, lambda side, ps, eng, w=w, q=q: nc.scalar.activation(
                w.tok[:, 4 * q:4 * q + 4].rearrange("p i c -> p (i c)"), ps, ACT.Copy), "act")
        for q in range(4):
            def emit(bank, q=q):
                for i in range(4 * q, 4 * q + 4):
                    c0 = 2048 + CH * i - CH
                    last = nc.tensor.transpose(K.ps[:, bank, i % 4 * P:(i % 4 + 1) * P], m.rkv[:, c0:c0 + P], K.ident)
                return last
            job(emit, lambda side, ps, eng, w=w, q=q: nc.scalar.activation(
                w.uv[64:128, 4 * q:4 * q + 4].rearrange("p i h v -> p (i h v)"), ps[64:128], ACT.Copy), "act")
    gemm_stage(K, 0, jobs, "rwkv_products")


def rwkv_inverse(K, m):
    nc, levels = K.nc, 6
    jobs = []
    for i in range(1, levels):
        jobs += [(i, "z", d, q) for d in range(2) for q in range(4)]
        jobs += [(i, kind, d, q) for d in range(2) for q in range(4) for kind in (("x", "xT") if i < levels - 1 else ("xT",))]
    where = {job: j for j, job in enumerate(jobs)}
    quarter = lambda a, q: a[:, 4 * q:4 * q + 4, :]
    by_head = lambda a: a.rearrange("p i (h c) -> p (i h) c", h=2)

    level = lambda dd, i: m.level[:, dd, i, :].unsqueeze(1).broadcast_to([P, 8, CH])

    def begin(eng, t, name):
        eye = K.ident.unsqueeze(1).broadcast_to([P, 4, P])
        parts = [(d, q) for d in range(2) for q in range(4)]
        for i in range(len(parts) + 1):
            if i < len(parts):
                d, q = parts[i]
                w = m.of[d]
                eng.tensor_tensor(by_head(quarter(w.x[:, t], q)), by_head(quarter(w.n[:, t], q)), level((d, 1 - d)[t], 0), ALU.mult)\
                    .then_inc(*K.inc(f"{name}_blocks"))
            if i:
                d, q = parts[i - 1]
                x = quarter(m.of[d].x[:, t], q)
                eng.wait_ge(*K.at(f"{name}_blocks", i))
                eng.tensor_tensor(x, x, eye, ALU.add).then_inc(*K.inc(name))

    with K.block("rwkv_inverse") as block:
        @block.vector
        def _(dve):
            begin(nc.vector, 0, "inverse_begun")
            for j, (i, kind, d, q) in enumerate(jobs):
                w = m.of[d]
                ps = K.ps[:, j % NBANK, :].rearrange("p (i c) -> p i c", i=4)
                dve.wait_ge(*K.at("inverse_product", j + 1))
                if kind == "z":
                    out = quarter(w.n[:, 0], q)
                    last = nc.vector.tensor_tensor(by_head(out), by_head(ps), level(d, i), ALU.mult)
                else:
                    if kind == "x":
                        dve.wait_ge(*K.at("inverse_product", where[i, "xT", d, q] + 1))
                    x = quarter(w.x[:, 0 if kind == "x" else 1], q)
                    last = nc.vector.tensor_tensor(x, x, ps, ALU.add)
                last.then_inc(*K.inc("inverse_kept"))

        @block.tensor
        def _(pe):
            for j, (i, kind, d, q) in enumerate(jobs):
                w = m.of[d]
                if j >= NBANK:
                    pe.wait_ge(*K.at("inverse_kept", j - NBANK + 1))
                if kind == "z" and i == 1:
                    pe.wait_ge(*K.at("inverse_begun", 4 * d + q + 1))
                elif kind == "z":
                    pe.wait_ge(*K.at("inverse_kept", where[i - 1, "xT", d, q] + 1))
                else:
                    if i == 1:
                        pe.wait_ge(*K.at("transpose_begun", 4 * d + q + 1))
                    pe.wait_ge(*K.at("inverse_kept", where[i, "z", d, q] + 1))
                lhs, rhs = {"z": (w.n[:, 1], w.x[:, 0]), "x": (w.x[:, 1], w.n[:, 0]), "xT": (w.n[:, 0], w.x[:, 1])}[kind]
                for c in range(4 * q, 4 * q + 4):
                    last = nc.tensor.matmul(K.ps[:, j % NBANK, c % 4 * P:(c % 4 + 1) * P], lhs[:, c, :], rhs[:, c, :], start=True, stop=True)
                last.then_inc(*K.inc("inverse_product"))

        @block.gpsimd
        def _(pool):
            begin(nc.gpsimd, 1, "transpose_begun")
            pool.wait_ge(*K.at("transpose_begun", 8))
            for d in range(2):
                nc.gpsimd.memset(m.of[d].uv[0:64], 0.0)
    K.end_stage()


def rwkv_chunks(K, m, s):
    nc = K.nc
    order = (range(4), range(3, -1, -1))
    heads = [(b, h) for b in range(4) for h in range(2)]
    tags = ("forward", "backward")
    out = s == 0
    steps = [(n, d) for n in range(4) for d in range(2)]
    with K.block("rwkv_chunks") as block:
        @block.sync
        def _(sp):
            if s == 0:
                for i in range(K.issued, K.issued + RING):
                    if i % RING in m.idle_slots:
                        K.load(sp, i)

        @block.tensor
        def _(pe):
            def right_sides(n, d):
                w, c = m.of[d], order[d][n]
                if n:
                    pe.wait_ge(*K.at(f"state_{tags[d]}", n))
                for b, h in heads:
                    rows, i = slice(64 * h, 64 * h + 64), 4 * b + c
                    to = K.ps[rows, 3 * d, b * CH:(b + 1) * CH]
                    nc.tensor.matmul(to, w.ar[rows, i, 0, :], m.state[rows, d, b, :], start=True, stop=False)
                    last = nc.tensor.matmul(to, w.w[:, i, h, 0:CH], w.uv[:, i, h, :], start=False, stop=True)
                last.then_inc(*K.inc("right_sides"))

            def solve(n, d):
                w, c = m.of[d], order[d][n]
                pe.wait_ge(*K.at("right_sides_kept", 2 * n + d + 1))
                for b, h in heads:
                    rows, i = slice(64 * h, 64 * h + 64), 4 * b + c
                    last = nc.tensor.matmul(K.ps[0:64, 3 * d + 1 + h, b * CH:(b + 1) * CH], w.x[rows, 1, i, 64 * h:64 * h + 64],
                                            m.rhs[rows, d, b, :], start=True, stop=True)
                last.then_inc(*K.inc("solved"))

            def advance(n, d):
                w, c = m.of[d], order[d][n]
                pe.wait_ge(*K.at("solution_kept", 2 * n + d + 1))
                for b, h in heads:
                    rows, i = slice(64 * h, 64 * h + 64), 4 * b + c
                    if out:
                        to = K.ps[rows, 3 * d, 256 + b * CH:256 + (b + 1) * CH]
                        nc.tensor.matmul(to, m.state[rows, d, b, :], w.ar[rows, i, 1, :], start=True, stop=False)
                        nc.tensor.matmul(to, w.uv[:, i, h, :], w.w[:, i, h, CH:2 * CH], start=False, stop=True)
                    last = nc.tensor.matmul(K.ps[rows, 3 * d + 1, 256 + b * CH:256 + (b + 1) * CH], w.tok[:, i, 64 * h:64 * h + 64],
                                            w.uv[:, i, h, :], start=True, stop=True)
                last.then_inc(*K.inc("chunk_done"))
            for n in range(4):
                for phase in (right_sides, solve, advance):
                    for d in range(2):
                        phase(n, d)

        @block.scalar
        def _(act):
            for j, (n, d) in enumerate(steps):
                act.wait_ge(*K.at("right_sides", j + 1))
                nc.scalar.activation(m.rhs[:, d].rearrange("p b v -> p (b v)"), K.ps[:, 3 * d, 0:256], ACT.Copy)\
                    .then_inc(*K.inc("right_sides_kept"))

        @block.vector
        def _(dve):
            for n in range(4):
                for d in range(2):
                    w, c = m.of[d], order[d][n]
                    dve.wait_ge(*K.at("solved", 2 * n + d + 1))
                    for h in range(2):
                        uv = w.uv.rearrange("p (b c) h v -> p b c h v", b=4)[0:64, :, c, h, :]
                        last = nc.vector.tensor_copy(uv, K.ps[0:64, 3 * d + 1 + h, 0:256].rearrange("p (b v) -> p b v", b=4))
                    last.then_inc(*K.inc("solution_kept"))
                for d in range(2):
                    c, S = order[d][n], m.state[:, d]
                    g = m.g_end[:, d].rearrange("p (b c) -> p b c", b=4)[:, :, c:c + 1].broadcast_to([P, 4, CH])
                    dve.wait_ge(*K.at("chunk_done", 2 * n + d + 1))
                    if out:
                        y = m.y[:, :, c * CH:(c + 1) * CH]
                        nc.vector.tensor_tensor(y, y, K.ps[:, 3 * d, 256:512].rearrange("p (b t) -> p b t", b=4), ALU.add)
                    K.step(dve, nc.vector.tensor_tensor(S, S, K.ps[:, 3 * d + 1, 256:512].rearrange("p (b v) -> p b v", b=4), ALU.add), "dve_step")
                    nc.vector.tensor_tensor(S, S, g, ALU.mult).then_inc(*K.inc(f"state_{tags[d]}"))
    K.end_stage()


def store_stage(K, out):
    with K.block("store") as block:
        @block.sync
        def _(sp):
            sp.dma_start(out.rearrange("(k p) t -> p k t", p=P), K.XT[:, :, X]).then_inc(*K.inc("output_stored", 16))
            sp.wait_ge(*K.at("output_stored", 16))
    K.end_stage()


def build_program(nc, dram, out, layers=("f0", "f1", "s0", "s1")):
    with ExitStack() as ctx:
        K = Kit(nc, ctx, dram)
        K.const, K.eps = {}, {}
        K.u_dram = nc.dram_tensor("rwkv_inputs", (2, P, 15 * T), F32, kind="Internal").ap()
        for l in range(DEPTH):
            if f"f{l}" in layers:
                K.plan("w_mod", l, 0, EARLY)
                K.plan("w_in", l)
                K.plan("w_mod", l, EARLY)
                for name in ("w_out", "w_up", "w_down"):
                    K.plan(name, l)
        if "s0" in layers:
            plan_even(K)
        if "s1" in layers:
            plan_odd(K)
        prologue(K)
        for l in range(DEPTH):
            if f"f{l}" in layers:
                first_layer(K, l)
        if "s0" in layers:
            even_layer(K)
        if "s1" in layers:
            odd_layer(K)
        store_stage(K, out)


def tiled(w, parts):
    return np.concatenate([w[r0:r1, c0:c1].reshape((r1 - r0) // P, P, c1 - c0).transpose(1, 0, 2).ravel()
                           for r0, r1, c0, c1 in parts])


def constant_tables():
    out = {n: np.zeros((P, w), np.float64) for n, w in CONSTS.items()}
    out["ident"][:] = np.eye(P)
    out["ones"][:] = 1
    out["pair"][:64, :64] = out["pair"][64:, 64:] = 1
    t = np.arange(T)
    row, col = (t // GRID_W).astype(np.float32), (t % GRID_W).astype(np.float32)

    def rope(base, width, reps, swap, cos, sin):
        half, quarter = width // 2, width // 4
        inv = (np.float32(1.0) / np.float32(10000.0) ** (np.arange(0, half, 2, dtype=np.float32) / np.float32(half))).astype(np.float32)
        out[cos][:] = 1
        for r in range(reps):
            for i in range(width):
                j = i % half
                ang = ((row if i < half else col) * inv[j % quarter]).astype(np.float32).astype(np.float64)
                p = base + r * width + i
                out[cos][p], out[sin][p] = np.cos(ang), (-1 if j < quarter else 1) * np.sin(ang)
                out[swap][p + (quarter if j < quarter else -quarter), p] = 1
    rope(0, 64, 2, "swap1", "cos1", "sin1")
    rope(64, 32, 1, "swap2", "cos2", "sin2")
    ang = 2 * np.pi * (np.outer(t, t) % T) / T
    out["cn"][:] = (np.cos(ang) / 16).reshape(2, P, T).transpose(1, 0, 2).reshape(P, 512)
    out["sn"][:] = (np.sin(ang) / 16).reshape(2, P, T).transpose(1, 0, 2).reshape(P, 512)
    m = np.arange(64)
    ang = 2 * np.pi * (np.outer(m, m) % 64) / 64
    for g in range(2):
        s = slice(64 * g, 64 * g + 64)
        out["cm"][s, s], out["sm"][s, s] = np.cos(ang) / 8, -np.sin(ang) / 8
    out["tri"][:] = np.triu(np.ones((P, P)))
    out["iota"][:] = np.arange(1, 65)[None]
    c = np.arange(GRID_W)
    start = np.clip(c - 8, 0, GRID_W - 16)
    inside = (c[None] >= start[:, None]) & (c[None] < start[:, None] + 16)
    add = np.where(inside[t % GRID_W][:, t % GRID_W], 0.0, -1e30)
    out["window"][:] = add.reshape(2, P, T).transpose(1, 0, 2).reshape(P, 512)
    s, u = np.arange(CH)[:, None], np.arange(CH)[None]
    causal = [np.concatenate([before(s, u), ~before(u, s)], 1) for before in (np.less, np.greater)]
    out["causal"][:] = np.tile(np.concatenate(causal, 1), (2, 1))
    for i in range(6):
        b = 1 << i
        low = (s // (2 * b) == u // (2 * b)) & (s // b % 2 == 1) & (u // b % 2 == 0)
        for d, msk in enumerate((low, low.T)):
            at = (d * 6 + i) * 64
            out["level"][:, at:at + 64] = np.tile(msk, (2, 1))
    out["flip"][:] = np.kron(np.eye(2), np.eye(64)[::-1])
    return np.concatenate([out[n] for n in CONSTS], 1).astype(np.float32)


def as_columns(v):
    v = np.asarray(v, np.float32).reshape(-1)
    v = np.concatenate([v, np.zeros(-len(v) % P, np.float32)])
    return v.reshape(-1, P).T


def host_arrays(a):
    f = {k: np.asarray(v) for k, v in a.items()}
    vec = {
        "c": f["c"], "c_ctx": f["c_ctx"], "c_2": f["c_2"], "c_ctx_2": f["c_ctx_2"],
        "q_norm": f["mla_q_norm_2"], "kv_norm": f["mla_kv_norm_2"], "q_g": f["mla_q_g_2"], "k_g": f["mla_k_g_2"],
        "dw_w": f["cv_dw_w_2"], "dw_b": f["cv_dw_b_2"], "cln_g": f["cv_ln_g_2"], "cln_b": f["cv_ln_b_2"],
        "shift_w": f["rw_shift_w_2"], "w0": f["rw_w0_2"], "a0": f["rw_a0_2"], "k_k": f["rw_k_k_2"], "k_a": f["rw_k_a_2"],
        "r_k": f["rw_r_k_2"], "gn_g": f["rw_gn_g_2"], "gn_b": f["rw_gn_b_2"],
        "na_q": np.tile(f["na_q_g_2"].reshape(-1), 2), "na_k": np.tile(f["na_k_g_2"].reshape(-1), 2),
    }
    for l in range(DEPTH):
        vec |= {f"b_mod{l}": f["b_mod"][l], f"ada_b{l}": f["ada_b_2"][l], f"subln{l}": f["subln_w"][l],
                f"conv_w{l}": f["conv_w"][l], f"conv_b{l}": f["conv_b"][l],
                f"norm1_g{l}": f["norm1_g_2"][l], f"norm2_g{l}": f["norm2_g_2"][l]}
        vec |= {f"{n}{l}": f[n][l] for n in ("ln1_g", "ln1_b", "ln2_g", "ln2_b")}
    out = {"cols": np.concatenate([as_columns(vec[n]) for n in COLS], 1), "consts": constant_tables(),
           "diff_lambda": f["diff_lambda"].reshape(-1), "na_rpb": f["na_rpb_2"].reshape(-1)}
    out |= {n: np.ascontiguousarray(f[n][0].T) for n in ("x", "ctx", "ctx_2")}
    weights = {
        "w_mod": f["w_mod"], "w_in": f["w_in"], "w_out": f["w_out"], "w_up": f["w_up"], "w_down": f["w_down"],
        "ada_w": f["ada_w_2"], "ev_w_in": f["ev_w_in_2"], "ev_w_out": f["ev_w_out_2"], "w_uq": f["mla_w_uq_2"],
        "w_ukv": f["mla_w_ukv_2"], "router": f["moe_router_2"], "od_w_in": f["od_w_in_2"], "od_w_out": f["od_w_out_2"],
        "lora": np.concatenate([f["rw_w2_2"].reshape(1, P, 512), f["rw_a2_2"].reshape(1, P, 512), f["rw_g2_2"]], 1),
    }
    for n, w in weights.items():
        out[n] = np.stack([tiled(w[l], PARTS[n]) for l in range(w.shape[0])])
    for n in ("moe_w1_2", "moe_w3_2", "moe_w2_2"):
        w = f[n]
        out[n[:6]] = np.ascontiguousarray(w.reshape(DEPTH, NE, KD, P, 2, 512).transpose(0, 1, 4, 3, 2, 5)).reshape(DEPTH, NE, 2, P, SLOT)
    return {k: np.ascontiguousarray(v) for k, v in out.items()}


def kernel(**inputs):
    import concourse.bacc as bacc
    from concourse.bass_utils import run_bass_kernel_spmd

    nc = bacc.Bacc("TRN2", target_bir_lowering=False, num_devices=1)
    arrays = {f"in_{n}": a for n, a in host_arrays(inputs).items()}
    dram = {n[3:]: nc.dram_tensor(n, a.shape, mybir.dt.from_np(a.dtype), kind="ExternalInput").ap() for n, a in arrays.items()}
    out = nc.dram_tensor("out_x", (D, T), F32, kind="ExternalOutput").ap()
    build_program(nc, dram, out)
    r = run_bass_kernel_spmd(nc, [arrays], core_ids=[0])
    return np.ascontiguousarray(np.asarray(r.results[0]["out_x"]).T).reshape(1, T, D)
```
